# Optimizing a Trainium2 kernel written in Bass

```python
import math
import jax, jax.numpy as jnp
from jax import lax
import numpy as np

D_MODEL = 1024
BATCH = 1
SEQ = 256
DEPTH = 2

CHUNK = 64
Q_BLOCK = 128
EPS = 1e-6
N_EVEN = (DEPTH + 1) // 2
N_ODD = DEPTH // 2

A_HEADS = 8
A_NOPE = 64
A_ROPE = 32
A_V = 64
A_Q_LORA = 256
A_KV_LORA = 128
A_THETA = 10000.0
B_HEADS = 8
B_DH = 64
B_LEFT_CHUNKS = 8
B_BAND = B_LEFT_CHUNKS + 1
B_REL_CLIP = 128
EVEN_IN = A_Q_LORA + A_KV_LORA + A_ROPE + 3 * B_HEADS * B_DH
EVEN_MIX = A_HEADS * A_V + B_HEADS * B_DH
C_HEADS = 8
C_DH = 64
C_ROPE = C_DH // 4
ROPE_THETA = 500000.0
C_MIX = C_HEADS * 2 * C_DH
FF_DENSE = 2752
N_EXPERTS = 8
TOP_K = 2
FF_EXPERT = 3584

kernel_name = 'hybrid_mla_band_diffattn_moe_trunk'

def rmsnorm(x, g):
    xf = x.astype(jnp.float32)
    y = xf * lax.rsqrt(jnp.mean(xf * xf, axis=-1, keepdims=True) + EPS)
    return y.astype(x.dtype) * g

def rope_tables(positions, dim, theta):
    inv = 1.0 / (theta ** (jnp.arange(0, dim, 2, dtype=jnp.float32) / dim))
    ang = positions.astype(jnp.float32)[..., None] * inv
    return jnp.cos(ang), jnp.sin(ang)

def apply_rope(x, cos, sin):
    shape = (cos.shape[0],) + (1,) * (x.ndim - 3) + cos.shape[1:]
    c = cos.reshape(shape)
    s = sin.reshape(shape)
    x1, x2 = jnp.split(x.astype(jnp.float32), 2, axis=-1)
    return jnp.concatenate([x1 * c - x2 * s, x2 * c + x1 * s], axis=-1).astype(x.dtype)

def partial_rope(x, cos, sin, rot_dim):
    return jnp.concatenate([apply_rope(x[..., :rot_dim], cos, sin), x[..., rot_dim:]], axis=-1)

def split_heads(t, n_heads):
    b, s, _ = t.shape
    return t.reshape(b, s, n_heads, -1).transpose(0, 2, 1, 3)

def chunk_causal_softmax(scores, q0):
    nq, nk = scores.shape[-2:]
    q_chunk = (q0 + jnp.arange(nq)) // CHUNK
    k_chunk = jnp.arange(nk) // CHUNK
    mask = k_chunk[None, :] <= q_chunk[:, None]
    return jax.nn.softmax(jnp.where(mask, scores, -jnp.inf), axis=-1)

def mla_attention(c_q, c_kv, k_rope, cos, sin, g_cq, g_ckv, w_uq, w_ukv, g_qn, g_kn):
    q = jnp.einsum('bsr,rhd->bhsd', rmsnorm(c_q, g_cq), w_uq)
    kv = jnp.einsum('bsr,rhd->bhsd', rmsnorm(c_kv, g_ckv), w_ukv)
    q_nope = rmsnorm(q[..., :A_NOPE], g_qn[:A_NOPE])
    q_rot = apply_rope(rmsnorm(q[..., A_NOPE:], g_qn[A_NOPE:]), cos, sin)
    k_nope = rmsnorm(kv[..., :A_NOPE], g_kn[:A_NOPE])
    v = kv[..., A_NOPE:]
    k_rot = apply_rope(rmsnorm(k_rope, g_kn[A_NOPE:]), cos, sin)
    scale = (A_NOPE + A_ROPE) ** -0.5
    outs = []
    for i in range(q.shape[2] // Q_BLOCK):
        q0, k_end = i * Q_BLOCK, (i + 1) * Q_BLOCK
        s = (jnp.einsum('bhqd,bhkd->bhqk', q_nope[:, :, q0:k_end], k_nope[:, :, :k_end],
                        preferred_element_type=jnp.float32)
             + jnp.einsum('bhqd,bkd->bhqk', q_rot[:, :, q0:k_end], k_rot[:, :k_end],
                          preferred_element_type=jnp.float32)) * scale
        p = chunk_causal_softmax(s, q0)
        outs.append(jnp.einsum('bhqk,bhkd->bhqd', p.astype(v.dtype), v[:, :, :k_end]))
    return jnp.concatenate(outs, axis=2)

def band_attention(q, k, v, rel_table):
    b, h, s_len, dh = q.shape
    nc = s_len // CHUNK
    qc = q.reshape(b, h, nc, CHUNK, dh)
    pad = ((0, 0), (0, 0), (B_LEFT_CHUNKS, 0), (0, 0), (0, 0))
    kp = jnp.pad(k.reshape(b, h, nc, CHUNK, dh), pad)
    vp = jnp.pad(v.reshape(b, h, nc, CHUNK, dh), pad)
    k_band = jnp.concatenate([kp[:, :, j:j + nc] for j in range(B_BAND)], axis=3)
    v_band = jnp.concatenate([vp[:, :, j:j + nc] for j in range(B_BAND)], axis=3)
    qi = np.arange(CHUNK)[:, None]
    km = np.arange(B_BAND * CHUNK)[None, :]
    rel = np.clip(B_LEFT_CHUNKS * CHUNK + qi - km, -B_REL_CLIP, B_REL_CLIP) + B_REL_CLIP
    bias = rel_table[:, rel].astype(jnp.float32)
    s = jnp.einsum('bhcqd,bhckd->bhcqk', qc, k_band, preferred_element_type=jnp.float32) * dh ** -0.5
    s = s + bias[None, :, None]
    key_chunk = np.arange(nc)[:, None] - B_LEFT_CHUNKS + (np.arange(B_BAND * CHUNK) // CHUNK)[None, :]
    valid = key_chunk >= 0
    p = jax.nn.softmax(jnp.where(valid[:, None, :], s, -jnp.inf), axis=-1)
    out = jnp.einsum('bhcqk,bhckd->bhcqd', p.astype(v.dtype), v_band)
    return out.reshape(b, h, s_len, dh)

def diff_attention(q, k, v, cos, sin, g_qn, g_kn, lam_q1, lam_k1, lam_q2, lam_k2, g_sub, lam_init):
    q = partial_rope(rmsnorm(q, g_qn), cos, sin, C_ROPE)
    k = partial_rope(rmsnorm(k, g_kn), cos, sin, C_ROPE)
    lam = (jnp.exp(jnp.sum((lam_q1 * lam_k1).astype(jnp.float32)))
           - jnp.exp(jnp.sum((lam_q2 * lam_k2).astype(jnp.float32))) + lam_init)
    scale = C_DH ** -0.5
    outs = []
    for i in range(q.shape[3] // Q_BLOCK):
        q0, k_end = i * Q_BLOCK, (i + 1) * Q_BLOCK
        s = jnp.einsum('bhmqd,bhmkd->bhmqk', q[:, :, :, q0:k_end], k[:, :, :, :k_end],
                       preferred_element_type=jnp.float32) * scale
        p = chunk_causal_softmax(s, q0)
        a = p[:, :, 0] - lam * p[:, :, 1]
        outs.append(jnp.einsum('bhqk,bhkd->bhqd', a.astype(v.dtype), v[:, :, :k_end]))
    o = jnp.concatenate(outs, axis=2)
    return rmsnorm(o, g_sub) * (1.0 - lam_init)

def swiglu(h, w_gate, w_up, w_down):
    return (jax.nn.silu(h @ w_gate) * (h @ w_up)) @ w_down

def moe_swiglu(h, w_router, w_gate, w_up, w_down):
    b, s_len, d = h.shape
    t = h.reshape(-1, d)
    logits = jnp.dot(t, w_router, preferred_element_type=jnp.float32)
    top_val, top_idx = lax.top_k(logits, TOP_K)
    gates = jax.nn.softmax(top_val, axis=-1)
    combine = jnp.sum(jax.nn.one_hot(top_idx, N_EXPERTS, dtype=jnp.float32) * gates[..., None], axis=1)
    out = jnp.zeros_like(t)
    for e in range(N_EXPERTS):
        out = out + combine[:, e:e + 1].astype(t.dtype) * swiglu(t, w_gate[e], w_up[e], w_down[e])
    return out.reshape(b, s_len, d)

def setup_inputs(seed: int = 0) -> dict:
    key = jax.random.key(seed)
    ks = iter(jax.random.split(key, 40))
    nrm = lambda shape, scale: jax.random.normal(next(ks), shape, jnp.float32) * scale
    gain = lambda shape: 1.0 + nrm(shape, 0.1)
    d = D_MODEL
    x = nrm((BATCH, SEQ, d), 1.0)
    positions = (jax.random.randint(next(ks), (BATCH, 1), 0, 8192, dtype=jnp.int32)
                 + jnp.arange(SEQ, dtype=jnp.int32)[None, :])
    return {
        'x': x,
        'positions': positions,
        'ev_norm_mix': gain((N_EVEN, d)),
        'ev_w_in': nrm((N_EVEN, d, EVEN_IN), d ** -0.5),
        'ev_g_cq': gain((N_EVEN, A_Q_LORA)),
        'ev_g_ckv': gain((N_EVEN, A_KV_LORA)),
        'ev_w_uq': nrm((N_EVEN, A_Q_LORA, A_HEADS, A_NOPE + A_ROPE), A_Q_LORA ** -0.5),
        'ev_w_ukv': nrm((N_EVEN, A_KV_LORA, A_HEADS, A_NOPE + A_V), A_KV_LORA ** -0.5),
        'ev_a_qnorm': gain((N_EVEN, A_NOPE + A_ROPE)),
        'ev_a_knorm': gain((N_EVEN, A_NOPE + A_ROPE)),
        'ev_b_qnorm': gain((N_EVEN, B_DH)),
        'ev_b_knorm': gain((N_EVEN, B_DH)),
        'ev_b_rel_bias': nrm((N_EVEN, B_HEADS, 2 * B_REL_CLIP + 1), 0.5),
        'ev_w_out': nrm((N_EVEN, EVEN_MIX, d), EVEN_MIX ** -0.5),
        'ev_norm_ff': gain((N_EVEN, d)),
        'ev_ff_gate': nrm((N_EVEN, d, FF_DENSE), d ** -0.5),
        'ev_ff_up': nrm((N_EVEN, d, FF_DENSE), d ** -0.5),
        'ev_ff_down': nrm((N_EVEN, FF_DENSE, d), FF_DENSE ** -0.5),
        'od_norm_mix': gain((N_ODD, d)),
        'od_w_qkv': nrm((N_ODD, d, 3 * C_MIX), d ** -0.5),
        'od_c_qnorm': gain((N_ODD, C_DH)),
        'od_c_knorm': gain((N_ODD, C_DH)),
        'od_lam_q1': nrm((N_ODD, C_DH), 0.1),
        'od_lam_k1': nrm((N_ODD, C_DH), 0.1),
        'od_lam_q2': nrm((N_ODD, C_DH), 0.1),
        'od_lam_k2': nrm((N_ODD, C_DH), 0.1),
        'od_c_subnorm': gain((N_ODD, 2 * C_DH)),
        'od_w_out': nrm((N_ODD, C_MIX, d), C_MIX ** -0.5),
        'od_norm_ff': gain((N_ODD, d)),
        'od_router': nrm((N_ODD, d, N_EXPERTS), d ** -0.5),
        'od_ex_gate': nrm((N_ODD, N_EXPERTS, d, FF_EXPERT), d ** -0.5),
        'od_ex_up': nrm((N_ODD, N_EXPERTS, d, FF_EXPERT), d ** -0.5),
        'od_ex_down': nrm((N_ODD, N_EXPERTS, FF_EXPERT, d), FF_EXPERT ** -0.5),
    }

def reference(x, positions, ev_norm_mix, ev_w_in, ev_g_cq, ev_g_ckv, ev_w_uq, ev_w_ukv,
              ev_a_qnorm, ev_a_knorm, ev_b_qnorm, ev_b_knorm, ev_b_rel_bias, ev_w_out,
              ev_norm_ff, ev_ff_gate, ev_ff_up, ev_ff_down,
              od_norm_mix, od_w_qkv, od_c_qnorm, od_c_knorm, od_lam_q1, od_lam_k1,
              od_lam_q2, od_lam_k2, od_c_subnorm, od_w_out, od_norm_ff, od_router,
              od_ex_gate, od_ex_up, od_ex_down):
    b, s_len, _ = x.shape
    cos_a, sin_a = rope_tables(positions, A_ROPE, A_THETA)
    cos_c, sin_c = rope_tables(positions, C_ROPE, ROPE_THETA)
    o1 = A_Q_LORA
    o2 = o1 + A_KV_LORA
    o3 = o2 + A_ROPE
    bw = B_HEADS * B_DH
    h = x
    for layer in range(DEPTH):
        i = layer // 2
        if layer % 2 == 0:
            u = rmsnorm(h, ev_norm_mix[i]) @ ev_w_in[i]
            ya = mla_attention(u[..., :o1], u[..., o1:o2], u[..., o2:o3], cos_a, sin_a,
                               ev_g_cq[i], ev_g_ckv[i], ev_w_uq[i], ev_w_ukv[i],
                               ev_a_qnorm[i], ev_a_knorm[i])
            qb = rmsnorm(split_heads(u[..., o3:o3 + bw], B_HEADS), ev_b_qnorm[i])
            kb = rmsnorm(split_heads(u[..., o3 + bw:o3 + 2 * bw], B_HEADS), ev_b_knorm[i])
            vb = split_heads(u[..., o3 + 2 * bw:o3 + 3 * bw], B_HEADS)
            yb = band_attention(qb, kb, vb, ev_b_rel_bias[i])
            y = jnp.concatenate([ya, yb], axis=1).transpose(0, 2, 1, 3).reshape(b, s_len, EVEN_MIX)
            h = h + y @ ev_w_out[i]
            h = h + swiglu(rmsnorm(h, ev_norm_ff[i]), ev_ff_gate[i], ev_ff_up[i], ev_ff_down[i])
        else:
            qkv = rmsnorm(h, od_norm_mix[i]) @ od_w_qkv[i]
            q, k, v = jnp.split(qkv, 3, axis=-1)
            q = q.reshape(b, s_len, C_HEADS, 2, C_DH).transpose(0, 2, 3, 1, 4)
            k = k.reshape(b, s_len, C_HEADS, 2, C_DH).transpose(0, 2, 3, 1, 4)
            v = v.reshape(b, s_len, C_HEADS, 2 * C_DH).transpose(0, 2, 1, 3)
            lam_init = 0.8 - 0.6 * math.exp(-0.3 * layer)
            yc = diff_attention(q, k, v, cos_c, sin_c, od_c_qnorm[i], od_c_knorm[i],
                                od_lam_q1[i], od_lam_k1[i], od_lam_q2[i], od_lam_k2[i],
                                od_c_subnorm[i], lam_init)
            h = h + yc.transpose(0, 2, 1, 3).reshape(b, s_len, C_MIX) @ od_w_out[i]
            h = h + moe_swiglu(rmsnorm(h, od_norm_ff[i]), od_router[i], od_ex_gate[i],
                               od_ex_up[i], od_ex_down[i])
    return h


_drawn_inputs = setup_inputs


def setup_inputs(seed=0):
    import zlib

    import numpy as np

    out = dict(_drawn_inputs(seed))
    spreads = {}
    factors = {'od_lam_k1': 8.0, 'od_lam_k2': 6.587}
    for name, (base, spread) in spreads.items():
        noise = np.random.default_rng([zlib.crc32(name.encode()), seed]).standard_normal(out[name].shape)
        drawn = base * np.exp(spread * noise) if base else spread * noise
        out[name] = __import__('jax').numpy.asarray(drawn.astype(out[name].dtype))
    for name, factor in factors.items():
        out[name] = (out[name] * factor).astype(out[name].dtype)
    return out
```

```python
import math
from contextlib import ExitStack

import numpy as np

import concourse.bass as bass
from concourse import mybir

F32 = mybir.dt.float32
I32 = mybir.dt.int32
ALU = mybir.AluOpType
ACT = mybir.ActivationFunctionType
AX = mybir.AxisListType

P = 128
D = 1024
T = 256
TT = T // P
DC = D // P
CHUNK = 64
EPS = 1e-6
NEG = -1e30

A_HEADS, A_NOPE, A_ROPE, A_V, A_QL, A_KVL = 8, 64, 32, 64, 256, 128
A_QK = A_NOPE + A_ROPE
B_HEADS, B_DH, B_CLIP = 8, 64, 128
EVEN_IN = A_QL + A_KVL + A_ROPE + 3 * B_HEADS * B_DH
O_CKV = A_QL
O_KR = O_CKV + A_KVL
O_BQ = O_KR + A_ROPE
O_BK = O_BQ + B_HEADS * B_DH
O_BV = O_BK + B_HEADS * B_DH
C_HEADS, C_DH, C_ROPE = 8, 64, 16
C_MIX = C_HEADS * 2 * C_DH
C_GROUPS = 2 * C_HEADS
FF = 2752
E = 8
FE = 3584
N = 512

RING = 7
SLOT = 4096
FCH = -(-FF // N)
FK = -(-FF // P)
ECH = FE // N
SPARE = 3
ITEMS = E + SPARE
FAR = 1024.0

G_MIX0, G_FF0, G_MIX1, G_FF1 = 0, 8, 16, 24
G_C = 32
G_AQ, G_AK, G_BQ, G_BK, G_CQ, G_CK, G_SUB = 35, 36, 37, 38, 39, 40, 41
G_ROWS = 42

FREQ = np.concatenate([
    np.float32(1.0) / (np.float32(theta) ** (np.arange(0, dim, 2, dtype=np.float32) / np.float32(dim)))
    for dim, theta in ((A_ROPE, 10000.0), (C_ROPE, 500000.0))]).astype(np.float32)
NF_A = A_ROPE // 2
NF_C = C_ROPE // 2
NF = NF_A + NF_C
TURN_1 = 6.28125
TURN_2 = float(np.float32(round((2 * math.pi - TURN_1) * 2 ** 21) / 2 ** 21))
TURN_3 = 2 * math.pi - TURN_1 - TURN_2
ROUND = 1.5 * 2 ** 23
PI_BELOW = 3.1415925
LAM_INIT = 0.8 - 0.6 * math.exp(-0.3 * 1)


def weight_stream():
    s = [("in", j) for j in range(-(-EVEN_IN // N))] + [("up_a", 0)]
    s += [("out0", 0), ("out0", 1)]
    for j in range(FCH):
        s += [("gate", j), ("up", j)]
    s += [("down", j) for j in range(-(-FK // 4))]
    s += [("qkv", j) for j in range(3 * C_MIX // N)]
    s += [("out1", 0), ("out1", 1)]
    return s


def expert_stream():
    s = []
    for j in range(ECH):
        s += [("gate", j), ("up", j)]
        if j >= 2:
            s.append(("down", j - 2))
    return s + [("down", ECH - 2), ("down", ECH - 1)]


STREAM = weight_stream()
FIRST_RING = 5
EXPERT = expert_stream()
assert len(EXPERT) % RING == 0 and (len(STREAM) - FIRST_RING) % RING == 0


def slot_of(n):
    return n if n < FIRST_RING else (n - FIRST_RING) % RING


def uses(n):
    return sum((2 if STREAM[m][0] == "up_a" else 1) for m in range(n + 1) if slot_of(m) == slot_of(n))


AT = {item: n for n, item in enumerate(STREAM)}
SLOT_USES = [max(uses(n) for n in range(len(STREAM)) if slot_of(n) == s) for s in range(RING)]


def trunk(nc, w, out):
    with ExitStack() as ctx:
        ctx.enter_context(nc.allow_non_contiguous_dma(reason="short gain, position and router loads"))

        def sb(name, shape, dt=F32):
            return ctx.enter_context(nc.sbuf_tensor(name, shape, dt))

        def sem(name):
            return ctx.enter_context(nc.semaphore(name))

        ring = sb("ring", [P, RING, SLOT])
        h = sb("h", [P, TT, D])
        xT = sb("xT", [P, DC, T])
        xs = sb("xs", [P, TT, D])
        ident = sb("ident", [P, P])
        tri = sb("tri", [P, P])
        ones = sb("ones", [P, P])
        slots_i = sb("slots_i", [P, P], I32)
        slots_f = sb("slots_f", [P, P])
        mask = sb("mask", [P, 384])
        eps = sb("eps", [P, 1])
        freq = sb("freq", [P, NF])
        gain_rows = sb("gain_rows", [G_ROWS, P])
        gcol = sb("gcol", [P, G_ROWS])
        ga_rot = sb("ga_rot", [P, 2, A_ROPE])
        gc_rot = sb("gc_rot", [P, 2, C_ROPE])
        lamv = sb("lamv", [P, 4, C_DH])
        lams = sb("lams", [P, 8])
        pos_i = sb("pos_i", [P, TT], I32)
        pos_f = sb("pos_f", [P, TT])
        router = sb("router", [P, DC, E])
        trig = sb("trig", [P, 2, TT, NF])
        turns = sb("turns", [P, 2, TT, NF])
        angle = sb("angle", [P, TT, NF])
        ssq = sb("ssq", [P, 8])
        root = sb("root", [P, 8])
        rstd = sb("rstd", [P, 8])
        ss = sb("ss", [P, 64])
        rs = sb("rs", [P, 64])
        negmax = sb("negmax", [P, 2 * C_HEADS, TT])
        psum_l = sb("psum_l", [P, 2 * C_HEADS, TT])
        rinv = sb("rinv", [P, 2 * C_HEADS, TT])
        coef = sb("coef", [P, C_HEADS, TT])
        gate_t = sb("gate_t", [P, 12, TT, E])
        gate_s = sb("gate_s", [P, 12, TT])
        rank = sb("rank", [P, TT, ITEMS])
        comb = sb("comb", [P, TT, ITEMS])
        load8 = sb("load8", [P, 8, E])
        over_s = sb("over_s", [P, 8])
        over_i = sb("over_i", [P, 4], I32)
        WORK = 15168
        work = sb("work", [P, WORK])

        def carve(base, at, *dims):
            n = math.prod(dims)
            assert at + n <= base.shape[1]
            v = base[:, at:at + n]
            names = "abc"[:len(dims)]
            if len(dims) == 1:
                return v
            return v.rearrange(f"p ({' '.join(names)}) -> p {' '.join(names)}",
                               **{k: d for k, d in zip(names[1:], dims[1:])})

        tail = ring[:, 5:7, :].rearrange("p a b -> p (a b)")
        u0 = carve(work, 0, TT, EVEN_IN)
        qa = carve(work, 3904, TT, A_HEADS * A_QK)
        kva = carve(work, 5440, TT, A_HEADS * (A_NOPE + A_V))
        ka = carve(work, 7488, TT, A_HEADS * A_QK)
        bias = carve(work, 9024, B_HEADS, 384)
        s0 = carve(work, 12096, 8, 384)
        qta, kta = carve(tail, 0, A_HEADS, T), carve(tail, 2048, A_HEADS, T)
        qtb, ktb = carve(tail, 4096, B_HEADS // 2, T), carve(tail, 5120, B_HEADS // 2, T)
        pt0 = carve(tail, 6144, 2, 384)
        cT = carve(tail, 6912, 3, T)
        bias_rev = carve(tail, 0, B_HEADS, T)
        rel = carve(work, 5440, 384)[0:B_HEADS, :]
        sq0 = carve(work, 12096, TT, O_BV)
        sqa = carve(work, 12096, TT * A_HEADS, A_QK)
        sqk = carve(work, 12096 + 1536, TT, A_HEADS, A_NOPE)
        xs_flat = xs[:, :, :].rearrange("p a b -> p (a b)")
        rot_a = [carve(xs_flat, 256 * n, TT, A_HEADS, NF_A) for n in range(4)]
        rot_k = [carve(xs_flat, 1024 + 64 * n, TT, NF_A) for n in range(4)]
        rot_c = [carve(xs_flat, 512 * n, TT, 2 * C_GROUPS, NF_C) for n in range(4)]
        kr = carve(xs_flat, 1280, TT, A_ROPE)
        u1 = carve(work, 0, TT, 3 * C_MIX)
        qtc, ktc = carve(work, 6144, C_HEADS, T), carve(work, 8192, C_HEADS, T)
        sqc = carve(work, 6144, TT, 2 * C_MIX)
        s1 = carve(work, 10240, 8, 384)
        sqo = carve(work, 10240, TT, C_MIX)
        pt1 = carve(work, 13312, 2, 384)
        hT0 = carve(work, 0, FK, T)
        sil = carve(work, 5632, 2, N)
        prod = carve(work, 6656, 2, N)
        xg = carve(work, 0, DC, P)
        sel = carve(work, 1024, TT, P)
        wsel = carve(work, 1280, TT, P)
        wselT = carve(work, 1536, TT, P)
        hT1 = carve(work, 1792, 2, 4, P)
        ysb = carve(work, 2816, D)

        ps = ctx.enter_context(nc.psum_tensor("ps", [P, 8, N], F32))

        rel_scratch = nc.dram_tensor("rel_scratch", (B_HEADS, 384), F32, kind="Internal").ap()
        w_in = w["ev_w_in"][0].rearrange("(k p) n -> p k n", p=P)
        w_uq = w["ev_w_uq"][0].rearrange("(k p) h d -> p k (h d)", p=P)
        w_ukv = w["ev_w_ukv"][0].rearrange("p h d -> p (h d)")
        w_out0 = w["ev_w_out"][0].rearrange("(k p) n -> p k n", p=P)
        w_out1 = w["od_w_out"][0].rearrange("(k p) n -> p k n", p=P)
        ff_gate = w["ev_ff_gate"][0].rearrange("(k p) n -> p k n", p=P)
        ff_up = w["ev_ff_up"][0].rearrange("(k p) n -> p k n", p=P)
        ff_down = w["ev_ff_down"][0]
        w_qkv = w["od_w_qkv"][0].rearrange("(k p) n -> p k n", p=P)
        ex_gate = w["od_ex_gate"][0].rearrange("e (k p) n -> e p k n", p=P)
        ex_up = w["od_ex_up"][0].rearrange("e (k p) n -> e p k n", p=P)
        ex_down = w["od_ex_down"][0].rearrange("e (k p) n -> e p k n", p=P)

        landed = [sem(f"landed{s}") for s in range(RING)]
        x_landed = sem("x_landed")
        gains_landed = sem("gains_landed")
        rows_landed = sem("rows_landed")
        rel_landed = sem("rel_landed")
        rel_extended = sem("rel_extended")
        rel_stored = sem("rel_stored")
        bias_landed = sem("bias_landed")
        pool_chain = sem("pool_chain")
        gain_ones = sem("gain_ones")
        consts_ready = sem("consts_ready")
        gains_turned = sem("gains_turned")
        gains_ready = sem("gains_ready")
        vec_chain = sem("vec_chain")
        act_chain = sem("act_chain")
        angles_ready = sem("angles_ready")
        trig_ready = sem("trig_ready")
        root_ready = sem("root_ready")
        xs_ready = sem("xs_ready")
        xT_psum = sem("xT_psum")
        xT_ready = sem("xT_ready")
        proj_psum = [sem("proj_psum0"), sem("proj_psum1")]
        proj_act = [sem("proj_act0"), sem("proj_act1")]
        proj_vec = [sem("proj_vec0"), sem("proj_vec1")]
        u_squared = sem("u_squared")
        u_sums = sem("u_sums")
        u_roots = sem("u_roots")
        c_normed = sem("c_normed")
        c_psum = sem("c_psum")
        c_ready = sem("c_ready")
        up_psum = sem("up_psum")
        up_act = sem("up_act")
        up_vec = sem("up_vec")
        a_squared = sem("a_squared")
        a_sums = sem("a_sums")
        a_roots = sem("a_roots")
        qk_normed = sem("qk_normed")
        qk_psum = sem("qk_psum")
        q_turned = sem("q_turned")
        k_turned = sem("k_turned")
        scores_psum = sem("scores_psum")
        scores_read = sem("scores_read")
        max_ready = sem("max_ready")
        exp_done = sem("exp_done")
        diff_done = sem("diff_done")
        p_psum = sem("p_psum")
        p_turned = sem("p_turned")
        pv_done = sem("pv_done")
        y_ready = sem("y_ready")
        yT_psum = sem("yT_psum")
        yT_ready = sem("yT_ready")
        out_psum = sem("out_psum")
        h_ready = sem("h_ready")
        lam_sums = sem("lam_sums")
        lam_exps = sem("lam_exps")
        o_normed = sem("o_normed")
        o_squared = sem("o_squared")
        o_roots = sem("o_roots")
        ff_gate_done = sem("ff_gate_done")
        ff_up_done = sem("ff_up_done")
        ff_silu = sem("ff_silu")
        ff_prod = sem("ff_prod")
        ff_turned = sem("ff_turned")
        ff_hT = sem("ff_hT")
        ff_down_used = sem("ff_down_used")
        ff_down_psum = sem("ff_down_psum")
        logits_psum = sem("logits_psum")
        gate_diff = sem("gate_diff")
        gate_exp = sem("gate_exp")
        chosen_ready = sem("chosen_ready")
        rank_psum = sem("rank_psum")
        routed = sem("routed")
        sel_ready = sem("sel_ready")
        wselT_psum = sem("wselT_psum")
        wselT_ready = sem("wselT_ready")
        gather_psum = sem("gather_psum")
        xg_ready = sem("xg_ready")
        gate_done = sem("gate_done")
        up_done = sem("up_done")
        down_done = sem("down_done")
        silu_done = sem("silu_done")
        prod_done = sem("prod_done")
        turn_done = sem("turn_done")
        hT_ready = sem("hT_ready")
        y_act = sem("y_act")
        y_vec = sem("y_vec")
        scatter_psum = sem("scatter_psum")
        scatter_read = sem("scatter_read")
        h_final = sem("h_final")
        stored = sem("stored")

        n_gains = 17
        n_rows = 10
        IN_J = -(-EVEN_IN // N)
        QKV_J = 3 * C_MIX // N

        def cols(j, total):
            return j * N, min(N, total - j * N)

        def blocks(bank, n=4):
            return ps[:, bank, 0:n * P].rearrange("p (a b) -> p a b", b=P)

        def gains(first, n, width):
            return gcol[:, first:first + n].unsqueeze(2).to_broadcast([P, n, width])

        block = ctx.enter_context(nc.Block())

        @block.sync
        def _(sp):
            sp.dma_start(h[:, :, :], w["x"][0].rearrange("(t p) d -> p t d", p=P)).then_inc(x_landed, 16)

            def slot_free(n):
                if n < FIRST_RING:
                    return
                before = [m for m in range(n) if slot_of(m) == slot_of(n)]
                if not before:
                    sp.wait_ge(pv_done, A_HEADS + B_HEADS)
                    return
                kind, j = STREAM[before[-1]]
                if kind == "in":
                    sp.wait_ge(proj_psum[0], 2 * j + 2)
                elif kind == "up_a":
                    sp.wait_ge(up_psum, 8)
                elif kind == "out0":
                    sp.wait_ge(out_psum, 4)
                elif kind == "gate":
                    sp.wait_ge(ff_gate_done, 2 * j + 2)
                elif kind == "up":
                    sp.wait_ge(ff_up_done, 2 * j + 2)
                elif kind == "down" and j == FK // 4:
                    sp.wait_ge(ff_down_psum, 4)
                elif kind == "down":
                    sp.wait_ge(ff_down_used, j + 1)
                elif kind == "qkv":
                    sp.wait_ge(proj_psum[1], 2 * j + 2)
                else:
                    sp.wait_ge(out_psum, 8)

            for n, (kind, j) in enumerate(STREAM):
                slot_free(n)
                s = slot_of(n)
                if kind in ("in", "gate", "up", "qkv"):
                    src, total = {"in": (w_in, EVEN_IN), "gate": (ff_gate, FF), "up": (ff_up, FF),
                                  "qkv": (w_qkv, 3 * C_MIX)}[kind]
                    a, m = cols(j, total)
                    sp.dma_start(carve(ring[:, s, :], 0, DC, m), src[:, :, a:a + m]).then_inc(landed[s], 16)
                elif kind == "up_a":
                    sp.dma_start(carve(ring[:, s, :], 0, 2, A_HEADS * A_QK), w_uq).then_inc(landed[s], 16)
                    sp.dma_start(ring[:, s, 2048:3072], w_ukv).then_inc(landed[s], 16)
                elif kind in ("out0", "out1"):
                    src = w_out0 if kind == "out0" else w_out1
                    sp.dma_start(carve(ring[:, s, :], 0, 4, D), src[:, 4 * j:4 * j + 4, :]).then_inc(landed[s], 16)
                else:
                    k0, k1 = 4 * j, min(4 * j + 4, FK)
                    whole = FF // P
                    if k1 <= whole:
                        sp.dma_start(carve(ring[:, s, :], 0, 4, D),
                                     ff_down[k0 * P:k1 * P, :].rearrange("(k p) n -> p k n", p=P)).then_inc(landed[s], 16)
                    else:
                        assert whole - k0 == 1
                        sp.dma_start(ring[:, s, 0:D], ff_down[k0 * P:whole * P, :]).then_inc(landed[s], 16)
                        sp.dma_start(ring[0:FF - whole * P, s, D:2 * D], ff_down[whole * P:FF, :]).then_inc(landed[s], 16)

            def load_expert(i, e, before_first):
                for q, (kind, j) in enumerate(EXPERT):
                    s = q % RING
                    used = {"gate": gate_done, "up": up_done, "down": down_done}
                    if q >= RING:
                        k, m = EXPERT[q - RING]
                        sp.wait_ge(used[k], i * ECH + m + 1)
                    elif before_first:
                        slot_free(len(STREAM) + q)
                    else:
                        k, m = EXPERT[q - RING + len(EXPERT)]
                        sp.wait_ge(used[k], i * ECH + m + 1 - ECH)
                    if kind == "down":
                        dst = carve(ring[:, s, :], 0, 4, D)
                        src = ex_down[bass.ds(e, 1), :, 4 * j:4 * j + 4, :] if not isinstance(e, int) else ex_down[e:e + 1, :, 4 * j:4 * j + 4, :]
                    else:
                        dst = carve(ring[:, s, :], 0, DC, N)
                        m = ex_gate if kind == "gate" else ex_up
                        src = m[bass.ds(e, 1), :, :, j * N:(j + 1) * N] if not isinstance(e, int) else m[e:e + 1, :, :, j * N:(j + 1) * N]
                    sp.dma_start(dst, src.rearrange("e p k n -> p (e k) n")).then_inc(landed[s], 16)

            load_expert(0, 0, True)
            with sp.Fori(1, E) as i:
                load_expert(i, i, False)
            sp.wait_ge(routed, 1)
            n_over = sp.value_load(over_i[0:1, SPARE:SPARE + 1], min_val=0, max_val=SPARE)
            for s in range(SPARE):
                with sp.If(n_over > s):
                    e = sp.value_load(over_i[0:1, s:s + 1], min_val=0, max_val=E - 1)
                    load_expert(E + s, e, False)
            sp.wait_ge(h_final, 1)
            sp.dma_start(out[0].rearrange("(t p) d -> p t d", p=P), h[:, :, :]).then_inc(stored, 16)
            sp.wait_ge(stored, 16)

        @block.gpsimd
        def _(pool):
            pool.memset(gain_rows[:, :], 1.0).then_inc(gain_ones, 1)
            pool.memset(ident[:, :], 0.0).then_inc(pool_chain, 1)
            pool.memset(tri[:, :], 1.0).then_inc(pool_chain, 1)
            pool.memset(mask[:, :], 0.0).then_inc(pool_chain, 1)
            pool.wait_ge(pool_chain, 3)
            pool.affine_select(out=ident[:, :], in_=ident[:, :], compare_op=ALU.not_equal, fill=1.0,
                               base=0, pattern=[[-1, P]], channel_multiplier=1).then_inc(consts_ready, 1)
            pool.affine_select(out=tri[:, :], in_=tri[:, :], compare_op=ALU.is_gt, fill=0.0,
                               base=0, pattern=[[1, P]], channel_multiplier=-1).then_inc(consts_ready, 1)
            pool.memset(mask[0:CHUNK, CHUNK:P], NEG).then_inc(consts_ready, 1)
            pool.memset(mask[0:CHUNK, 384 - CHUNK:384], NEG).then_inc(consts_ready, 1)
            pool.memset(ones[:, :], 1.0).then_inc(consts_ready, 1)
            pool.memset(eps[:, :], EPS).then_inc(consts_ready, 1)
            for f in range(NF):
                pool.memset(freq[:, f:f + 1], float(FREQ[f])).then_inc(consts_ready, 1)
            pool.iota(slots_i[:, :], pattern=[[1, P]], base=0, channel_multiplier=0).then_inc(consts_ready, 1)

        n_consts = 6 + NF + 1

        @block.scalar
        def _(act):
            chain = [0]

            def link(ins):
                chain[0] += 1
                ins.then_inc(act_chain, 1)
                act.wait_ge(act_chain, chain[0])

            act.wait_ge(gain_ones, 1)
            for first, name in ((G_MIX0, "ev_norm_mix"), (G_FF0, "ev_norm_ff"), (G_MIX1, "od_norm_mix"), (G_FF1, "od_norm_ff")):
                act.dma_start(gain_rows[first:first + DC, :], w[name][0].rearrange("(k p) -> k p", p=P)).then_inc(gains_landed, 16)
            act.dma_start(gain_rows[G_C:G_C + 2, :], w["ev_g_cq"][0].rearrange("(k p) -> k p", p=P)).then_inc(gains_landed, 16)
            act.dma_start(gain_rows[G_C + 2:G_C + 3, :], w["ev_g_ckv"]).then_inc(gains_landed, 16)
            act.dma_start(gain_rows[G_SUB:G_SUB + 1, :], w["od_c_subnorm"]).then_inc(gains_landed, 16)
            for row, name in ((G_AQ, "ev_a_qnorm"), (G_AK, "ev_a_knorm")):
                act.dma_start(gain_rows[row:row + 1, 0:A_NOPE], w[name][:, 0:A_NOPE]).then_inc(gains_landed, 16)
            for row, name in ((G_BQ, "ev_b_qnorm"), (G_BK, "ev_b_knorm")):
                for m in range(2):
                    act.dma_start(gain_rows[row:row + 1, m * B_DH:(m + 1) * B_DH], w[name]).then_inc(gains_landed, 16)
            for row, name in ((G_CQ, "od_c_qnorm"), (G_CK, "od_c_knorm")):
                for m in range(2):
                    act.dma_start(gain_rows[row:row + 1, m * C_DH + C_ROPE:(m + 1) * C_DH], w[name][:, C_ROPE:C_DH]).then_inc(gains_landed, 16)
            act.dma_start(pos_i[:, :], w["positions"][0].rearrange("(t p) -> p t", p=P)).then_inc(rows_landed, 16)
            act.dma_start(rel[:, 0:2 * B_CLIP + 1], w["ev_b_rel_bias"][0]).then_inc(rel_landed, 16)
            for m, name in enumerate(("ev_a_qnorm", "ev_a_knorm")):
                act.dma_start(ga_rot[:, m, :], w[name][0, A_NOPE:A_QK].partition_broadcast(P)).then_inc(rows_landed, 16)
            for m, name in enumerate(("od_c_qnorm", "od_c_knorm")):
                act.dma_start(gc_rot[:, m, :], w[name][0, 0:C_ROPE].partition_broadcast(P)).then_inc(rows_landed, 16)
            for m, name in enumerate(("od_lam_q1", "od_lam_k1", "od_lam_q2", "od_lam_k2")):
                act.dma_start(lamv[:, m, :], w[name][0].partition_broadcast(P)).then_inc(rows_landed, 16)
            act.dma_start(router[:, :, :], w["od_router"][0].rearrange("(k p) e -> p k e", p=P)).then_inc(rows_landed, 16)

            def norm_roots(k):
                for t in range(TT):
                    if k == 0:
                        act.wait_ge(x_landed, 16)
                        act.wait_ge(consts_ready, n_consts)
                    else:
                        act.wait_ge(h_ready, 4 * k)
                    if k:
                        act.wait_ge(xT_psum, 4 * k)
                    link(act.activation(xs[:, t, :], h[:, t, :], ACT.Square, accum_out=ssq[:, 2 * k + t:2 * k + t + 1]))
                    act.activation(root[:, 2 * k + t:2 * k + t + 1], ssq[:, 2 * k + t:2 * k + t + 1], ACT.Sqrt,
                                   scale=1.0 / D, bias=eps[:, 0:1]).then_inc(root_ready, 1)

            def project(layer, u, total):
                for j in range(-(-total // N)):
                    a, m = cols(j, total)
                    act.wait_ge(proj_psum[layer], 2 * j + 1)
                    act.activation(u[:, 0, a:a + m], ps[:, 4 + 2 * (j % 2), 0:m], ACT.Copy).then_inc(proj_act[layer], 1)

            def turn_q(f, dst, rows, col):
                act.wait_ge(qk_psum, f + 1)
                act.activation(dst, blocks(f % 4)[0:rows], ACT.Copy, scale=gcol[0:rows, col:col + 1]).then_inc(q_turned, 1)

            def exponentials(u, unit, s):
                act.wait_ge(max_ready, unit + 1)
                act.activation(s[:, u % 8, 0:P], s[:, u % 8, 0:P], ACT.Exp,
                               bias=negmax[:, u, 0:1], accum_out=psum_l[:, u, 0:1])
                act.activation(s[:, u % 8, P:384], s[:, u % 8, P:384], ACT.Exp,
                               bias=negmax[:, u, 1:2], accum_out=psum_l[:, u, 1:2]).then_inc(exp_done, 1)

            def turn_p(head, pt):
                act.wait_ge(p_psum, head + 1)
                if head >= 2:
                    act.wait_ge(pv_done, head - 1)
                act.activation(pt[:, head % 2, :], ps[:, 2 + head % 2, 0:384], ACT.Copy).then_inc(p_turned, 1)

            def turn_y(layer):
                for f in range(4):
                    half, t = divmod(f, TT)
                    act.wait_ge(yT_psum, 4 * layer + f + 1)
                    scale = 1.0 if layer == 0 else gcol[:, G_SUB:G_SUB + 1]
                    act.activation(xT[:, 4 * half:4 * half + 4, t * P:(t + 1) * P], blocks(f), ACT.Copy,
                                   scale=scale).then_inc(yT_ready, 1)

            norm_roots(0)
            project(0, u0, EVEN_IN)
            act.wait_ge(proj_vec[0], IN_J)
            act.wait_ge(proj_act[0], IN_J)
            act.activation(sq0, u0[:, :, 0:O_BV], ACT.Square).then_inc(u_squared, 1)
            act.wait_ge(u_sums, 1)
            act.activation(rs[:, 0:2], ss[:, 0:2], ACT.Sqrt, scale=1.0 / A_QL, bias=eps[:, 0:1])
            act.activation(rs[:, 2:4], ss[:, 2:4], ACT.Sqrt, scale=1.0 / A_KVL, bias=eps[:, 0:1])
            act.activation(rs[:, 4:6], ss[:, 4:6], ACT.Sqrt, scale=1.0 / A_ROPE, bias=eps[:, 0:1])
            act.activation(rs[:, 6:38], ss[:, 6:38], ACT.Sqrt, scale=1.0 / B_DH, bias=eps[:, 0:1]).then_inc(u_roots, 1)
            for t in range(TT):
                for m, (a, n) in enumerate(((0, 512), (512, 256))):
                    act.wait_ge(up_psum, 4 * t + m + 1)
                    act.activation(qa[:, t, a:a + n], ps[:, (4 + m) if t == 0 else m, 0:n], ACT.Copy).then_inc(up_act, 1)
            act.wait_ge(up_act, 4)
            act.wait_ge(up_vec, 4)
            act.activation(sqa, qa.rearrange("p t (g d) -> p (t g) d", d=A_QK), ACT.Square)
            act.activation(sqk, kva.rearrange("p t (g d) -> p t g d", d=A_NOPE + A_V)[:, :, :, 0:A_NOPE],
                           ACT.Square).then_inc(a_squared, 1)
            act.wait_ge(a_sums, 1)
            act.activation(rs[:, 0:32], ss[:, 0:32], ACT.Sqrt, scale=1.0 / A_NOPE, bias=eps[:, 0:1])
            act.activation(rs[:, 32:48], ss[:, 32:48], ACT.Sqrt, scale=1.0 / A_ROPE, bias=eps[:, 0:1]).then_inc(a_roots, 1)
            act.wait_ge(angles_ready, 1)
            act.activation(trig[:, :, :, :], turns[:, :, :, :], ACT.Sin).then_inc(trig_ready, 1)
            for t in range(TT):
                for half in range(2):
                    turn_q(4 * t + 2 * half, qta[0:A_QK, 4 * half:4 * half + 4, t * P:(t + 1) * P], A_QK, G_AQ)
            for t in range(TT):
                turn_q(8 + 2 * t, qtb[:, :, t * P:(t + 1) * P], P, G_BQ)
            act.wait_ge(lam_sums, 1)
            act.activation(lams[:, 2:4], lams[:, 0:2], ACT.Exp).then_inc(lam_exps, 1)
            for i in range(A_HEADS + B_HEADS + 2):
                if i < A_HEADS + B_HEADS:
                    exponentials(i, i, s0)
                if i >= 2:
                    turn_p(i - 2, pt0)
            turn_y(0)

            norm_roots(1)
            FS = TT * FCH
            for s in range(FS + 1):
                if s < FS:
                    m = cols(s // TT, FF)[1]
                    act.wait_ge(ff_gate_done, s + 1)
                    if s >= 2:
                        act.wait_ge(ff_prod, s - 1)
                    act.activation(sil[:, s % 2, 0:m], ps[:, 2 * (s % 2), 0:m], ACT.Silu).then_inc(ff_silu, 1)
                if s >= 1:
                    j, t = divmod(s - 1, TT)
                    m = cols(j, FF)[1]
                    act.wait_ge(ff_turned, s)
                    whole = m // P
                    bank = 4 + (s - 1) % 2
                    if m % P:
                        act.activation(hT0[0:m % P, 4 * j + whole, t * P:(t + 1) * P],
                                       ps[0:m % P, bank, whole * P:(whole + 1) * P], ACT.Copy)
                    act.activation(hT0[:, 4 * j:4 * j + whole, t * P:(t + 1) * P], blocks(bank, whole), ACT.Copy).then_inc(ff_hT, 1)

            norm_roots(2)
            project(1, u1, 3 * C_MIX)
            act.wait_ge(proj_vec[1], QKV_J)
            act.wait_ge(proj_act[1], QKV_J)
            act.activation(sqc, u1[:, :, 0:2 * C_MIX], ACT.Square).then_inc(u_squared, 1)
            act.wait_ge(u_sums, 2)
            act.activation(rs[:, :], ss[:, :], ACT.Sqrt, scale=1.0 / C_DH, bias=eps[:, 0:1]).then_inc(u_roots, 1)
            for t in range(TT):
                for half in range(2):
                    turn_q(12 + 4 * t + 2 * half, qtc[:, 4 * half:4 * half + 4, t * P:(t + 1) * P], P, G_CQ)
            for i in range(C_HEADS + 1):
                if i < C_HEADS:
                    for m in range(2):
                        exponentials(2 * i + m, A_HEADS + B_HEADS + 2 * i + m, s1)
                if i >= 1:
                    turn_p(A_HEADS + B_HEADS + i - 1, pt1)
            act.wait_ge(o_normed, 1)
            act.activation(sqo, xs[:, :, :], ACT.Square).then_inc(o_squared, 1)
            act.wait_ge(o_squared, 2)
            act.activation(rs[:, 0:16], ss[:, 0:16], ACT.Sqrt, scale=1.0 / (2 * C_DH), bias=eps[:, 0:1]).then_inc(o_roots, 1)
            turn_y(1)

            norm_roots(3)
            act.wait_ge(gate_diff, 1)
            act.activation(gate_s[:, 5, :], gate_s[:, 4, :], ACT.Exp).then_inc(gate_exp, 1)

            def expert(i):
                act.wait_ge(wselT_psum, i + 1)
                act.activation(wselT, blocks(4, 2), ACT.Copy).then_inc(wselT_ready, 1)
                for j in range(ECH + 1):
                    if j < ECH:
                        act.wait_ge(gate_done, i * ECH + j + 1)
                        if j >= 2:
                            act.wait_ge(prod_done, i * ECH + j - 1)
                        act.activation(sil[:, j % 2, :], ps[:, 2 * (j % 2), :], ACT.Silu).then_inc(silu_done, 1)
                    if j >= 1:
                        act.wait_ge(turn_done, i * ECH + j)
                        if j >= 3:
                            act.wait_ge(down_done, i * ECH + j - 2)
                        act.activation(hT1[:, (j - 1) % 2, :, :], blocks(4 + (j - 1) % 2), ACT.Copy).then_inc(hT_ready, 1)
                act.wait_ge(down_done, i * ECH + ECH)
                act.activation(ysb[:, 0:N], ps[:, 6, :], ACT.Copy).then_inc(y_act, 1)

            with act.Fori(0, E) as i:
                expert(i)
            act.wait_ge(routed, 1)
            n_over = act.value_load(over_i[0:1, SPARE:SPARE + 1], min_val=0, max_val=SPARE)
            for s in range(SPARE):
                with act.If(n_over > s):
                    expert(E + s)

        @block.vector
        def _(dve):
            chain = [0]

            def link(ins):
                chain[0] += 1
                ins.then_inc(vec_chain, 1)
                dve.wait_ge(vec_chain, chain[0])

            def norm_apply(k, first):
                for t in range(TT):
                    c = slice(2 * k + t, 2 * k + t + 1)
                    dve.wait_ge(root_ready, 2 * k + t + 1)
                    link(dve.reciprocal(rstd[:, c], root[:, c]))
                    dve.tensor_scalar(xs[:, t, :], h[:, t, :], rstd[:, c], None, ALU.mult).then_inc(xs_ready, 1)
                if k == 0:
                    turn_gains()
                for t in range(TT):
                    for half in range(2):
                        dve.wait_ge(xT_psum, 4 * k + 2 * t + half + 1)
                        dve.tensor_tensor(xT[:, 4 * half:4 * half + 4, t * P:(t + 1) * P], blocks(2 * t + half),
                                          gains(first + 4 * half, 4, P), ALU.mult).then_inc(xT_ready, 1)

            def turn_gains():
                dve.wait_ge(gains_turned, 1)
                dve.tensor_copy(gcol[:, :], ps[:, 7, 0:G_ROWS]).then_inc(gains_ready, 1)
                dve.wait_ge(gains_ready, 1)
                dve.tensor_scalar(gcol[:, G_SUB:G_SUB + 1], gcol[:, G_SUB:G_SUB + 1], 1.0 - LAM_INIT, None,
                                  ALU.mult).then_inc(gains_ready, 1)

            def project(layer, u, total):
                for j in range(-(-total // N)):
                    a, m = cols(j, total)
                    dve.wait_ge(proj_psum[layer], 2 * j + 2)
                    dve.tensor_copy(u[:, 1, a:a + m], ps[:, 5 + 2 * (j % 2), 0:m]).then_inc(proj_vec[layer], 1)

            def rotate(x1, x2, cos, sin, tmp):
                dve.tensor_tensor(tmp[0], x1, cos, ALU.mult)
                dve.tensor_tensor(tmp[1], x2, sin, ALU.mult)
                dve.tensor_tensor(tmp[2], x2, cos, ALU.mult)
                link(dve.tensor_tensor(tmp[3], x1, sin, ALU.mult))
                dve.tensor_tensor(x1, tmp[0], tmp[1], ALU.subtract)
                link(dve.tensor_tensor(x2, tmp[2], tmp[3], ALU.add))

            def turn_k(f, dst, rows, col):
                dve.wait_ge(qk_psum, f + 1)
                dve.tensor_scalar(dst, blocks(f % 4)[0:rows], gcol[0:rows, col:col + 1], None, ALU.mult).then_inc(k_turned, 1)

            def scores(u, unit, s, scale, added, slot_head):
                dve.wait_ge(scores_psum, unit + 1)
                if slot_head is not None:
                    dve.wait_ge(p_psum, slot_head + 1)
                dve.scalar_tensor_tensor(out=s[:, u % 8, :], in0=ps[:, unit % 2, 0:384], scalar=scale, in1=added,
                                         op0=ALU.mult, op1=ALU.add).then_inc(scores_read, 1)
                dve.wait_ge(scores_read, unit + 1)
                dve.tensor_reduce(negmax[:, u, 0:1], s[:, u % 8, 0:P], AX.X, ALU.max, negate=True)
                dve.tensor_reduce(negmax[:, u, 1:2], s[:, u % 8, P:384], AX.X, ALU.max, negate=True).then_inc(max_ready, 1)

            def add_out(count, banks, sem_psum, base):
                for n in range(4):
                    t, nn = divmod(n, 2)
                    dve.wait_ge(sem_psum, base + n + 1)
                    dve.tensor_tensor(h[:, t, nn * N:(nn + 1) * N], h[:, t, nn * N:(nn + 1) * N],
                                      ps[:, banks[n], :], ALU.add).then_inc(h_ready, 1)

            dve.wait_ge(rel_landed, 16)
            dve.tensor_copy(rel[:, 2 * B_CLIP + 1:384],
                            rel[:, 2 * B_CLIP:2 * B_CLIP + 1].to_broadcast([B_HEADS, 383 - 2 * B_CLIP])).then_inc(rel_extended, 1)
            dve.wait_ge(rows_landed, 16 * n_rows)
            dve.wait_ge(consts_ready, n_consts)
            dve.tensor_copy(slots_f[:, :], slots_i[:, :])
            link(dve.tensor_copy(pos_f[:, :], pos_i[:, :]))
            for t in range(TT):
                ins = dve.tensor_scalar(angle[:, t, :], freq[:, :], pos_f[:, t:t + 1], None, ALU.mult)
            link(ins)
            dve.tensor_scalar(turns[:, 0, :, :], angle[:, :, :], 1.0 / (2 * math.pi), None, ALU.mult)
            link(dve.tensor_scalar(turns[:, 1, :, :], angle[:, :, :], 1.0 / (2 * math.pi), 0.25, ALU.mult, ALU.add))
            link(dve.tensor_scalar(turns[:, :, :, :], turns[:, :, :, :], ROUND, None, ALU.add))
            link(dve.tensor_scalar(turns[:, :, :, :], turns[:, :, :, :], ROUND, None, ALU.subtract))
            for m in range(2):
                ins = dve.scalar_tensor_tensor(out=trig[:, m, :, :], in0=turns[:, m, :, :], scalar=-TURN_1,
                                               in1=angle[:, :, :], op0=ALU.mult, op1=ALU.add)
            link(ins)
            for part in (TURN_2, TURN_3):
                link(dve.scalar_tensor_tensor(out=trig[:, :, :, :], in0=turns[:, :, :, :], scalar=-part,
                                              in1=trig[:, :, :, :], op0=ALU.mult, op1=ALU.add))
            link(dve.tensor_scalar(trig[:, 1, :, :], trig[:, 1, :, :], math.pi / 2, None, ALU.add))
            dve.tensor_scalar(turns[:, :, :, :], trig[:, :, :, :], PI_BELOW, -PI_BELOW, ALU.min, ALU.max).then_inc(angles_ready, 1)
            for m in range(2):
                ins = dve.tensor_tensor(lamv[:, 2 * m, :], lamv[:, 2 * m, :], lamv[:, 2 * m + 1, :], ALU.mult)
            link(ins)
            for m in range(2):
                ins = dve.tensor_reduce(lams[:, m:m + 1], lamv[:, 2 * m, :], AX.X, ALU.add)
            ins.then_inc(lam_sums, 1)

            norm_apply(0, G_MIX0)
            dve.wait_ge(bias_landed, 16 * B_HEADS)
            st = bias_rev.ap[0][0]

            def reversed_keys(head, first, n):
                last = bias_rev[:, head, T - 1 - first:T - first]
                return bass.AP(last.tensor, last.offset, [[st, P], [-1, n]])

            for head in range(B_HEADS):
                dve.tensor_tensor(bias[:, head, 0:P], reversed_keys(head, P, P), mask[:, 0:P], ALU.add)
                ins = dve.tensor_tensor(bias[:, head, P:384], reversed_keys(head, 0, T), mask[:, P:384], ALU.add)
            link(ins)

            project(0, u0, EVEN_IN)
            dve.wait_ge(u_squared, 1)
            dve.tensor_reduce(ss[:, 0:2], sq0[:, :, 0:O_CKV], AX.X, ALU.add)
            dve.tensor_reduce(ss[:, 2:4], sq0[:, :, O_CKV:O_KR], AX.X, ALU.add)
            dve.tensor_reduce(ss[:, 4:6], sq0[:, :, O_KR:O_BQ], AX.X, ALU.add)
            dve.tensor_reduce(ss[:, 6:38].rearrange("p (t g) -> p t g", t=TT),
                              sq0[:, :, O_BQ:O_BV].rearrange("p t (g d) -> p t g d", d=B_DH), AX.X, ALU.add).then_inc(u_sums, 1)
            dve.wait_ge(u_roots, 1)
            link(dve.reciprocal(rs[:, 0:38], rs[:, 0:38]))
            for t in range(TT):
                dve.tensor_scalar(u0[:, t, 0:O_CKV], u0[:, t, 0:O_CKV], rs[:, t:t + 1], None, ALU.mult)
                dve.tensor_scalar(u0[:, t, O_CKV:O_KR], u0[:, t, O_CKV:O_KR], rs[:, 2 + t:3 + t], None, ALU.mult).then_inc(c_normed, 1)
            for t in range(TT):
                dve.wait_ge(c_psum, t + 1)
                dve.tensor_tensor(cT[:, :, t * P:(t + 1) * P], blocks(t, 3), gains(G_C, 3, P), ALU.mult).then_inc(c_ready, 1)
            for t in range(TT):
                dve.scalar_tensor_tensor(out=kr[:, t, :], in0=u0[:, t, O_KR:O_BQ], scalar=rs[:, 4 + t:5 + t],
                                         in1=ga_rot[:, 1, :], op0=ALU.mult, op1=ALU.mult)
                heads = u0[:, t, O_BQ:O_BV].rearrange("p (g d) -> p g d", d=B_DH)
                ins = dve.tensor_tensor(heads, heads, rs[:, 6 + 16 * t:22 + 16 * t].unsqueeze(2).to_broadcast([P, 16, B_DH]), ALU.mult)
            link(ins)
            for t in range(TT):
                for m in range(2):
                    dve.wait_ge(up_psum, 4 * t + 3 + m)
                    dve.tensor_copy(kva[:, t, m * N:(m + 1) * N], ps[:, (6 if t == 0 else 2) + m, :]).then_inc(up_vec, 1)
            dve.wait_ge(a_squared, 1)
            dve.tensor_reduce(ss[:, 0:16], sqa[:, :, 0:A_NOPE], AX.X, ALU.add)
            dve.tensor_reduce(ss[:, 16:32].rearrange("p (t g) -> p t g", t=TT), sqk, AX.X, ALU.add)
            dve.tensor_reduce(ss[:, 32:48], sqa[:, :, A_NOPE:A_QK], AX.X, ALU.add).then_inc(a_sums, 1)
            dve.wait_ge(a_roots, 1)
            link(dve.reciprocal(rs[:, 0:48], rs[:, 0:48]))
            qh = qa.rearrange("p t (g d) -> p (t g) d", d=A_QK)
            kh = ka.rearrange("p t (g d) -> p t g d", d=A_QK)
            kvh = kva.rearrange("p t (g d) -> p t g d", d=A_NOPE + A_V)
            dve.tensor_tensor(qh[:, :, 0:A_NOPE], qh[:, :, 0:A_NOPE], rs[:, 0:16].unsqueeze(2).to_broadcast([P, 16, A_NOPE]), ALU.mult)
            for t in range(TT):
                dve.tensor_tensor(kh[:, t, :, 0:A_NOPE], kvh[:, t, :, 0:A_NOPE],
                                  rs[:, 16 + 8 * t:24 + 8 * t].unsqueeze(2).to_broadcast([P, 8, A_NOPE]), ALU.mult)
            link(dve.tensor_tensor(qh[:, :, A_NOPE:A_QK], qh[:, :, A_NOPE:A_QK],
                                   rs[:, 32:48].unsqueeze(2).to_broadcast([P, 16, A_ROPE]), ALU.mult))
            link(dve.tensor_tensor(qh[:, :, A_NOPE:A_QK], qh[:, :, A_NOPE:A_QK],
                                   ga_rot[:, 0:1, :].to_broadcast([P, 16, A_ROPE]), ALU.mult))
            dve.wait_ge(trig_ready, 1)
            q4 = qa.rearrange("p t (g d) -> p t g d", d=A_QK)

            def tables(first, n, groups):
                return [trig[:, m, :, first:first + n].unsqueeze(2).to_broadcast([P, TT, groups, n]) for m in (1, 0)]

            cos, sin = tables(0, NF_A, A_HEADS)
            rotate(q4[:, :, :, A_NOPE:A_NOPE + NF_A], q4[:, :, :, A_NOPE + NF_A:A_QK], cos, sin, rot_a)
            rotate(kr[:, :, 0:NF_A], kr[:, :, NF_A:A_ROPE], trig[:, 1, :, 0:NF_A], trig[:, 0, :, 0:NF_A], rot_k)
            dve.tensor_copy(kh[:, :, :, A_NOPE:A_QK], kr.unsqueeze(2).to_broadcast([P, TT, A_HEADS, A_ROPE])).then_inc(qk_normed, 1)
            for t in range(TT):
                for half in range(2):
                    turn_k(4 * t + 2 * half + 1, kta[0:A_QK, 4 * half:4 * half + 4, t * P:(t + 1) * P], A_QK, G_AK)
            for t in range(TT):
                turn_k(8 + 2 * t + 1, ktb[:, :, t * P:(t + 1) * P], P, G_BK)

            def head_outputs(layer, first, heads, width, banks, y, dst_col):
                for t in range(TT):
                    for n, bank in enumerate(banks[t]):
                        k = heads // len(banks[t])
                        c = first + n * k * (2 if layer else 1)
                        r = rinv[:, c:c + k, t] if not layer else rinv[:, c:c + 2 * k:2, t]
                        o = y[:, t, dst_col + n * N:dst_col + (n + 1) * N].rearrange("p (g d) -> p g d", d=width)
                        ins = dve.tensor_tensor(o, ps[:, bank, :].rearrange("p (g d) -> p g d", d=width),
                                                r.unsqueeze(2).to_broadcast([P, k, width]), ALU.mult)
                return ins

            for u in range(A_HEADS + B_HEADS):
                added = mask[:, :] if u < A_HEADS else bias[:, u - A_HEADS, :]
                scale = A_QK ** -0.5 if u < A_HEADS else B_DH ** -0.5
                scores(u, u, s0, scale, added, u - 8 if u >= 8 else None)
                if u == A_HEADS + 4:
                    dve.wait_ge(pv_done, A_HEADS)
                    link(dve.reciprocal(rinv[:, 0:A_HEADS, :], psum_l[:, 0:A_HEADS, :]))
                    head_outputs(0, 0, A_HEADS, A_V, [[4], [5]], xs, 0).then_inc(y_ready, 1)
            dve.wait_ge(pv_done, A_HEADS + B_HEADS)
            link(dve.reciprocal(rinv[:, A_HEADS:16, :], psum_l[:, A_HEADS:16, :]))
            head_outputs(0, A_HEADS, B_HEADS, B_DH, [[6], [7]], xs, N).then_inc(y_ready, 1)
            add_out(0, [4, 5, 6, 7], out_psum, 0)

            norm_apply(1, G_FF0)
            for s in range(TT * FCH):
                m = cols(s // TT, FF)[1]
                dve.wait_ge(ff_silu, s + 1)
                dve.wait_ge(ff_up_done, s + 1)
                if s >= 2:
                    dve.wait_ge(ff_turned, s - 1)
                dve.tensor_tensor(prod[:, s % 2, 0:m], sil[:, s % 2, 0:m], ps[:, 2 * (s % 2) + 1, 0:m], ALU.mult).then_inc(ff_prod, 1)
            add_out(1, [6, 7, 0, 1], ff_down_psum, 0)

            norm_apply(2, G_MIX1)
            dve.wait_ge(lam_exps, 1)
            link(dve.tensor_tensor(lams[:, 4:5], lams[:, 3:4], lams[:, 2:3], ALU.subtract))
            link(dve.tensor_scalar(lams[:, 5:6], lams[:, 4:5], -LAM_INIT, None, ALU.add))
            project(1, u1, 3 * C_MIX)
            dve.wait_ge(u_squared, 2)
            dve.tensor_reduce(ss[:, :], sqc.rearrange("p t (g d) -> p (t g) d", d=C_DH), AX.X, ALU.add).then_inc(u_sums, 1)
            dve.wait_ge(u_roots, 2)
            link(dve.reciprocal(rs[:, :], rs[:, :]))
            for t in range(TT):
                heads = u1[:, t, 0:2 * C_MIX].rearrange("p (g d) -> p g d", d=C_DH)
                ins = dve.tensor_tensor(heads, heads, rs[:, 32 * t:32 * t + 32].unsqueeze(2).to_broadcast([P, 32, C_DH]), ALU.mult)
            link(ins)
            for t in range(TT):
                rot = u1[:, t, 0:2 * C_MIX].rearrange("p (m g d) -> p m g d", m=2, d=C_DH)[:, :, :, 0:C_ROPE]
                ins = dve.tensor_tensor(rot, rot, gc_rot[:, :, :].unsqueeze(2).to_broadcast([P, 2, C_GROUPS, C_ROPE]), ALU.mult)
            link(ins)
            g4 = u1[:, :, 0:2 * C_MIX].rearrange("p t (g d) -> p t g d", d=C_DH)
            cos, sin = tables(NF_A, NF_C, 2 * C_GROUPS)
            rotate(g4[:, :, :, 0:NF_C], g4[:, :, :, NF_C:C_ROPE], cos, sin, rot_c)
            dve.engine_nop().then_inc(qk_normed, 1)
            for t in range(TT):
                for half in range(2):
                    turn_k(12 + 4 * t + 2 * half + 1, ktc[:, 4 * half:4 * half + 4, t * P:(t + 1) * P], P, G_CK)

            def difference(i):
                dve.wait_ge(exp_done, 16 + 2 * i + 2)
                link(dve.reciprocal(rinv[:, 2 * i:2 * i + 2, :], psum_l[:, 2 * i:2 * i + 2, :]))
                link(dve.scalar_tensor_tensor(out=coef[:, i, :], in0=psum_l[:, 2 * i, :], scalar=lams[:, 5:6],
                                              in1=rinv[:, 2 * i + 1, :], op0=ALU.mult, op1=ALU.mult))
                a, b = (2 * i) % 8, (2 * i + 1) % 8
                for t, (c0, c1) in enumerate(((0, P), (P, 384))):
                    ins = dve.scalar_tensor_tensor(out=s1[:, a, c0:c1], in0=s1[:, b, c0:c1], scalar=coef[:, i, t:t + 1],
                                                   in1=s1[:, a, c0:c1], op0=ALU.mult, op1=ALU.add)
                ins.then_inc(diff_done, 1)

            for i in range(C_HEADS + 1):
                if i < C_HEADS:
                    for m in range(2):
                        scores(2 * i + m, 16 + 2 * i + m, s1, C_DH ** -0.5, mask[:, :], 16 + i - 4 if i >= 4 else None)
                if i >= 1:
                    difference(i - 1)
            dve.wait_ge(pv_done, 16 + C_HEADS)
            head_outputs(1, 0, C_HEADS, 2 * C_DH, [[4, 5], [6, 7]], xs, 0).then_inc(o_normed, 1)
            dve.wait_ge(o_squared, 1)
            dve.tensor_reduce(ss[:, 0:16], sqo.rearrange("p t (g d) -> p (t g) d", d=2 * C_DH), AX.X, ALU.add).then_inc(o_squared, 1)
            dve.wait_ge(o_roots, 1)
            link(dve.reciprocal(rs[:, 0:16], rs[:, 0:16]))
            yh = xs[:, :, :].rearrange("p t (g d) -> p (t g) d", d=2 * C_DH)
            dve.tensor_tensor(yh, yh, rs[:, 0:16].unsqueeze(2).to_broadcast([P, 16, 2 * C_DH]), ALU.mult).then_inc(y_ready, 1)
            add_out(2, [4, 5, 6, 7], out_psum, 4)

            norm_apply(3, G_FF1)
            g, gs = gate_t, gate_s

            def per_token(a):
                return a.unsqueeze(2).to_broadcast([P, TT, E])

            link(dve.tensor_scalar(load8[:, 7, :], slots_f[:, 0:E], -1.0, float(E), ALU.mult, ALU.add))
            keys = load8[:, 7:8, :].to_broadcast([P, TT, E])
            dve.wait_ge(logits_psum, 1)
            link(dve.tensor_copy(g[:, 0, :, :], ps[:, 4, 0:TT * E].rearrange("p (t e) -> p t e", e=E)))

            def top(src, m, key, hot):
                link(dve.tensor_reduce(gs[:, m, :], g[:, src, :, :], AX.X, ALU.max))
                link(dve.tensor_tensor(g[:, key, :, :], g[:, src, :, :], per_token(gs[:, m, :]), ALU.is_equal))
                link(dve.tensor_tensor(g[:, key, :, :], g[:, key, :, :], keys, ALU.mult))
                link(dve.tensor_reduce(gs[:, m + 1, :], g[:, key, :, :], AX.X, ALU.max))
                link(dve.tensor_tensor(g[:, hot, :, :], g[:, key, :, :], per_token(gs[:, m + 1, :]), ALU.is_equal))

            top(0, 0, 1, 2)
            link(dve.scalar_tensor_tensor(out=g[:, 3, :, :], in0=g[:, 2, :, :], scalar=-3e38, in1=g[:, 0, :, :],
                                          op0=ALU.mult, op1=ALU.add))
            top(3, 2, 4, 5)
            dve.tensor_tensor(g[:, 6, :, :], g[:, 2, :, :], g[:, 5, :, :], ALU.add).then_inc(chosen_ready, 1)
            dve.tensor_tensor(gs[:, 4, :], gs[:, 2, :], gs[:, 0, :], ALU.subtract).then_inc(gate_diff, 1)
            dve.wait_ge(gate_exp, 1)
            link(dve.tensor_scalar(gs[:, 6, :], gs[:, 5, :], 1.0, None, ALU.add))
            link(dve.reciprocal(gs[:, 7, :], gs[:, 6, :]))
            link(dve.tensor_tensor(gs[:, 8, :], gs[:, 5, :], gs[:, 7, :], ALU.mult))
            dve.tensor_tensor(g[:, 7, :, :], g[:, 2, :, :], per_token(gs[:, 7, :]), ALU.mult)
            link(dve.tensor_tensor(g[:, 8, :, :], g[:, 5, :, :], per_token(gs[:, 8, :]), ALU.mult))
            dve.tensor_tensor(comb[:, :, 0:E], g[:, 7, :, :], g[:, 8, :, :], ALU.add)
            dve.wait_ge(chosen_ready, 1)
            link(dve.tensor_scalar(g[:, 9, :, :], g[:, 6, :, :], -FAR, FAR, ALU.mult, ALU.add))
            dve.wait_ge(rank_psum, 1)
            dve.tensor_tensor(rank[:, :, 0:E], g[:, 9, :, :], ps[:, 5, 0:TT * E].rearrange("p (t e) -> p t e", e=E), ALU.add)
            link(dve.tensor_scalar(load8[:, 0, :], ps[:, 5, TT * E:(TT + 1) * E], float(P), None, ALU.is_gt))
            link(dve.memset(load8[:, 1, :], 0.0))
            for e in range(1, E):
                link(dve.tensor_tensor(load8[:, 1, e:e + 1], load8[:, 1, e - 1:e], load8[:, 0, e - 1:e], ALU.add))
            dve.tensor_tensor(over_s[:, SPARE:SPARE + 1], load8[:, 1, E - 1:E], load8[:, 0, E - 1:E], ALU.add)
            for s in range(SPARE):
                link(dve.scalar_tensor_tensor(out=load8[:, 2, :], in0=load8[:, 1, :], scalar=float(s), in1=load8[:, 0, :],
                                              op0=ALU.is_equal, op1=ALU.mult))
                pick = load8[:, 2:3, :].to_broadcast([P, TT, E])
                dve.tensor_reduce(over_s[:, 4:5], load8[:, 2, :], AX.X, ALU.add)
                dve.tensor_tensor(load8[:, 3, :], load8[:, 2, :], slots_f[:, 0:E], ALU.mult)
                dve.tensor_tensor(g[:, 10, :, :], pick, rank[:, :, 0:E], ALU.mult)
                link(dve.tensor_tensor(g[:, 11, :, :], pick, comb[:, :, 0:E], ALU.mult))
                dve.tensor_reduce(over_s[:, s:s + 1], load8[:, 3, :], AX.X, ALU.add)
                dve.tensor_scalar(over_s[:, 5:6], over_s[:, 4:5], -FAR, FAR - P, ALU.mult, ALU.add)
                dve.tensor_reduce(gs[:, 9, :], g[:, 10, :, :], AX.X, ALU.add)
                link(dve.tensor_reduce(comb[:, :, E + s], g[:, 11, :, :], AX.X, ALU.add))
                link(dve.tensor_scalar(rank[:, :, E + s], gs[:, 9, :], over_s[:, 5:6], None, ALU.add))
            dve.tensor_copy(over_i[:, :], over_s[:, 0:4]).then_inc(routed, 1)

            def expert(i):
                for t in range(TT):
                    r, c = rank[:, t, bass.ds(i, 1)], comb[:, t, bass.ds(i, 1)]
                    dve.tensor_scalar(sel[:, t, :], slots_f[:, :], r, None, ALU.is_equal)
                    ins = dve.tensor_scalar(wsel[:, t, :], slots_f[:, :], r, c, ALU.is_equal, ALU.mult)
                ins.then_inc(sel_ready, 1)
                for half in range(2):
                    dve.wait_ge(gather_psum, 2 * i + half + 1)
                    dve.tensor_tensor(xg[:, 4 * half:4 * half + 4, :], blocks(6 + half), gains(G_FF1 + 4 * half, 4, P),
                                      ALU.mult).then_inc(xg_ready, 1)
                for j in range(ECH):
                    dve.wait_ge(silu_done, i * ECH + j + 1)
                    dve.wait_ge(up_done, i * ECH + j + 1)
                    if j >= 2:
                        dve.wait_ge(turn_done, i * ECH + j - 1)
                    dve.tensor_tensor(prod[:, j % 2, :], sil[:, j % 2, :], ps[:, 2 * (j % 2) + 1, :], ALU.mult).then_inc(prod_done, 1)
                dve.wait_ge(down_done, i * ECH + ECH)
                dve.tensor_copy(ysb[:, N:D], ps[:, 7, :]).then_inc(y_vec, 1)
                for n in range(4):
                    t, nn = divmod(n, 2)
                    dve.wait_ge(scatter_psum, 4 * i + n + 1)
                    dve.tensor_tensor(h[:, t, nn * N:(nn + 1) * N], h[:, t, nn * N:(nn + 1) * N], ps[:, n, :],
                                      ALU.add).then_inc(scatter_read, 1)
                dve.wait_ge(scatter_read, 4 * i + 5)

            dve.wait_ge(routed, 1)
            dve.engine_nop().then_inc(scatter_read, 1)
            with dve.Fori(0, E) as i:
                expert(i)
            n_over = dve.value_load(over_i[0:1, SPARE:SPARE + 1], min_val=0, max_val=SPARE)
            for s in range(SPARE):
                with dve.If(n_over > s):
                    expert(E + s)
            dve.engine_nop().then_inc(h_final, 1)

        @block.tensor
        def _(pe):
            def arrived(kind, j):
                n = AT[kind, j]
                extra = 1 if kind == "down" and 4 * j + 4 > FF // P else 0
                pe.wait_ge(landed[slot_of(n)], 16 * (uses(n) + extra_before(n) + extra))

            def extra_before(n):
                last = AT["down", -(-FK // 4) - 1]
                return 1 if n > last and slot_of(n) == slot_of(last) else 0

            def norm_turn(k):
                for t in range(TT):
                    pe.wait_ge(xs_ready, 2 * k + t + 1)
                    for c in range(DC):
                        ins = pe.transpose(ps[:, 2 * t + c // 4, (c % 4) * P:(c % 4 + 1) * P], xs[:, t, c * P:(c + 1) * P], ident[:, :])
                        if c % 4 == 3:
                            ins.then_inc(xT_psum, 1)

            def project(layer, kind, total, k):
                pe.wait_ge(xT_ready, 4 * k + 4)
                for j in range(-(-total // N)):
                    m = cols(j, total)[1]
                    arrived(kind, j)
                    wv = carve(ring[:, slot_of(AT[kind, j]), :], 0, DC, m)
                    for t in range(TT):
                        if j >= 2:
                            pe.wait_ge((proj_act if t == 0 else proj_vec)[layer], j - 1)
                        for c in range(DC):
                            ins = pe.matmul(ps[:, 4 + (2 * j + t) % 4, 0:m], xT[:, c, t * P:(t + 1) * P], wv[:, c, :],
                                            start=(c == 0), stop=(c == DC - 1))
                        ins.then_inc(proj_psum[layer], 1)

            def turn_heads(f, src, rows):
                if f % 12 >= 4:
                    pe.wait_ge(k_turned if f % 2 else q_turned, f // 2 - 1)
                for n in range(4):
                    ins = pe.transpose(ps[0:rows, f % 4, n * P:(n + 1) * P], src(n), ident[:, :])
                ins.then_inc(qk_psum, 1)

            def scores(unit, q, k):
                if unit % 16 >= 2:
                    pe.wait_ge(scores_read, unit - 1)
                b = unit % 2
                pe.matmul(ps[:, b, 0:P], q(0), k(P), start=True, stop=True)
                pe.matmul(ps[:, b, P:384], q(1), k(T), start=True, stop=True).then_inc(scores_psum, 1)

            def turn_p(head, ready, count, s, slot):
                pe.wait_ge(ready, count)
                if head >= 2:
                    pe.wait_ge(p_turned, head - 1)
                for n in range(3):
                    ins = pe.transpose(ps[:, 2 + head % 2, n * P:(n + 1) * P], s[:, slot, n * P:(n + 1) * P], ident[:, :])
                ins.then_inc(p_psum, 1)

            def weigh_values(head, pt, v, out0, out1):
                pe.wait_ge(p_turned, head + 1)
                p = pt[:, head % 2, :]
                pe.matmul(out0, p[:, 0:P], v(0), start=True, stop=True)
                pe.matmul(out1, p[:, P:2 * P], v(0), start=True, stop=False)
                pe.matmul(out1, p[:, 2 * P:384], v(1), start=False, stop=True).then_inc(pv_done, 1)

            def out_projection(layer):
                for f in range(4):
                    half, t = divmod(f, TT)
                    if t == 0:
                        pe.wait_ge(y_ready, 2 * layer + half + 1 if layer == 0 else 3)
                    for n in range(4):
                        c = 4 * half + n
                        ins = pe.transpose(ps[:, f, n * P:(n + 1) * P], xs[:, t, c * P:(c + 1) * P], ident[:, :])
                    ins.then_inc(yT_psum, 1)
                pe.wait_ge(yT_ready, 4 * layer + 4)
                kind = f"out{layer}"
                for k in range(DC):
                    if k % 4 == 0:
                        arrived(kind, k // 4)
                    wv = carve(ring[:, slot_of(AT[kind, k // 4]), :], 0, 4, D)
                    for n in range(4):
                        t, nn = divmod(n, 2)
                        ins = pe.matmul(ps[:, 4 + n, :], xT[:, k, t * P:(t + 1) * P], wv[:, k % 4, nn * N:(nn + 1) * N],
                                        start=(k == 0), stop=(k == DC - 1))
                        if k == DC - 1:
                            ins.then_inc(out_psum, 1)

            pe.wait_ge(consts_ready, n_consts)
            pe.wait_ge(gains_landed, 16 * n_gains)
            pe.transpose(ps[:, 7, 0:G_ROWS], gain_rows[:, :], ident[0:G_ROWS, 0:G_ROWS]).then_inc(gains_turned, 1)
            norm_turn(0)
            project(0, "in", EVEN_IN, 0)
            for t in range(TT):
                pe.wait_ge(c_normed, t + 1)
                for n in range(3):
                    ins = pe.transpose(ps[:, t, n * P:(n + 1) * P], u0[:, t, n * P:(n + 1) * P], ident[:, :])
                ins.then_inc(c_psum, 1)
            arrived("up_a", 0)
            s = slot_of(AT["up_a", 0])
            wq, wkv = carve(ring[:, s, :], 0, 2, A_HEADS * A_QK), ring[:, s, 2048:3072]
            pe.wait_ge(c_ready, TT)
            for t in range(TT):
                for m, (a, n) in enumerate(((0, 512), (512, 256))):
                    for c in range(2):
                        ins = pe.matmul(ps[:, (4 + m) if t == 0 else m, 0:n], cT[:, c, t * P:(t + 1) * P], wq[:, c, a:a + n],
                                        start=(c == 0), stop=(c == 1))
                    ins.then_inc(up_psum, 1)
                for m in range(2):
                    pe.matmul(ps[:, (6 if t == 0 else 2) + m, :], cT[:, 2, t * P:(t + 1) * P], wkv[:, m * N:(m + 1) * N],
                              start=True, stop=True).then_inc(up_psum, 1)
            pe.wait_ge(qk_normed, 1)
            for t in range(TT):
                for half in range(2):
                    for m, src in enumerate((qa, ka)):
                        turn_heads(4 * t + 2 * half + m,
                                   lambda n: src[:, t, (4 * half + n) * A_QK:(4 * half + n + 1) * A_QK], A_QK)
            for t in range(TT):
                for m, first in enumerate((O_BQ, O_BK)):
                    turn_heads(8 + 2 * t + m, lambda n: u0[:, t, first + n * P:first + (n + 1) * P], P)
            pe.wait_ge(q_turned, 6)
            pe.wait_ge(k_turned, 6)
            heads = A_HEADS + B_HEADS
            for i in range(heads + 3):
                if i < A_HEADS:
                    scores(i, lambda t: qta[0:A_QK, i, t * P:(t + 1) * P], lambda n: kta[0:A_QK, i, 0:n])
                elif i < heads:
                    pair, m = divmod(i - A_HEADS, 2)
                    r = slice(m * B_DH, (m + 1) * B_DH)
                    scores(i, lambda t: qtb[r, pair, t * P:(t + 1) * P], lambda n: ktb[r, pair, 0:n])
                if 2 <= i < heads + 2:
                    turn_p(i - 2, exp_done, i - 1, s0, (i - 2) % 8)
                if i >= 3:
                    n = i - 3
                    if n < A_HEADS:
                        weigh_values(n, pt0, lambda t: kva[:, t, n * P + A_NOPE:(n + 1) * P],
                                     ps[:, 4, n * A_V:(n + 1) * A_V], ps[:, 5, n * A_V:(n + 1) * A_V])
                    else:
                        m = n - A_HEADS
                        weigh_values(n, pt0, lambda t: u0[:, t, O_BV + m * B_DH:O_BV + (m + 1) * B_DH],
                                     ps[:, 6, m * B_DH:(m + 1) * B_DH], ps[:, 7, m * B_DH:(m + 1) * B_DH])
            out_projection(0)

            norm_turn(1)
            pe.wait_ge(xT_ready, 8)
            FS = TT * FCH
            for s in range(FS + 1):
                if s < FS:
                    j, t = divmod(s, TT)
                    m = cols(j, FF)[1]
                    if s >= 2:
                        pe.wait_ge(ff_silu, s - 1)
                        pe.wait_ge(ff_prod, s - 1)
                    for kind, bank, done in (("gate", 0, ff_gate_done), ("up", 1, ff_up_done)):
                        arrived(kind, j)
                        wv = carve(ring[:, slot_of(AT[kind, j]), :], 0, DC, m)
                        for c in range(DC):
                            ins = pe.matmul(ps[:, 2 * (s % 2) + bank, 0:m], xT[:, c, t * P:(t + 1) * P], wv[:, c, :],
                                            start=(c == 0), stop=(c == DC - 1))
                        ins.then_inc(done, 1)
                if s >= 1:
                    m = cols((s - 1) // TT, FF)[1]
                    pe.wait_ge(ff_prod, s)
                    if s >= 3:
                        pe.wait_ge(ff_hT, s - 2)
                    for n in range(-(-m // P)):
                        k = min(P, m - n * P)
                        ins = pe.transpose(ps[0:k, 4 + (s - 1) % 2, n * P:(n + 1) * P], prod[:, (s - 1) % 2, n * P:n * P + k], ident[:, :])
                    ins.then_inc(ff_turned, 1)
            pe.wait_ge(ff_hT, FS)
            banks = [6, 7, 0, 1]
            for k in range(FK):
                if k % 4 == 0:
                    arrived("down", k // 4)
                r = min(P, FF - k * P)
                wv = carve(ring[:, slot_of(AT["down", k // 4]), :], 0, 4, D)
                for n in range(4):
                    t, nn = divmod(n, 2)
                    ins = pe.matmul(ps[:, banks[n], :], hT0[0:r, k, t * P:(t + 1) * P], wv[0:r, k % 4, nn * N:(nn + 1) * N],
                                    start=(k == 0), stop=(k == FK - 1))
                    if k == FK - 1:
                        ins.then_inc(ff_down_psum, 1)
                if k % 4 == 3:
                    ins.then_inc(ff_down_used, 1)

            norm_turn(2)
            project(1, "qkv", 3 * C_MIX, 2)
            pe.wait_ge(qk_normed, 2)
            for t in range(TT):
                for half in range(2):
                    for m in range(2):
                        turn_heads(12 + 4 * t + 2 * half + m,
                                   lambda n: u1[:, t, m * C_MIX + (4 * half + n) * P:m * C_MIX + (4 * half + n + 1) * P], P)
            pe.wait_ge(q_turned, 10)
            pe.wait_ge(k_turned, 10)
            for i in range(C_HEADS + 2):
                if i < C_HEADS:
                    for m in range(2):
                        r = slice(m * C_DH, (m + 1) * C_DH)
                        scores(16 + 2 * i + m, lambda t: qtc[r, i, t * P:(t + 1) * P], lambda n: ktc[r, i, 0:n])
                if i >= 1 and i <= C_HEADS:
                    turn_p(16 + i - 1, diff_done, i, s1, (2 * (i - 1)) % 8)
                if i >= 2:
                    n = i - 2
                    c = (n % 4) * P
                    weigh_values(16 + n, pt1, lambda t: u1[:, t, 2 * C_MIX + n * P:2 * C_MIX + (n + 1) * P],
                                 ps[:, 4 + n // 4, c:c + P], ps[:, 6 + n // 4, c:c + P])
            out_projection(1)

            norm_turn(3)
            pe.wait_ge(xT_ready, 16)
            pe.wait_ge(rows_landed, 16 * n_rows)
            for t in range(TT):
                for c in range(DC):
                    ins = pe.matmul(ps[:, 4, t * E:(t + 1) * E], xT[:, c, t * P:(t + 1) * P], router[:, c, :],
                                    start=(c == 0), stop=(c == DC - 1))
            ins.then_inc(logits_psum, 1)
            pe.wait_ge(chosen_ready, 1)
            chosen = gate_t[:, 6, :, :]
            pe.matmul(ps[:, 5, 0:E], tri[:, :], chosen[:, 0, :], start=True, stop=True)
            pe.matmul(ps[:, 5, E:2 * E], ones[:, :], chosen[:, 0, :], start=True, stop=False)
            pe.matmul(ps[:, 5, E:2 * E], tri[:, :], chosen[:, 1, :], start=False, stop=True)
            pe.matmul(ps[:, 5, 2 * E:3 * E], ones[:, :], chosen[:, 0, :], start=True, stop=False)
            pe.matmul(ps[:, 5, 2 * E:3 * E], ones[:, :], chosen[:, 1, :], start=False, stop=True).then_inc(rank_psum, 1)
            pe.wait_ge(routed, 1)

            base = [SLOT_USES[s] for s in range(RING)]
            last = AT["down", -(-FK // 4) - 1]
            base[slot_of(last)] += 1

            def expert(i):
                def landed_at(q):
                    pe.wait_ge(landed[q % RING], i * (16 * len(EXPERT) // RING) + 16 * (base[q % RING] + q // RING + 1))

                pe.wait_ge(sel_ready, i + 1)
                for t in range(TT):
                    ins = pe.transpose(ps[:, 4, t * P:(t + 1) * P], wsel[:, t, :], ident[:, :])
                ins.then_inc(wselT_psum, 1)
                for c in range(DC):
                    for t in range(TT):
                        ins = pe.matmul(ps[:, 6 + c // 4, (c % 4) * P:(c % 4 + 1) * P], xs[:, t, c * P:(c + 1) * P], sel[:, t, :],
                                        start=(t == 0), stop=(t == TT - 1))
                    if c % 4 == 3:
                        ins.then_inc(gather_psum, 1)
                pe.wait_ge(xg_ready, 2 * i + 2)
                pe.wait_ge(wselT_ready, i + 1)
                pe.wait_ge(scatter_read, 4 * i + 1)

                def down(j):
                    q = EXPERT.index(("down", j))
                    landed_at(q)
                    pe.wait_ge(hT_ready, i * ECH + j + 1)
                    wv = carve(ring[:, q % RING, :], 0, 4, D)
                    for k in range(4):
                        for nn in range(2):
                            ins = pe.matmul(ps[:, 6 + nn, :], hT1[:, j % 2, k, :], wv[:, k, nn * N:(nn + 1) * N],
                                            start=(j == 0 and k == 0), stop=(j == ECH - 1 and k == 3))
                    ins.then_inc(down_done, 1)

                for j in range(ECH + 2):
                    if j < ECH:
                        if j >= 2:
                            pe.wait_ge(silu_done, i * ECH + j - 1)
                            pe.wait_ge(prod_done, i * ECH + j - 1)
                        for kind, bank, done in (("gate", 0, gate_done), ("up", 1, up_done)):
                            q = EXPERT.index((kind, j))
                            landed_at(q)
                            wv = carve(ring[:, q % RING, :], 0, DC, N)
                            for c in range(DC):
                                ins = pe.matmul(ps[:, 2 * (j % 2) + bank, :], xg[:, c, :], wv[:, c, :],
                                                start=(c == 0), stop=(c == DC - 1))
                            ins.then_inc(done, 1)
                    if 1 <= j <= ECH:
                        pe.wait_ge(prod_done, i * ECH + j)
                        if j >= 3:
                            pe.wait_ge(hT_ready, i * ECH + j - 2)
                        for n in range(4):
                            ins = pe.transpose(ps[:, 4 + (j - 1) % 2, n * P:(n + 1) * P], prod[:, (j - 1) % 2, n * P:(n + 1) * P], ident[:, :])
                        ins.then_inc(turn_done, 1)
                    if j >= 2:
                        down(j - 2)
                pe.wait_ge(y_act, i + 1)
                pe.wait_ge(y_vec, i + 1)
                for n in range(4):
                    t, nn = divmod(n, 2)
                    pe.matmul(ps[:, n, :], wselT[:, t, :], ysb[:, nn * N:(nn + 1) * N], start=True, stop=True).then_inc(scatter_psum, 1)

            with pe.Fori(0, E) as i:
                expert(i)
            n_over = pe.value_load(over_i[0:1, SPARE:SPARE + 1], min_val=0, max_val=SPARE)
            for s in range(SPARE):
                with pe.If(n_over > s):
                    expert(E + s)

        @block.gpsimd
        def _(pool):
            pool.wait_ge(rel_extended, 1)
            pool.dma_start(rel_scratch, rel[:, :]).then_inc(rel_stored, 16)
            pool.wait_ge(rel_stored, 16)
            for head in range(B_HEADS):
                shifted = bass.AP(rel_scratch.tensor, head * 384 + 1, [[1, P], [1, T]])
                pool.dma_start(bias_rev[:, head, :], shifted).then_inc(bias_landed, 16)


_INS = ['x', 'positions', 'ev_norm_mix', 'ev_w_in', 'ev_g_cq', 'ev_g_ckv', 'ev_w_uq', 'ev_w_ukv',
        'ev_a_qnorm', 'ev_a_knorm', 'ev_b_qnorm', 'ev_b_knorm', 'ev_b_rel_bias', 'ev_w_out',
        'ev_norm_ff', 'ev_ff_gate', 'ev_ff_up', 'ev_ff_down',
        'od_norm_mix', 'od_w_qkv', 'od_c_qnorm', 'od_c_knorm', 'od_lam_q1', 'od_lam_k1',
        'od_lam_q2', 'od_lam_k2', 'od_c_subnorm', 'od_w_out', 'od_norm_ff', 'od_router',
        'od_ex_gate', 'od_ex_up', 'od_ex_down']


def kernel(**inputs):
    import numpy as _np
    import concourse.bacc as _bacc
    from concourse import mybir as _mybir
    from concourse.bass_utils import run_bass_kernel_spmd as _run

    nc = _bacc.Bacc("TRN2", target_bir_lowering=False, num_devices=1)
    arrays, aps = {}, {}
    for name in _INS:
        a = _np.ascontiguousarray(inputs[name])
        arrays[f"in_{name}_dram"] = a
        aps[name] = nc.dram_tensor(f"in_{name}_dram", a.shape, _mybir.dt.from_np(a.dtype), kind="ExternalInput").ap()
    out = nc.dram_tensor("out_0_dram", (1, T, D), _mybir.dt.float32, kind="ExternalOutput").ap()
    trunk(nc, aps, out)
    r = _run(nc, [arrays], core_ids=[0])
    return r.results[0]["out_0_dram"]
```

```python
import math
from contextlib import ExitStack

import numpy as np

import concourse.bass as bass
from concourse import mybir

F32 = mybir.dt.float32
F32R = mybir.dt.float32r
I32 = mybir.dt.int32
ALU = mybir.AluOpType
ACT = mybir.ActivationFunctionType
AX = mybir.AxisListType

P = 128
D = 1024
T = 256
TT = T // P
DC = D // P
CHUNK = 64
EPS = 1e-6
NEG = -1e30

A_HEADS, A_NOPE, A_ROPE, A_V, A_QL, A_KVL = 8, 64, 32, 64, 256, 128
A_QK = A_NOPE + A_ROPE
B_HEADS, B_DH, B_CLIP = 8, 64, 128
EVEN_IN = A_QL + A_KVL + A_ROPE + 3 * B_HEADS * B_DH
O_CKV = A_QL
O_KR = O_CKV + A_KVL
O_BQ = O_KR + A_ROPE
O_BK = O_BQ + B_HEADS * B_DH
O_BV = O_BK + B_HEADS * B_DH
C_HEADS, C_DH, C_ROPE = 8, 64, 16
C_MIX = C_HEADS * 2 * C_DH
C_GROUPS = 2 * C_HEADS
FF = 2752
E = 8
FE = 3584
N = 512

RAW = 7
SPLIT = 3
UNIT = 2048
FCH = -(-FF // N)
FK = -(-FF // P)
ECH = FE // N
SPARE = 3
ITEMS = E + SPARE
FAR = 1024.0

G_MIX0, G_FF0, G_MIX1, G_FF1 = 0, 8, 16, 24
G_C = 32
G_AQ, G_AK, G_BQ, G_BK, G_CQ, G_CK, G_SUB = 35, 36, 37, 38, 39, 40, 41
G_ROWS = 42

FREQ = np.concatenate([
    np.float32(1.0) / (np.float32(theta) ** (np.arange(0, dim, 2, dtype=np.float32) / np.float32(dim)))
    for dim, theta in ((A_ROPE, 10000.0), (C_ROPE, 500000.0))]).astype(np.float32)
NF_A = A_ROPE // 2
NF_C = C_ROPE // 2
NF = NF_A + NF_C
TURN_1 = 6.28125
TURN_2 = float(np.float32(round((2 * math.pi - TURN_1) * 2 ** 21) / 2 ** 21))
TURN_3 = 2 * math.pi - TURN_1 - TURN_2
ROUND = 1.5 * 2 ** 23
PI_BELOW = 3.1415925
LAM_INIT = 0.8 - 0.6 * math.exp(-0.3 * 1)


def weight_stream():
    s = [("in", j, u) for j in range(-(-EVEN_IN // N)) for u in range(2)]
    s += [("uq", 0, 0), ("ukv", 0, 0)]
    s += [("out0", 0, u) for u in range(DC // 2)]
    for j in range(FCH + 1):
        if j < FCH:
            s += [("gate", j, 0), ("gate", j, 1), ("up", j, 0), ("up", j, 1)]
        if j >= 1:
            s += [("down", j - 1, u) for u in range(-(-min(4, FK - 4 * (j - 1)) // 2))]
    s += [("qkv", j, u) for j in range(3 * C_MIX // N) for u in range(2)]
    s += [("out1", 0, u) for u in range(DC // 2)]
    return s


def expert_stream():
    s = []
    for j in range(ECH + 1):
        if j < ECH:
            s += [("gate", j, 0), ("gate", j, 1), ("up", j, 0), ("up", j, 1)]
        if j >= 1:
            s += [("down", j - 1, 0), ("down", j - 1, 1)]
    return s


STREAM = weight_stream()
DENSE = len(STREAM)
EXPERT = expert_stream()
AT = {item: n for n, item in enumerate(STREAM)}
NARROW = 4
WIDE_FROM = AT["gate", 0, 0]
assert len(EXPERT) % RAW == 0 and len(EXPERT) % SPLIT == 0


def raw_of(n):
    return n % NARROW if n < WIDE_FROM else (n - WIDE_FROM) % RAW


def before(n):
    found = [m for m in range(max(0, n - RAW - NARROW), n) if raw_of(m) == raw_of(n)]
    return found[-1] if found else None


def pieces(n):
    kind, j, u = STREAM[n]
    if kind in ("in", "gate", "up", "qkv"):
        total = {"in": EVEN_IN, "gate": FF, "up": FF, "qkv": 3 * C_MIX}[kind]
        return [(P, 0, 4 * min(N, total - j * N))]
    if kind == "uq":
        return [(P, 0, 2 * A_HEADS * A_QK)]
    if kind == "ukv":
        return [(P, 0, A_HEADS * (A_NOPE + A_V))]
    k = 4 * j + 2 * u
    if kind == "down" and (k + 2) * P > FF:
        return [(P, 0, D), (FF - (k + 1) * P, D, D)]
    return [(P, 0, 2 * D)]


def landings(n):
    return sum(len(pieces(m)) for m in range(n + 1) if raw_of(m) == raw_of(n))


DENSE_LANDINGS = [sum(len(pieces(m)) for m in range(DENSE) if raw_of(m) == r) for r in range(RAW)]


def trunk(nc, w, out):
    with ExitStack() as ctx:
        ctx.enter_context(nc.allow_non_contiguous_dma(reason="short gain, position and router loads"))

        def sb(name, shape, dt=F32):
            return ctx.enter_context(nc.sbuf_tensor(name, shape, dt))

        def sem(name):
            return ctx.enter_context(nc.semaphore(name))

        raw = sb("raw", [P, RAW, UNIT])
        w_hi = sb("w_hi", [P, SPLIT, UNIT], F32R)
        w_lo = sb("w_lo", [P, SPLIT, UNIT], F32R)
        h = sb("h", [P, TT, D])
        xT_hi = sb("xT_hi", [P, DC, T], F32R)
        xT_lo = sb("xT_lo", [P, DC, T], F32R)
        hT_hi = sb("hT_hi", [P, 4, T], F32R)
        hT_lo = sb("hT_lo", [P, 4, T], F32R)
        xs = sb("xs", [P, TT, D])
        ident = sb("ident", [P, P])
        tri = sb("tri", [P, P])
        ones = sb("ones", [P, P])
        slots_f = sb("slots_f", [P, P])
        mask = sb("mask", [P, 384])
        eps = sb("eps", [P, 1])
        freq = sb("freq", [P, NF])
        gain_rows = sb("gain_rows", [G_ROWS, P])
        gcol = sb("gcol", [P, G_ROWS])
        ga_rot = sb("ga_rot", [P, 2, A_ROPE])
        gc_rot = sb("gc_rot", [P, 2, C_ROPE])
        lamv = sb("lamv", [P, 4, C_DH])
        lams = sb("lams", [P, 8])
        pos_i = sb("pos_i", [P, TT], I32)
        pos_f = sb("pos_f", [P, TT])
        router = sb("router", [P, DC, E])
        router_hi = sb("router_hi", [P, DC, E], F32R)
        router_lo = sb("router_lo", [P, DC, E], F32R)
        trig = sb("trig", [P, 2, TT, NF])
        turns = sb("turns", [P, 2, TT, NF])
        angle = sb("angle", [P, TT, NF])
        ssq = sb("ssq", [P, 8])
        root = sb("root", [P, 8])
        rstd = sb("rstd", [P, 8])
        ss = sb("ss", [P, 64])
        rs = sb("rs", [P, 64])
        negmax = sb("negmax", [P, 2 * C_HEADS, TT])
        psum_l = sb("psum_l", [P, 2 * C_HEADS, TT])
        rinv = sb("rinv", [P, 2 * C_HEADS, TT])
        coef = sb("coef", [P, C_HEADS, TT])
        gate_t = sb("gate_t", [P, 12, TT, E])
        gate_s = sb("gate_s", [P, 12, TT])
        rank = sb("rank", [P, TT, ITEMS])
        comb = sb("comb", [P, TT, ITEMS])
        load8 = sb("load8", [P, 8, E])
        over_s = sb("over_s", [P, 8])
        over_i = sb("over_i", [P, 4], I32)
        WORK = 13760
        work = sb("work", [P, WORK])

        def carve(base, at, *dims):
            n = math.prod(dims)
            assert at + n <= base.shape[1]
            v = base[:, at:at + n]
            names = "abc"[:len(dims)]
            if len(dims) == 1:
                return v
            return v.rearrange(f"p ({' '.join(names)}) -> p {' '.join(names)}",
                               **{k: d for k, d in zip(names[1:], dims[1:])})

        tail = raw[:, NARROW:RAW, :].rearrange("p a b -> p (a b)")
        u0 = carve(work, 0, TT, EVEN_IN)
        qa = carve(work, 3904, TT, A_HEADS * A_QK)
        kva = carve(work, 5440, TT, A_HEADS * (A_NOPE + A_V))
        ka = carve(work, 7488, TT, A_HEADS * A_QK)
        bias = carve(work, 9024, B_HEADS, T)
        S0 = 7
        s0 = carve(work, 11072, S0, 384)
        qta, kta = carve(tail, 0, A_HEADS, T), carve(tail, 2048, A_HEADS, T)
        qtb, ktb = carve(tail, 4096, B_HEADS // 2, T), carve(tail, 5120, B_HEADS // 2, T)
        pt0 = carve(work, 7488, 2, 384)
        bias_rev = carve(tail, 0, B_HEADS, T)
        rel = carve(work, 5440, 384)[0:B_HEADS, :]
        sq0 = carve(work, 3904, TT, O_BK + B_HEADS * B_DH)
        sqa = carve(work, 11072, TT * A_HEADS, A_QK)
        sqk = carve(work, 11072 + 1536, TT, A_HEADS, A_NOPE)
        xs_flat = xs[:, :, :].rearrange("p a b -> p (a b)")
        rot_a = [carve(xs_flat, 256 * n, TT, A_HEADS, NF_A) for n in range(4)]
        rot_k = [carve(xs_flat, 1024 + 64 * n, TT, NF_A) for n in range(4)]
        rot_c = [carve(xs_flat, 512 * n, TT, 2 * C_GROUPS, NF_C) for n in range(4)]
        kr = carve(xs_flat, 1280, TT, A_ROPE)
        slots_i = work[:, 11072:11072 + P].bitcast(I32)
        u1 = carve(work, 0, TT, 3 * C_MIX)
        qtc, ktc = carve(work, 6144, C_HEADS, T), carve(work, 8192, C_HEADS, T)
        sqc = carve(work, 6144, TT, 2 * C_MIX)
        S1 = 8
        s1 = carve(work, 10240, S1, 384)
        sqo = carve(work, 10240, TT, C_MIX)
        pt1 = carve(xs_flat, 0, 2, 384)
        sil = carve(work, 8192, 2, N)
        prod = carve(work, 9216, 2, N)
        scaled = carve(work, 12288, 2, N)
        sel = carve(work, 1024, TT, P)
        wsel = carve(work, 1280, TT, P)
        wselT = carve(work, 1536, TT, P)
        ysb = carve(work, 2816, D)

        ps = ctx.enter_context(nc.psum_tensor("ps", [P, 8, N], F32))

        rel_scratch = nc.dram_tensor("rel_scratch", (B_HEADS, 384), F32, kind="Internal").ap()
        w_in = w["ev_w_in"][0].rearrange("(k p) n -> p k n", p=P)
        w_uq = w["ev_w_uq"][0].rearrange("(k p) h d -> p k (h d)", p=P)
        w_ukv = w["ev_w_ukv"][0].rearrange("p h d -> p (h d)")
        w_out0 = w["ev_w_out"][0].rearrange("(k p) n -> p k n", p=P)
        w_out1 = w["od_w_out"][0].rearrange("(k p) n -> p k n", p=P)
        ff_gate = w["ev_ff_gate"][0].rearrange("(k p) n -> p k n", p=P)
        ff_up = w["ev_ff_up"][0].rearrange("(k p) n -> p k n", p=P)
        ff_down = w["ev_ff_down"][0]
        w_qkv = w["od_w_qkv"][0].rearrange("(k p) n -> p k n", p=P)
        ex_gate = w["od_ex_gate"][0].rearrange("e (k p) n -> e p k n", p=P)
        ex_up = w["od_ex_up"][0].rearrange("e (k p) n -> e p k n", p=P)
        ex_down = w["od_ex_down"][0].rearrange("e (k p) n -> e p k n", p=P)

        landed = [sem(f"landed{r}") for r in range(RAW)]
        hi_ready = sem("hi_ready")
        lo_ready = sem("lo_ready")
        unit_used = sem("unit_used")
        scaled_ready = sem("scaled_ready")
        parts_hi = sem("parts_hi")
        x_landed = sem("x_landed")
        gains_landed = sem("gains_landed")
        rows_landed = sem("rows_landed")
        rel_landed = sem("rel_landed")
        rel_extended = sem("rel_extended")
        rel_stored = sem("rel_stored")
        bias_landed = sem("bias_landed")
        pool_chain = sem("pool_chain")
        gain_ones = sem("gain_ones")
        consts_ready = sem("consts_ready")
        gains_turned = sem("gains_turned")
        gains_ready = sem("gains_ready")
        vec_chain = sem("vec_chain")
        act_chain = sem("act_chain")
        angles_ready = sem("angles_ready")
        trig_ready = sem("trig_ready")
        root_ready = sem("root_ready")
        xs_ready = sem("xs_ready")
        xT_psum = sem("xT_psum")
        xT_ready = sem("xT_ready")
        proj_act = [sem("proj_act0"), sem("proj_act1")]
        proj_vec = [sem("proj_vec0"), sem("proj_vec1")]
        u_squared = sem("u_squared")
        u_sums = sem("u_sums")
        u_roots = sem("u_roots")
        c_normed = sem("c_normed")
        c_psum = sem("c_psum")
        c_ready = sem("c_ready")
        up_act = sem("up_act")
        up_vec = sem("up_vec")
        a_squared = sem("a_squared")
        a_sums = sem("a_sums")
        a_roots = sem("a_roots")
        qk_normed = sem("qk_normed")
        qk_psum = sem("qk_psum")
        q_turned = sem("q_turned")
        k_turned = sem("k_turned")
        scores_psum = sem("scores_psum")
        scores_read = sem("scores_read")
        max_ready = sem("max_ready")
        exp_done = sem("exp_done")
        diff_done = sem("diff_done")
        p_psum = sem("p_psum")
        p_turned = sem("p_turned")
        pv_done = sem("pv_done")
        y_ready = sem("y_ready")
        yT_psum = sem("yT_psum")
        yT_hi = sem("yT_hi")
        yT_ready = sem("yT_ready")
        router_split = sem("router_split")
        h_ready = sem("h_ready")
        lam_sums = sem("lam_sums")
        lam_exps = sem("lam_exps")
        o_normed = sem("o_normed")
        o_squared = sem("o_squared")
        o_roots = sem("o_roots")
        ff_silu = sem("ff_silu")
        ff_prod = sem("ff_prod")
        ff_turned = sem("ff_turned")
        ff_hT_hi = sem("ff_hT_hi")
        ff_hT = sem("ff_hT")
        logits_psum = sem("logits_psum")
        gate_diff = sem("gate_diff")
        gate_exp = sem("gate_exp")
        chosen_ready = sem("chosen_ready")
        rank_psum = sem("rank_psum")
        routed = sem("routed")
        sel_ready = sem("sel_ready")
        wselT_psum = sem("wselT_psum")
        wselT_ready = sem("wselT_ready")
        gather_psum = sem("gather_psum")
        xg_ready = sem("xg_ready")
        silu_done = sem("silu_done")
        prod_done = sem("prod_done")
        turn_done = sem("turn_done")
        hT_part = sem("hT_part")
        hT_ready = sem("hT_ready")
        y_act = sem("y_act")
        y_vec = sem("y_vec")
        scatter_psum = sem("scatter_psum")
        scatter_read = sem("scatter_read")
        h_final = sem("h_final")
        stored = sem("stored")

        n_gains = 17
        n_rows = 10
        IN_J = -(-EVEN_IN // N)
        QKV_J = 3 * C_MIX // N

        def cols(j, total):
            return j * N, min(N, total - j * N)

        def blocks(bank, n=4):
            return ps[:, bank, 0:n * P].rearrange("p (a b) -> p a b", b=P)

        def gains(first, n, width):
            return gcol[:, first:first + n].unsqueeze(2).to_broadcast([P, n, width])

        def cT(x, t):
            return x[:, 0:3, t * P:(t + 1) * P]

        block = ctx.enter_context(nc.Block())

        @block.sync
        def _(sp):
            sp.dma_start(h[:, :, :], w["x"][0].rearrange("(t p) d -> p t d", p=P)).then_inc(x_landed, 16)

            def rows(n):
                kind, j, u = STREAM[n]
                if kind in ("in", "gate", "up", "qkv"):
                    src, total = {"in": (w_in, EVEN_IN), "gate": (ff_gate, FF), "up": (ff_up, FF),
                                  "qkv": (w_qkv, 3 * C_MIX)}[kind]
                    a, m = cols(j, total)
                    return [src[:, 4 * u:4 * u + 4, a:a + m]]
                if kind == "uq":
                    return [w_uq]
                if kind == "ukv":
                    return [w_ukv.unsqueeze(1)]
                if kind in ("out0", "out1"):
                    return [(w_out0 if kind == "out0" else w_out1)[:, 2 * u:2 * u + 2, :]]
                k = 4 * j + 2 * u
                if len(pieces(n)) == 2:
                    return [ff_down[k * P:(k + 1) * P, :].unsqueeze(1), ff_down[(k + 1) * P:FF, :].unsqueeze(1)]
                return [ff_down[k * P:(k + 2) * P, :].rearrange("(k p) n -> p k n", p=P)]

            for n in range(DENSE):
                if before(n) is not None:
                    sp.wait_ge(lo_ready, before(n) + 1)
                elif raw_of(n) >= NARROW:
                    sp.wait_ge(pv_done, A_HEADS + B_HEADS)
                for (r, a, m), src in zip(pieces(n), rows(n)):
                    k = src.shape[1]
                    dst = raw[0:r, raw_of(n), a:a + m].rearrange("p (k n) -> p k n", k=k)
                    sp.dma_start(dst, src).then_inc(landed[raw_of(n)], 16)

            def load_expert(i, e):
                for q, (kind, j, u) in enumerate(EXPERT):
                    sp.wait_ge(lo_ready, i * len(EXPERT) + DENSE + q - RAW + 1)
                    one = bass.ds(e, 1)
                    if kind == "down":
                        src = ex_down[one, :, 4 * j + 2 * u:4 * j + 2 * u + 2, :]
                    else:
                        src = (ex_gate if kind == "gate" else ex_up)[one, :, 4 * u:4 * u + 4, j * N:(j + 1) * N]
                    r = raw_of(DENSE + q)
                    dst = raw[:, r, :].rearrange("p (k n) -> p k n", k=2 if kind == "down" else 4)
                    sp.dma_start(dst, src.rearrange("e p k n -> p (e k) n")).then_inc(landed[r], 16)

            with sp.Fori(0, E) as i:
                load_expert(i, i)
            sp.wait_ge(routed, 1)
            n_over = sp.value_load(over_i[0:1, SPARE:SPARE + 1], min_val=0, max_val=SPARE)
            for s in range(SPARE):
                with sp.If(n_over > s):
                    e = sp.value_load(over_i[0:1, s:s + 1], min_val=0, max_val=E - 1)
                    load_expert(E + s, e)
            sp.wait_ge(h_final, 1)
            sp.dma_start(out[0].rearrange("(t p) d -> p t d", p=P), h[:, :, :]).then_inc(stored, 16)
            sp.wait_ge(stored, 16)

        @block.gpsimd
        def _(pool):
            pool.memset(gain_rows[:, :], 1.0).then_inc(gain_ones, 1)
            pool.memset(ident[:, :], 0.0).then_inc(pool_chain, 1)
            pool.memset(tri[:, :], 1.0).then_inc(pool_chain, 1)
            pool.memset(mask[:, :], 0.0).then_inc(pool_chain, 1)
            pool.wait_ge(pool_chain, 3)
            pool.affine_select(out=ident[:, :], in_=ident[:, :], compare_op=ALU.not_equal, fill=1.0,
                               base=0, pattern=[[-1, P]], channel_multiplier=1).then_inc(consts_ready, 1)
            pool.affine_select(out=tri[:, :], in_=tri[:, :], compare_op=ALU.is_gt, fill=0.0,
                               base=0, pattern=[[1, P]], channel_multiplier=-1).then_inc(consts_ready, 1)
            pool.memset(mask[0:CHUNK, CHUNK:P], NEG).then_inc(consts_ready, 1)
            pool.memset(mask[0:CHUNK, 384 - CHUNK:384], NEG).then_inc(consts_ready, 1)
            pool.memset(ones[:, :], 1.0).then_inc(consts_ready, 1)
            pool.memset(eps[:, :], EPS).then_inc(consts_ready, 1)
            for f in range(NF):
                pool.memset(freq[:, f:f + 1], float(FREQ[f])).then_inc(consts_ready, 1)
            pool.iota(slots_i[:, :], pattern=[[1, P]], base=0, channel_multiplier=0).then_inc(consts_ready, 1)

        n_consts = 6 + NF + 1

        @block.scalar
        def _(act):
            chain = [0]

            def link(ins):
                chain[0] += 1
                ins.then_inc(act_chain, 1)
                act.wait_ge(act_chain, chain[0])

            act.wait_ge(gain_ones, 1)
            for first, name in ((G_MIX0, "ev_norm_mix"), (G_FF0, "ev_norm_ff"), (G_MIX1, "od_norm_mix"), (G_FF1, "od_norm_ff")):
                act.dma_start(gain_rows[first:first + DC, :], w[name][0].rearrange("(k p) -> k p", p=P)).then_inc(gains_landed, 16)
            act.dma_start(gain_rows[G_C:G_C + 2, :], w["ev_g_cq"][0].rearrange("(k p) -> k p", p=P)).then_inc(gains_landed, 16)
            act.dma_start(gain_rows[G_C + 2:G_C + 3, :], w["ev_g_ckv"]).then_inc(gains_landed, 16)
            act.dma_start(gain_rows[G_SUB:G_SUB + 1, :], w["od_c_subnorm"]).then_inc(gains_landed, 16)
            for row, name in ((G_AQ, "ev_a_qnorm"), (G_AK, "ev_a_knorm")):
                act.dma_start(gain_rows[row:row + 1, 0:A_NOPE], w[name][:, 0:A_NOPE]).then_inc(gains_landed, 16)
            for row, name in ((G_BQ, "ev_b_qnorm"), (G_BK, "ev_b_knorm")):
                for m in range(2):
                    act.dma_start(gain_rows[row:row + 1, m * B_DH:(m + 1) * B_DH], w[name]).then_inc(gains_landed, 16)
            for row, name in ((G_CQ, "od_c_qnorm"), (G_CK, "od_c_knorm")):
                for m in range(2):
                    act.dma_start(gain_rows[row:row + 1, m * C_DH + C_ROPE:(m + 1) * C_DH], w[name][:, C_ROPE:C_DH]).then_inc(gains_landed, 16)
            act.dma_start(pos_i[:, :], w["positions"][0].rearrange("(t p) -> p t", p=P)).then_inc(rows_landed, 16)
            act.dma_start(rel[:, 0:2 * B_CLIP + 1], w["ev_b_rel_bias"][0]).then_inc(rel_landed, 16)
            for m, name in enumerate(("ev_a_qnorm", "ev_a_knorm")):
                act.dma_start(ga_rot[:, m, :], w[name][0, A_NOPE:A_QK].partition_broadcast(P)).then_inc(rows_landed, 16)
            for m, name in enumerate(("od_c_qnorm", "od_c_knorm")):
                act.dma_start(gc_rot[:, m, :], w[name][0, 0:C_ROPE].partition_broadcast(P)).then_inc(rows_landed, 16)
            for m, name in enumerate(("od_lam_q1", "od_lam_k1", "od_lam_q2", "od_lam_k2")):
                act.dma_start(lamv[:, m, :], w[name][0].partition_broadcast(P)).then_inc(rows_landed, 16)
            act.dma_start(router[:, :, :], w["od_router"][0].rearrange("(k p) e -> p k e", p=P)).then_inc(rows_landed, 16)

            done = [0]

            def split_to(end):
                for n in range(done[0], min(end, DENSE)):
                    act.wait_ge(landed[raw_of(n)], 16 * landings(n))
                    if n >= SPLIT:
                        act.wait_ge(unit_used, n - SPLIT + 1)
                    for r, a, m in pieces(n):
                        ins = act.activation(w_hi[0:r, n % SPLIT, a:a + m], raw[0:r, raw_of(n), a:a + m], ACT.Copy)
                    ins.then_inc(hi_ready, 1)
                done[0] = max(done[0], end)

            def parts(c, dst, n=N):
                act.wait_ge(scaled_ready, c + 1)
                act.activation(dst, scaled[:, c % 2, 0:n].rearrange("p (a b) -> p a b", b=P), ACT.Copy).then_inc(parts_hi, 1)

            def norm_parts(k, c):
                for f in range(4):
                    t, half = divmod(f, 2)
                    parts(c + f, xT_hi[:, 4 * half:4 * half + 4, t * P:(t + 1) * P])

            def norm_roots(k):
                for t in range(TT):
                    if k == 0:
                        act.wait_ge(x_landed, 16)
                        act.wait_ge(consts_ready, n_consts)
                    else:
                        act.wait_ge(h_ready, 4 * k)
                    if k:
                        act.wait_ge(xT_psum, 4 * k)
                    link(act.activation(xs[:, t, :], h[:, t, :], ACT.Square, accum_out=ssq[:, 2 * k + t:2 * k + t + 1]))
                    act.activation(root[:, 2 * k + t:2 * k + t + 1], ssq[:, 2 * k + t:2 * k + t + 1], ACT.Sqrt,
                                   scale=1.0 / D, bias=eps[:, 0:1]).then_inc(root_ready, 1)

            def project(kind, layer, u, total):
                for j in range(-(-total // N)):
                    a, m = cols(j, total)
                    n = AT[kind, j, 1]
                    split_to(n + SPLIT + 1)
                    act.wait_ge(unit_used, n + 1)
                    act.activation(u[:, 0, a:a + m], ps[:, 4 + 2 * (j % 2), 0:m], ACT.Copy).then_inc(proj_act[layer], 1)

            def turn_q(f, dst, rows, col):
                act.wait_ge(qk_psum, f + 1)
                act.activation(dst, blocks(f % 4)[0:rows], ACT.Copy, scale=gcol[0:rows, col:col + 1]).then_inc(q_turned, 1)

            def exponentials(u, unit, s, slot):
                act.wait_ge(max_ready, unit + 1)
                act.activation(s[:, slot, 0:P], s[:, slot, 0:P], ACT.Exp,
                               bias=negmax[:, u, 0:1], accum_out=psum_l[:, u, 0:1])
                act.activation(s[:, slot, P:384], s[:, slot, P:384], ACT.Exp,
                               bias=negmax[:, u, 1:2], accum_out=psum_l[:, u, 1:2]).then_inc(exp_done, 1)

            def turn_p(head, pt):
                act.wait_ge(p_psum, head + 1)
                if head >= 2:
                    act.wait_ge(pv_done, head - 1)
                act.activation(pt[:, head % 2, :], ps[:, 2 + head % 2, 0:384], ACT.Copy).then_inc(p_turned, 1)

            def turn_y(layer):
                for f in range(4):
                    half, t = divmod(f, TT)
                    act.wait_ge(yT_psum, 4 * layer + f + 1)
                    scale = 1.0 if layer == 0 else gcol[:, G_SUB:G_SUB + 1]
                    act.activation(xT_hi[:, 4 * half:4 * half + 4, t * P:(t + 1) * P], blocks(f), ACT.Copy,
                                   scale=scale).then_inc(yT_hi, 1)

            norm_roots(0)
            split_to(1)
            norm_parts(0, 0)
            split_to(SPLIT)
            act.activation(router_hi[:, :, :], router[:, :, :], ACT.Copy).then_inc(router_split, 1)
            project("in", 0, u0, EVEN_IN)
            act.wait_ge(proj_vec[0], IN_J)
            act.wait_ge(proj_act[0], IN_J)
            act.activation(sq0, u0[:, :, 0:O_BV], ACT.Square).then_inc(u_squared, 1)
            act.wait_ge(u_sums, 1)
            act.activation(rs[:, 0:2], ss[:, 0:2], ACT.Sqrt, scale=1.0 / A_QL, bias=eps[:, 0:1])
            act.activation(rs[:, 2:4], ss[:, 2:4], ACT.Sqrt, scale=1.0 / A_KVL, bias=eps[:, 0:1])
            act.activation(rs[:, 4:6], ss[:, 4:6], ACT.Sqrt, scale=1.0 / A_ROPE, bias=eps[:, 0:1])
            act.activation(rs[:, 6:38], ss[:, 6:38], ACT.Sqrt, scale=1.0 / B_DH, bias=eps[:, 0:1]).then_inc(u_roots, 1)
            for t in range(TT):
                parts(4 + t, cT(xT_hi, t), 3 * P)
            act.wait_ge(unit_used, AT["uq", 0, 0] + 1)
            for t in range(TT):
                for m, (a, n) in enumerate(((0, 512), (512, 256))):
                    act.activation(qa[:, t, a:a + n], ps[:, (4 + m) if t == 0 else m, 0:n], ACT.Copy).then_inc(up_act, 1)
            split_to(AT["ukv", 0, 0] + SPLIT + 1)
            act.wait_ge(up_act, 4)
            act.wait_ge(up_vec, 4)
            act.activation(sqa, qa.rearrange("p t (g d) -> p (t g) d", d=A_QK), ACT.Square)
            act.activation(sqk, kva.rearrange("p t (g d) -> p t g d", d=A_NOPE + A_V)[:, :, :, 0:A_NOPE],
                           ACT.Square).then_inc(a_squared, 1)
            act.wait_ge(a_sums, 1)
            act.activation(rs[:, 0:32], ss[:, 0:32], ACT.Sqrt, scale=1.0 / A_NOPE, bias=eps[:, 0:1])
            act.activation(rs[:, 32:48], ss[:, 32:48], ACT.Sqrt, scale=1.0 / A_ROPE, bias=eps[:, 0:1]).then_inc(a_roots, 1)
            act.wait_ge(angles_ready, 1)
            act.activation(trig[:, :, :, :], turns[:, :, :, :], ACT.Sin).then_inc(trig_ready, 1)
            for t in range(TT):
                for half in range(2):
                    turn_q(4 * t + 2 * half, qta[0:A_QK, 4 * half:4 * half + 4, t * P:(t + 1) * P], A_QK, G_AQ)
            for t in range(TT):
                turn_q(8 + 2 * t, qtb[:, :, t * P:(t + 1) * P], P, G_BQ)
            act.wait_ge(lam_sums, 1)
            act.activation(lams[:, 2:4], lams[:, 0:2], ACT.Exp).then_inc(lam_exps, 1)
            for i in range(A_HEADS + B_HEADS + 2):
                if i < A_HEADS + B_HEADS:
                    exponentials(i, i, s0, i % S0)
                if i >= 2:
                    turn_p(i - 2, pt0)
            turn_y(0)

            split_to(WIDE_FROM + SPLIT - 1)
            norm_roots(1)
            norm_parts(1, 6)
            split_to(WIDE_FROM + SPLIT)
            for j in range(FCH + 1):
                for t in range(TT):
                    if j < FCH:
                        split_to(AT["gate", j, t] + SPLIT + 1)
                    if j >= 1:
                        m = cols(j - 1, FF)[1]
                        whole, s = m // P, TT * (j - 1) + t
                        act.wait_ge(ff_turned, s + 1)
                        if m % P:
                            act.activation(hT_hi[0:m % P, whole, t * P:(t + 1) * P], ps[0:m % P, 3, whole * P:(whole + 1) * P], ACT.Copy)
                        act.activation(hT_hi[:, 0:whole, t * P:(t + 1) * P], blocks(3, whole), ACT.Copy).then_inc(ff_hT_hi, 1)
                if j < FCH:
                    m = cols(j, FF)[1]
                    act.wait_ge(unit_used, AT["gate", j, 1] + 1)
                    for t in range(TT):
                        if j >= 1:
                            act.wait_ge(ff_prod, TT * (j - 1) + t + 1)
                        act.activation(sil[:, t, 0:m], ps[:, (4 * j + t) % 3, 0:m], ACT.Silu).then_inc(ff_silu, 1)
                    split_to(AT["up", j, 1] + SPLIT + 1)
            last_down = AT["qkv", 0, 0] - 1
            split_to(last_down + SPLIT)

            norm_roots(2)
            split_to(last_down + SPLIT + 1)
            norm_parts(2, 10)
            project("qkv", 1, u1, 3 * C_MIX)
            act.wait_ge(proj_vec[1], QKV_J)
            act.wait_ge(proj_act[1], QKV_J)
            act.activation(sqc, u1[:, :, 0:2 * C_MIX], ACT.Square).then_inc(u_squared, 1)
            act.wait_ge(u_sums, 2)
            act.activation(rs[:, :], ss[:, :], ACT.Sqrt, scale=1.0 / C_DH, bias=eps[:, 0:1]).then_inc(u_roots, 1)
            for t in range(TT):
                for half in range(2):
                    turn_q(12 + 4 * t + 2 * half, qtc[:, 4 * half:4 * half + 4, t * P:(t + 1) * P], P, G_CQ)
            for i in range(C_HEADS + 1):
                if i < C_HEADS:
                    for m in range(2):
                        exponentials(2 * i + m, A_HEADS + B_HEADS + 2 * i + m, s1, (2 * i + m) % S1)
                if i >= 1:
                    turn_p(A_HEADS + B_HEADS + i - 1, pt1)
            act.wait_ge(o_normed, 1)
            act.activation(sqo, xs[:, :, :], ACT.Square).then_inc(o_squared, 1)
            act.wait_ge(o_squared, 2)
            act.activation(rs[:, 0:16], ss[:, 0:16], ACT.Sqrt, scale=1.0 / (2 * C_DH), bias=eps[:, 0:1]).then_inc(o_roots, 1)
            turn_y(1)
            split_to(DENSE)

            norm_roots(3)
            norm_parts(3, 14)
            act.wait_ge(gate_diff, 1)
            act.activation(gate_s[:, 5, :], gate_s[:, 4, :], ACT.Exp).then_inc(gate_exp, 1)

            def expert(i):
                first = i * len(EXPERT) + DENSE

                def split_unit(q):
                    r = raw_of(DENSE + q)
                    act.wait_ge(landed[r], i * (16 * len(EXPERT) // RAW) + 16 * (DENSE_LANDINGS[r] + q // RAW + 1))
                    act.wait_ge(unit_used, first + q - SPLIT + 1)
                    act.activation(w_hi[:, (DENSE + q) % SPLIT, :], raw[:, r, :], ACT.Copy).then_inc(hi_ready, 1)

                for q in range(SPLIT):
                    split_unit(q)
                act.wait_ge(wselT_psum, i + 1)
                act.activation(wselT, blocks(4, 2), ACT.Copy).then_inc(wselT_ready, 1)
                for half in range(2):
                    act.wait_ge(scaled_ready, 2 * i + 18 + half + 1)
                    act.activation(xT_hi[:, 4 * half:4 * half + 4, 0:P], scaled[:, half, :].rearrange("p (a b) -> p a b", b=P),
                                   ACT.Copy).then_inc(parts_hi, 1)
                for q, (kind, j, u) in enumerate(EXPERT):
                    if q + SPLIT < len(EXPERT):
                        split_unit(q + SPLIT)
                    if kind == "gate" and u == 1:
                        if j >= 2:
                            act.wait_ge(prod_done, i * ECH + j - 1)
                        act.wait_ge(unit_used, first + q + 1)
                        act.activation(sil[:, j % 2, :], ps[:, 2 * (j % 2), :], ACT.Silu).then_inc(silu_done, 1)
                    if (kind == "gate" and u == 1 and j >= 1) or (kind == "down" and u == 0 and j == ECH - 1):
                        m = j - 1 if kind == "gate" else j
                        act.wait_ge(turn_done, i * ECH + m + 1)
                        act.activation(hT_hi[:, :, 0:P], blocks(4 + m % 2), ACT.Copy).then_inc(hT_part, 1)
                act.wait_ge(unit_used, first + len(EXPERT))
                act.activation(ysb[:, 0:N], ps[:, 6, :], ACT.Copy).then_inc(y_act, 1)

            with act.Fori(0, E) as i:
                expert(i)
            act.wait_ge(routed, 1)
            n_over = act.value_load(over_i[0:1, SPARE:SPARE + 1], min_val=0, max_val=SPARE)
            for s in range(SPARE):
                with act.If(n_over > s):
                    expert(E + s)

        @block.vector
        def _(dve):
            chain = [0]

            def link(ins):
                chain[0] += 1
                ins.then_inc(vec_chain, 1)
                dve.wait_ge(vec_chain, chain[0])

            done = [0]

            def split_to(end):
                for n in range(done[0], min(end, DENSE)):
                    dve.wait_ge(hi_ready, n + 1)
                    for r, a, m in pieces(n):
                        ins = dve.tensor_tensor(w_lo[0:r, n % SPLIT, a:a + m], raw[0:r, raw_of(n), a:a + m],
                                                w_hi[0:r, n % SPLIT, a:a + m].bitcast(F32), ALU.subtract)
                    ins.then_inc(lo_ready, 1)
                done[0] = max(done[0], end)

            def scale(c, bank, n, first):
                dve.tensor_tensor(scaled[:, c % 2, 0:n * P].rearrange("p (a b) -> p a b", b=P), blocks(bank, n),
                                  gains(first, n, P), ALU.mult).then_inc(scaled_ready, 1)

            def low_part(c, lo, hi, n=4):
                dve.wait_ge(scaled_ready, c + 1)
                dve.wait_ge(parts_hi, c + 1)
                return dve.tensor_tensor(lo, scaled[:, c % 2, 0:n * P].rearrange("p (a b) -> p a b", b=P),
                                         hi.bitcast(F32), ALU.subtract)

            def norm_apply(k, first, c):
                for t in range(TT):
                    col = slice(2 * k + t, 2 * k + t + 1)
                    dve.wait_ge(root_ready, 2 * k + t + 1)
                    link(dve.reciprocal(rstd[:, col], root[:, col]))
                    dve.tensor_scalar(xs[:, t, :], h[:, t, :], rstd[:, col], None, ALU.mult).then_inc(xs_ready, 1)
                if k == 0:
                    turn_gains()
                for f in range(5):
                    if f < 4:
                        dve.wait_ge(xT_psum, 4 * k + f + 1)
                        if f >= 2:
                            dve.wait_ge(xT_ready, 4 * k + f - 1)
                        scale(c + f, f, 4, first + 4 * (f % 2))
                    if f >= 1:
                        t, half = divmod(f - 1, 2)
                        v = (slice(None), slice(4 * half, 4 * half + 4), slice(t * P, (t + 1) * P))
                        low_part(c + f - 1, xT_lo[v], xT_hi[v]).then_inc(xT_ready, 1)

            def turn_gains():
                dve.wait_ge(gains_turned, 1)
                dve.tensor_copy(gcol[:, :], ps[:, 7, 0:G_ROWS]).then_inc(gains_ready, 1)
                dve.wait_ge(gains_ready, 1)
                dve.tensor_scalar(gcol[:, G_SUB:G_SUB + 1], gcol[:, G_SUB:G_SUB + 1], 1.0 - LAM_INIT, None,
                                  ALU.mult).then_inc(gains_ready, 1)

            def project(kind, layer, u, total):
                for j in range(-(-total // N)):
                    a, m = cols(j, total)
                    n = AT[kind, j, 1]
                    split_to(n + SPLIT + 1)
                    dve.wait_ge(unit_used, n + 1)
                    dve.tensor_copy(u[:, 1, a:a + m], ps[:, 5 + 2 * (j % 2), 0:m]).then_inc(proj_vec[layer], 1)

            def rotate(x1, x2, cos, sin, tmp):
                dve.tensor_tensor(tmp[0], x1, cos, ALU.mult)
                dve.tensor_tensor(tmp[1], x2, sin, ALU.mult)
                dve.tensor_tensor(tmp[2], x2, cos, ALU.mult)
                link(dve.tensor_tensor(tmp[3], x1, sin, ALU.mult))
                dve.tensor_tensor(x1, tmp[0], tmp[1], ALU.subtract)
                link(dve.tensor_tensor(x2, tmp[2], tmp[3], ALU.add))

            def turn_k(f, dst, rows, col):
                dve.wait_ge(qk_psum, f + 1)
                dve.tensor_scalar(dst, blocks(f % 4)[0:rows], gcol[0:rows, col:col + 1], None, ALU.mult).then_inc(k_turned, 1)

            def scores(u, unit, s, slot, factor, added, slot_head):
                dve.wait_ge(scores_psum, unit + 1)
                if slot_head is not None:
                    dve.wait_ge(p_psum, slot_head + 1)
                for a, n, rows in added:
                    ins = dve.scalar_tensor_tensor(out=s[:, slot, a:a + n], in0=ps[:, unit % 2, a:a + n], scalar=factor,
                                                   in1=rows, op0=ALU.mult, op1=ALU.add)
                ins.then_inc(scores_read, 1)
                dve.wait_ge(scores_read, unit + 1)
                dve.tensor_reduce(negmax[:, u, 0:1], s[:, slot, 0:P], AX.X, ALU.max, negate=True)
                dve.tensor_reduce(negmax[:, u, 1:2], s[:, slot, P:384], AX.X, ALU.max, negate=True).then_inc(max_ready, 1)

            def low_y(layer):
                for f in range(4):
                    half, t = divmod(f, TT)
                    v = (slice(None), slice(4 * half, 4 * half + 4), slice(t * P, (t + 1) * P))
                    dve.wait_ge(yT_hi, 4 * layer + f + 1)
                    if layer == 0:
                        ins = dve.tensor_tensor(xT_lo[v], blocks(f), xT_hi[v].bitcast(F32), ALU.subtract)
                    else:
                        ins = dve.scalar_tensor_tensor(out=xT_lo[v], in0=blocks(f), scalar=gcol[:, G_SUB:G_SUB + 1],
                                                       in1=xT_hi[v].bitcast(F32), op0=ALU.mult, op1=ALU.subtract)
                    ins.then_inc(yT_ready, 1)

            def add_out(banks, last):
                dve.wait_ge(unit_used, last + 1)
                for n in range(4):
                    t, nn = divmod(n, 2)
                    dve.tensor_tensor(h[:, t, nn * N:(nn + 1) * N], h[:, t, nn * N:(nn + 1) * N],
                                      ps[:, banks[n], :], ALU.add).then_inc(h_ready, 1)

            dve.wait_ge(rel_landed, 16)
            dve.tensor_copy(rel[:, 2 * B_CLIP + 1:384],
                            rel[:, 2 * B_CLIP:2 * B_CLIP + 1].to_broadcast([B_HEADS, 383 - 2 * B_CLIP])).then_inc(rel_extended, 1)
            dve.wait_ge(rows_landed, 16 * n_rows)
            dve.wait_ge(consts_ready, n_consts)
            dve.tensor_copy(slots_f[:, :], slots_i[:, :])
            link(dve.tensor_copy(pos_f[:, :], pos_i[:, :]))
            for t in range(TT):
                ins = dve.tensor_scalar(angle[:, t, :], freq[:, :], pos_f[:, t:t + 1], None, ALU.mult)
            link(ins)
            dve.tensor_scalar(turns[:, 0, :, :], angle[:, :, :], 1.0 / (2 * math.pi), None, ALU.mult)
            link(dve.tensor_scalar(turns[:, 1, :, :], angle[:, :, :], 1.0 / (2 * math.pi), 0.25, ALU.mult, ALU.add))
            link(dve.tensor_scalar(turns[:, :, :, :], turns[:, :, :, :], ROUND, None, ALU.add))
            link(dve.tensor_scalar(turns[:, :, :, :], turns[:, :, :, :], ROUND, None, ALU.subtract))
            for m in range(2):
                ins = dve.scalar_tensor_tensor(out=trig[:, m, :, :], in0=turns[:, m, :, :], scalar=-TURN_1,
                                               in1=angle[:, :, :], op0=ALU.mult, op1=ALU.add)
            link(ins)
            for part in (TURN_2, TURN_3):
                link(dve.scalar_tensor_tensor(out=trig[:, :, :, :], in0=turns[:, :, :, :], scalar=-part,
                                              in1=trig[:, :, :, :], op0=ALU.mult, op1=ALU.add))
            link(dve.tensor_scalar(trig[:, 1, :, :], trig[:, 1, :, :], math.pi / 2, None, ALU.add))
            dve.tensor_scalar(turns[:, :, :, :], trig[:, :, :, :], PI_BELOW, -PI_BELOW, ALU.min, ALU.max).then_inc(angles_ready, 1)
            for m in range(2):
                ins = dve.tensor_tensor(lamv[:, 2 * m, :], lamv[:, 2 * m, :], lamv[:, 2 * m + 1, :], ALU.mult)
            link(ins)
            for m in range(2):
                ins = dve.tensor_reduce(lams[:, m:m + 1], lamv[:, 2 * m, :], AX.X, ALU.add)
            ins.then_inc(lam_sums, 1)

            norm_apply(0, G_MIX0, 0)
            dve.wait_ge(bias_landed, 16 * B_HEADS)
            st = bias_rev.ap[0][0]

            def reversed_keys(head, first, n):
                last = bias_rev[:, head, T - 1 - first:T - first]
                return bass.AP(last.tensor, last.offset, [[st, P], [-1, n]])

            split_to(SPLIT)
            dve.wait_ge(router_split, 1)
            dve.tensor_tensor(router_lo[:, :, :], router[:, :, :], router_hi[:, :, :].bitcast(F32), ALU.subtract).then_inc(router_split, 1)
            for head in range(B_HEADS):
                ins = dve.tensor_tensor(bias[:, head, :], reversed_keys(head, 0, T), mask[:, P:384], ALU.add)
            link(ins)

            project("in", 0, u0, EVEN_IN)
            dve.wait_ge(u_squared, 1)
            dve.tensor_reduce(ss[:, 0:2], sq0[:, :, 0:O_CKV], AX.X, ALU.add)
            dve.tensor_reduce(ss[:, 2:4], sq0[:, :, O_CKV:O_KR], AX.X, ALU.add)
            dve.tensor_reduce(ss[:, 4:6], sq0[:, :, O_KR:O_BQ], AX.X, ALU.add)
            dve.tensor_reduce(ss[:, 6:38].rearrange("p (t g) -> p t g", t=TT),
                              sq0[:, :, O_BQ:O_BV].rearrange("p t (g d) -> p t g d", d=B_DH), AX.X, ALU.add).then_inc(u_sums, 1)
            dve.wait_ge(u_roots, 1)
            link(dve.reciprocal(rs[:, 0:38], rs[:, 0:38]))
            for t in range(TT):
                dve.tensor_scalar(u0[:, t, 0:O_CKV], u0[:, t, 0:O_CKV], rs[:, t:t + 1], None, ALU.mult)
                dve.tensor_scalar(u0[:, t, O_CKV:O_KR], u0[:, t, O_CKV:O_KR], rs[:, 2 + t:3 + t], None, ALU.mult).then_inc(c_normed, 1)
            for t in range(TT):
                dve.wait_ge(c_psum, t + 1)
                scale(4 + t, t, 3, G_C)
            for t in range(TT):
                low_part(4 + t, cT(xT_lo, t), cT(xT_hi, t), 3).then_inc(c_ready, 1)
            for t in range(TT):
                dve.scalar_tensor_tensor(out=kr[:, t, :], in0=u0[:, t, O_KR:O_BQ], scalar=rs[:, 4 + t:5 + t],
                                         in1=ga_rot[:, 1, :], op0=ALU.mult, op1=ALU.mult)
                heads = u0[:, t, O_BQ:O_BV].rearrange("p (g d) -> p g d", d=B_DH)
                ins = dve.tensor_tensor(heads, heads, rs[:, 6 + 16 * t:22 + 16 * t].unsqueeze(2).to_broadcast([P, 16, B_DH]), ALU.mult)
            link(ins)
            dve.wait_ge(unit_used, AT["ukv", 0, 0] + 1)
            for t in range(TT):
                for m in range(2):
                    dve.tensor_copy(kva[:, t, m * N:(m + 1) * N], ps[:, (6 if t == 0 else 2) + m, :]).then_inc(up_vec, 1)
            split_to(AT["ukv", 0, 0] + SPLIT + 1)
            dve.wait_ge(a_squared, 1)
            dve.tensor_reduce(ss[:, 0:16], sqa[:, :, 0:A_NOPE], AX.X, ALU.add)
            dve.tensor_reduce(ss[:, 16:32].rearrange("p (t g) -> p t g", t=TT), sqk, AX.X, ALU.add)
            dve.tensor_reduce(ss[:, 32:48], sqa[:, :, A_NOPE:A_QK], AX.X, ALU.add).then_inc(a_sums, 1)
            dve.wait_ge(a_roots, 1)
            link(dve.reciprocal(rs[:, 0:48], rs[:, 0:48]))
            qh = qa.rearrange("p t (g d) -> p (t g) d", d=A_QK)
            kh = ka.rearrange("p t (g d) -> p t g d", d=A_QK)
            kvh = kva.rearrange("p t (g d) -> p t g d", d=A_NOPE + A_V)
            dve.tensor_tensor(qh[:, :, 0:A_NOPE], qh[:, :, 0:A_NOPE], rs[:, 0:16].unsqueeze(2).to_broadcast([P, 16, A_NOPE]), ALU.mult)
            for t in range(TT):
                dve.tensor_tensor(kh[:, t, :, 0:A_NOPE], kvh[:, t, :, 0:A_NOPE],
                                  rs[:, 16 + 8 * t:24 + 8 * t].unsqueeze(2).to_broadcast([P, 8, A_NOPE]), ALU.mult)
            link(dve.tensor_tensor(qh[:, :, A_NOPE:A_QK], qh[:, :, A_NOPE:A_QK],
                                   rs[:, 32:48].unsqueeze(2).to_broadcast([P, 16, A_ROPE]), ALU.mult))
            link(dve.tensor_tensor(qh[:, :, A_NOPE:A_QK], qh[:, :, A_NOPE:A_QK],
                                   ga_rot[:, 0:1, :].to_broadcast([P, 16, A_ROPE]), ALU.mult))
            dve.wait_ge(trig_ready, 1)
            q4 = qa.rearrange("p t (g d) -> p t g d", d=A_QK)

            def tables(first, n, groups):
                return [trig[:, m, :, first:first + n].unsqueeze(2).to_broadcast([P, TT, groups, n]) for m in (1, 0)]

            cos, sin = tables(0, NF_A, A_HEADS)
            rotate(q4[:, :, :, A_NOPE:A_NOPE + NF_A], q4[:, :, :, A_NOPE + NF_A:A_QK], cos, sin, rot_a)
            rotate(kr[:, :, 0:NF_A], kr[:, :, NF_A:A_ROPE], trig[:, 1, :, 0:NF_A], trig[:, 0, :, 0:NF_A], rot_k)
            dve.tensor_copy(kh[:, :, :, A_NOPE:A_QK], kr.unsqueeze(2).to_broadcast([P, TT, A_HEADS, A_ROPE])).then_inc(qk_normed, 1)
            for t in range(TT):
                for half in range(2):
                    turn_k(4 * t + 2 * half + 1, kta[0:A_QK, 4 * half:4 * half + 4, t * P:(t + 1) * P], A_QK, G_AK)
            for t in range(TT):
                turn_k(8 + 2 * t + 1, ktb[:, :, t * P:(t + 1) * P], P, G_BK)

            def head_outputs(layer, first, heads, width, banks, y, dst_col):
                for t in range(TT):
                    for n, bank in enumerate(banks[t]):
                        k = heads // len(banks[t])
                        c = first + n * k * (2 if layer else 1)
                        r = rinv[:, c:c + k, t] if not layer else rinv[:, c:c + 2 * k:2, t]
                        o = y[:, t, dst_col + n * N:dst_col + (n + 1) * N].rearrange("p (g d) -> p g d", d=width)
                        ins = dve.tensor_tensor(o, ps[:, bank, :].rearrange("p (g d) -> p g d", d=width),
                                                r.unsqueeze(2).to_broadcast([P, k, width]), ALU.mult)
                return ins

            for u in range(A_HEADS + B_HEADS):
                if u < A_HEADS:
                    added, factor = [(0, 384, mask[:, :])], A_QK ** -0.5
                else:
                    row = bias[:, u - A_HEADS, :]
                    added, factor = [(0, P, row[:, P:T]), (P, T, row)], B_DH ** -0.5
                scores(u, u, s0, u % S0, factor, added, u - S0 if u >= S0 else None)
                if u == A_HEADS + 4:
                    dve.wait_ge(pv_done, A_HEADS)
                    link(dve.reciprocal(rinv[:, 0:A_HEADS, :], psum_l[:, 0:A_HEADS, :]))
                    head_outputs(0, 0, A_HEADS, A_V, [[4], [5]], xs, 0).then_inc(y_ready, 1)
            dve.wait_ge(pv_done, A_HEADS + B_HEADS)
            link(dve.reciprocal(rinv[:, A_HEADS:16, :], psum_l[:, A_HEADS:16, :]))
            head_outputs(0, A_HEADS, B_HEADS, B_DH, [[6], [7]], xs, N).then_inc(y_ready, 1)
            low_y(0)
            split_to(WIDE_FROM + SPLIT - 1)
            add_out([4, 5, 6, 7], AT["out0", 0, DC // 2 - 1])

            norm_apply(1, G_FF0, 6)
            split_to(WIDE_FROM + SPLIT)
            for j in range(FCH + 1):
                for t in range(TT):
                    if j < FCH:
                        split_to(AT["gate", j, t] + SPLIT + 1)
                    if j >= 1:
                        m = cols(j - 1, FF)[1]
                        whole, s = m // P, TT * (j - 1) + t
                        dve.wait_ge(ff_hT_hi, s + 1)
                        if m % P:
                            v = (slice(0, m % P), whole, slice(t * P, (t + 1) * P))
                            dve.tensor_tensor(hT_lo[v], ps[0:m % P, 3, whole * P:(whole + 1) * P], hT_hi[v].bitcast(F32), ALU.subtract)
                        v = (slice(None), slice(0, whole), slice(t * P, (t + 1) * P))
                        dve.tensor_tensor(hT_lo[v], blocks(3, whole), hT_hi[v].bitcast(F32), ALU.subtract).then_inc(ff_hT, 1)
                if j < FCH:
                    m = cols(j, FF)[1]
                    split_to(AT["up", j, 0] + SPLIT + 1)
                    dve.wait_ge(unit_used, AT["up", j, 1] + 1)
                    for t in range(TT):
                        dve.wait_ge(ff_silu, TT * j + t + 1)
                        dve.tensor_tensor(prod[:, t, 0:m], sil[:, t, 0:m], ps[:, (4 * j + 2 + t) % 3, 0:m], ALU.mult).then_inc(ff_prod, 1)
                    split_to(AT["up", j, 1] + SPLIT + 1)
            last_down = AT["qkv", 0, 0] - 1
            split_to(last_down + SPLIT)
            add_out([4, 5, 6, 7], last_down)

            norm_apply(2, G_MIX1, 10)
            split_to(last_down + SPLIT + 1)
            dve.wait_ge(lam_exps, 1)
            link(dve.tensor_tensor(lams[:, 4:5], lams[:, 3:4], lams[:, 2:3], ALU.subtract))
            link(dve.tensor_scalar(lams[:, 5:6], lams[:, 4:5], -LAM_INIT, None, ALU.add))
            project("qkv", 1, u1, 3 * C_MIX)
            dve.wait_ge(u_squared, 2)
            dve.tensor_reduce(ss[:, :], sqc.rearrange("p t (g d) -> p (t g) d", d=C_DH), AX.X, ALU.add).then_inc(u_sums, 1)
            dve.wait_ge(u_roots, 2)
            link(dve.reciprocal(rs[:, :], rs[:, :]))
            for t in range(TT):
                heads = u1[:, t, 0:2 * C_MIX].rearrange("p (g d) -> p g d", d=C_DH)
                ins = dve.tensor_tensor(heads, heads, rs[:, 32 * t:32 * t + 32].unsqueeze(2).to_broadcast([P, 32, C_DH]), ALU.mult)
            link(ins)
            for t in range(TT):
                rot = u1[:, t, 0:2 * C_MIX].rearrange("p (m g d) -> p m g d", m=2, d=C_DH)[:, :, :, 0:C_ROPE]
                ins = dve.tensor_tensor(rot, rot, gc_rot[:, :, :].unsqueeze(2).to_broadcast([P, 2, C_GROUPS, C_ROPE]), ALU.mult)
            link(ins)
            g4 = u1[:, :, 0:2 * C_MIX].rearrange("p t (g d) -> p t g d", d=C_DH)
            cos, sin = tables(NF_A, NF_C, 2 * C_GROUPS)
            rotate(g4[:, :, :, 0:NF_C], g4[:, :, :, NF_C:C_ROPE], cos, sin, rot_c)
            dve.engine_nop().then_inc(qk_normed, 1)
            for t in range(TT):
                for half in range(2):
                    turn_k(12 + 4 * t + 2 * half + 1, ktc[:, 4 * half:4 * half + 4, t * P:(t + 1) * P], P, G_CK)

            def difference(i):
                dve.wait_ge(exp_done, 16 + 2 * i + 2)
                link(dve.reciprocal(rinv[:, 2 * i:2 * i + 2, :], psum_l[:, 2 * i:2 * i + 2, :]))
                link(dve.scalar_tensor_tensor(out=coef[:, i, :], in0=psum_l[:, 2 * i, :], scalar=lams[:, 5:6],
                                              in1=rinv[:, 2 * i + 1, :], op0=ALU.mult, op1=ALU.mult))
                a, b = (2 * i) % S1, (2 * i + 1) % S1
                for t, (c0, c1) in enumerate(((0, P), (P, 384))):
                    ins = dve.scalar_tensor_tensor(out=s1[:, a, c0:c1], in0=s1[:, b, c0:c1], scalar=coef[:, i, t:t + 1],
                                                   in1=s1[:, a, c0:c1], op0=ALU.mult, op1=ALU.add)
                ins.then_inc(diff_done, 1)

            for i in range(C_HEADS + 1):
                if i < C_HEADS:
                    for m in range(2):
                        scores(2 * i + m, 16 + 2 * i + m, s1, (2 * i + m) % S1, C_DH ** -0.5, [(0, 384, mask[:, :])],
                               16 + i - S1 // 2 if i >= S1 // 2 else None)
                if i >= 1:
                    difference(i - 1)
            dve.wait_ge(pv_done, 16 + C_HEADS)
            head_outputs(1, 0, C_HEADS, 2 * C_DH, [[4, 5], [6, 7]], xs, 0).then_inc(o_normed, 1)
            dve.wait_ge(o_squared, 1)
            dve.tensor_reduce(ss[:, 0:16], sqo.rearrange("p t (g d) -> p (t g) d", d=2 * C_DH), AX.X, ALU.add).then_inc(o_squared, 1)
            dve.wait_ge(o_roots, 1)
            link(dve.reciprocal(rs[:, 0:16], rs[:, 0:16]))
            yh = xs[:, :, :].rearrange("p t (g d) -> p (t g) d", d=2 * C_DH)
            dve.tensor_tensor(yh, yh, rs[:, 0:16].unsqueeze(2).to_broadcast([P, 16, 2 * C_DH]), ALU.mult).then_inc(y_ready, 1)
            low_y(1)
            split_to(DENSE)
            add_out([4, 5, 6, 7], AT["out1", 0, DC // 2 - 1])

            norm_apply(3, G_FF1, 14)
            g, gs = gate_t, gate_s

            def per_token(a):
                return a.unsqueeze(2).to_broadcast([P, TT, E])

            link(dve.tensor_scalar(load8[:, 7, :], slots_f[:, 0:E], -1.0, float(E), ALU.mult, ALU.add))
            keys = load8[:, 7:8, :].to_broadcast([P, TT, E])
            dve.wait_ge(logits_psum, 1)
            link(dve.tensor_copy(g[:, 0, :, :], ps[:, 4, 0:TT * E].rearrange("p (t e) -> p t e", e=E)))

            def top(src, m, key, hot):
                link(dve.tensor_reduce(gs[:, m, :], g[:, src, :, :], AX.X, ALU.max))
                link(dve.tensor_tensor(g[:, key, :, :], g[:, src, :, :], per_token(gs[:, m, :]), ALU.is_equal))
                link(dve.tensor_tensor(g[:, key, :, :], g[:, key, :, :], keys, ALU.mult))
                link(dve.tensor_reduce(gs[:, m + 1, :], g[:, key, :, :], AX.X, ALU.max))
                link(dve.tensor_tensor(g[:, hot, :, :], g[:, key, :, :], per_token(gs[:, m + 1, :]), ALU.is_equal))

            top(0, 0, 1, 2)
            link(dve.scalar_tensor_tensor(out=g[:, 3, :, :], in0=g[:, 2, :, :], scalar=-3e38, in1=g[:, 0, :, :],
                                          op0=ALU.mult, op1=ALU.add))
            top(3, 2, 4, 5)
            dve.tensor_tensor(g[:, 6, :, :], g[:, 2, :, :], g[:, 5, :, :], ALU.add).then_inc(chosen_ready, 1)
            dve.tensor_tensor(gs[:, 4, :], gs[:, 2, :], gs[:, 0, :], ALU.subtract).then_inc(gate_diff, 1)
            dve.wait_ge(gate_exp, 1)
            link(dve.tensor_scalar(gs[:, 6, :], gs[:, 5, :], 1.0, None, ALU.add))
            link(dve.reciprocal(gs[:, 7, :], gs[:, 6, :]))
            link(dve.tensor_tensor(gs[:, 8, :], gs[:, 5, :], gs[:, 7, :], ALU.mult))
            dve.tensor_tensor(g[:, 7, :, :], g[:, 2, :, :], per_token(gs[:, 7, :]), ALU.mult)
            link(dve.tensor_tensor(g[:, 8, :, :], g[:, 5, :, :], per_token(gs[:, 8, :]), ALU.mult))
            dve.tensor_tensor(comb[:, :, 0:E], g[:, 7, :, :], g[:, 8, :, :], ALU.add)
            dve.wait_ge(chosen_ready, 1)
            link(dve.tensor_scalar(g[:, 9, :, :], g[:, 6, :, :], -FAR, FAR, ALU.mult, ALU.add))
            dve.wait_ge(rank_psum, 1)
            dve.tensor_tensor(rank[:, :, 0:E], g[:, 9, :, :], ps[:, 5, 0:TT * E].rearrange("p (t e) -> p t e", e=E), ALU.add)
            link(dve.tensor_scalar(load8[:, 0, :], ps[:, 5, TT * E:(TT + 1) * E], float(P), None, ALU.is_gt))
            link(dve.memset(load8[:, 1, :], 0.0))
            for e in range(1, E):
                link(dve.tensor_tensor(load8[:, 1, e:e + 1], load8[:, 1, e - 1:e], load8[:, 0, e - 1:e], ALU.add))
            dve.tensor_tensor(over_s[:, SPARE:SPARE + 1], load8[:, 1, E - 1:E], load8[:, 0, E - 1:E], ALU.add)
            for s in range(SPARE):
                link(dve.scalar_tensor_tensor(out=load8[:, 2, :], in0=load8[:, 1, :], scalar=float(s), in1=load8[:, 0, :],
                                              op0=ALU.is_equal, op1=ALU.mult))
                pick = load8[:, 2:3, :].to_broadcast([P, TT, E])
                dve.tensor_reduce(over_s[:, 4:5], load8[:, 2, :], AX.X, ALU.add)
                dve.tensor_tensor(load8[:, 3, :], load8[:, 2, :], slots_f[:, 0:E], ALU.mult)
                dve.tensor_tensor(g[:, 10, :, :], pick, rank[:, :, 0:E], ALU.mult)
                link(dve.tensor_tensor(g[:, 11, :, :], pick, comb[:, :, 0:E], ALU.mult))
                dve.tensor_reduce(over_s[:, s:s + 1], load8[:, 3, :], AX.X, ALU.add)
                dve.tensor_scalar(over_s[:, 5:6], over_s[:, 4:5], -FAR, FAR - P, ALU.mult, ALU.add)
                dve.tensor_reduce(gs[:, 9, :], g[:, 10, :, :], AX.X, ALU.add)
                link(dve.tensor_reduce(comb[:, :, E + s], g[:, 11, :, :], AX.X, ALU.add))
                link(dve.tensor_scalar(rank[:, :, E + s], gs[:, 9, :], over_s[:, 5:6], None, ALU.add))
            dve.tensor_copy(over_i[:, :], over_s[:, 0:4]).then_inc(routed, 1)

            def expert(i):
                first = i * len(EXPERT) + DENSE

                def split_unit(q):
                    dve.wait_ge(hi_ready, first + q + 1)
                    k = (DENSE + q) % SPLIT
                    dve.tensor_tensor(w_lo[:, k, :], raw[:, raw_of(DENSE + q), :], w_hi[:, k, :].bitcast(F32),
                                      ALU.subtract).then_inc(lo_ready, 1)

                for t in range(TT):
                    r, c = rank[:, t, bass.ds(i, 1)], comb[:, t, bass.ds(i, 1)]
                    dve.tensor_scalar(sel[:, t, :], slots_f[:, :], r, None, ALU.is_equal)
                    ins = dve.tensor_scalar(wsel[:, t, :], slots_f[:, :], r, c, ALU.is_equal, ALU.mult)
                ins.then_inc(sel_ready, 1)
                split_unit(0)
                for half in range(2):
                    dve.wait_ge(gather_psum, 2 * i + half + 1)
                    dve.tensor_tensor(scaled[:, half, :].rearrange("p (a b) -> p a b", b=P), blocks(6 + half),
                                      gains(G_FF1 + 4 * half, 4, P), ALU.mult).then_inc(scaled_ready, 1)
                for half in range(2):
                    v = (slice(None), slice(4 * half, 4 * half + 4), slice(0, P))
                    dve.wait_ge(parts_hi, 2 * i + 18 + half + 1)
                    dve.tensor_tensor(xT_lo[v], scaled[:, half, :].rearrange("p (a b) -> p a b", b=P), xT_hi[v].bitcast(F32),
                                      ALU.subtract).then_inc(xg_ready, 1)
                for q in range(1, SPLIT):
                    split_unit(q)
                for q, (kind, j, u) in enumerate(EXPERT):
                    if q + SPLIT < len(EXPERT):
                        split_unit(q + SPLIT)
                    if (kind == "gate" and u == 1 and j >= 1) or (kind == "down" and u == 0 and j == ECH - 1):
                        m = j - 1 if kind == "gate" else j
                        dve.wait_ge(hT_part, i * ECH + m + 1)
                        dve.tensor_tensor(hT_lo[:, :, 0:P], blocks(4 + m % 2), hT_hi[:, :, 0:P].bitcast(F32),
                                          ALU.subtract).then_inc(hT_ready, 1)
                    if kind == "up" and u == 1:
                        dve.wait_ge(silu_done, i * ECH + j + 1)
                        dve.wait_ge(unit_used, first + q + 1)
                        dve.tensor_tensor(prod[:, j % 2, :], sil[:, j % 2, :], ps[:, 2 * (j % 2) + 1, :], ALU.mult).then_inc(prod_done, 1)
                dve.wait_ge(unit_used, first + len(EXPERT))
                dve.tensor_copy(ysb[:, N:D], ps[:, 7, :]).then_inc(y_vec, 1)
                for n in range(4):
                    t, nn = divmod(n, 2)
                    dve.wait_ge(scatter_psum, 4 * i + n + 1)
                    dve.tensor_tensor(h[:, t, nn * N:(nn + 1) * N], h[:, t, nn * N:(nn + 1) * N], ps[:, n, :],
                                      ALU.add).then_inc(scatter_read, 1)
                dve.wait_ge(scatter_read, 4 * i + 5)

            dve.wait_ge(routed, 1)
            dve.engine_nop().then_inc(scatter_read, 1)
            with dve.Fori(0, E) as i:
                expert(i)
            n_over = dve.value_load(over_i[0:1, SPARE:SPARE + 1], min_val=0, max_val=SPARE)
            for s in range(SPARE):
                with dve.If(n_over > s):
                    expert(E + s)
            dve.engine_nop().then_inc(h_final, 1)

        @block.tensor
        def _(pe):
            def split(n):
                pe.wait_ge(lo_ready, n + 1)
                k = {"uq": 2, "ukv": 1, "out0": 2, "out1": 2, "down": 2}.get(STREAM[n][0], 4)
                m = pieces(n)[0][2] if len(pieces(n)) == 1 else 2 * D
                return [x[:, n % SPLIT, 0:m].rearrange("p (k n) -> p k n", k=k) for x in (w_hi, w_lo)]

            def product(out, x_hi, x_lo, hi, lo, start, stop):
                pe.matmul(out, x_hi, hi, start=start, stop=False)
                pe.matmul(out, x_hi, lo, start=False, stop=False)
                return pe.matmul(out, x_lo, hi, start=False, stop=stop)

            def norm_turn(k):
                for t in range(TT):
                    pe.wait_ge(xs_ready, 2 * k + t + 1)
                    for c in range(DC):
                        ins = pe.transpose(ps[:, 2 * t + c // 4, (c % 4) * P:(c % 4 + 1) * P], xs[:, t, c * P:(c + 1) * P], ident[:, :])
                        if c % 4 == 3:
                            ins.then_inc(xT_psum, 1)

            def project(layer, kind, total, k):
                pe.wait_ge(xT_ready, 4 * k + 4)
                for j in range(-(-total // N)):
                    m = cols(j, total)[1]
                    for u in range(2):
                        hi, lo = split(AT[kind, j, u])
                        for t in range(TT):
                            if j >= 2 and u == 0:
                                pe.wait_ge((proj_act if t == 0 else proj_vec)[layer], j - 1)
                            tok = slice(t * P, (t + 1) * P)
                            for c in range(4):
                                k8 = 4 * u + c
                                ins = product(ps[:, 4 + (2 * j + t) % 4, 0:m], xT_hi[:, k8, tok], xT_lo[:, k8, tok],
                                              hi[:, c, :], lo[:, c, :], k8 == 0, k8 == DC - 1)
                        ins.then_inc(unit_used, 1)

            def turn_heads(f, src, rows):
                if f % 12 >= 4:
                    pe.wait_ge(k_turned if f % 2 else q_turned, f // 2 - 1)
                for n in range(4):
                    ins = pe.transpose(ps[0:rows, f % 4, n * P:(n + 1) * P], src(n), ident[:, :])
                ins.then_inc(qk_psum, 1)

            def scores(unit, q, k):
                if unit % 16 >= 2:
                    pe.wait_ge(scores_read, unit - 1)
                b = unit % 2
                pe.matmul(ps[:, b, 0:P], q(0), k(P), start=True, stop=True)
                pe.matmul(ps[:, b, P:384], q(1), k(T), start=True, stop=True).then_inc(scores_psum, 1)

            def turn_p(head, ready, count, s, slot):
                pe.wait_ge(ready, count)
                if head >= 2:
                    pe.wait_ge(p_turned, head - 1)
                for n in range(3):
                    ins = pe.transpose(ps[:, 2 + head % 2, n * P:(n + 1) * P], s[:, slot, n * P:(n + 1) * P], ident[:, :])
                ins.then_inc(p_psum, 1)

            def weigh_values(head, pt, v, out0, out1):
                pe.wait_ge(p_turned, head + 1)
                p = pt[:, head % 2, :]
                pe.matmul(out0, p[:, 0:P], v(0), start=True, stop=True)
                pe.matmul(out1, p[:, P:2 * P], v(0), start=True, stop=False)
                pe.matmul(out1, p[:, 2 * P:384], v(1), start=False, stop=True).then_inc(pv_done, 1)

            def out_projection(layer):
                for f in range(4):
                    half, t = divmod(f, TT)
                    if t == 0:
                        pe.wait_ge(y_ready, 2 * layer + half + 1 if layer == 0 else 3)
                    for n in range(4):
                        c = 4 * half + n
                        ins = pe.transpose(ps[:, f, n * P:(n + 1) * P], xs[:, t, c * P:(c + 1) * P], ident[:, :])
                    ins.then_inc(yT_psum, 1)
                pe.wait_ge(yT_ready, 4 * layer + 4)
                for u in range(DC // 2):
                    hi, lo = split(AT[f"out{layer}", 0, u])
                    for c in range(2):
                        k = 2 * u + c
                        for n in range(4):
                            t, nn = divmod(n, 2)
                            tok, col = slice(t * P, (t + 1) * P), slice(nn * N, (nn + 1) * N)
                            ins = product(ps[:, 4 + n, :], xT_hi[:, k, tok], xT_lo[:, k, tok], hi[:, c, col], lo[:, c, col],
                                          k == 0, k == DC - 1)
                    ins.then_inc(unit_used, 1)

            pe.wait_ge(consts_ready, n_consts)
            pe.wait_ge(gains_landed, 16 * n_gains)
            pe.transpose(ps[:, 7, 0:G_ROWS], gain_rows[:, :], ident[0:G_ROWS, 0:G_ROWS]).then_inc(gains_turned, 1)
            norm_turn(0)
            project(0, "in", EVEN_IN, 0)
            for t in range(TT):
                pe.wait_ge(c_normed, t + 1)
                for n in range(3):
                    ins = pe.transpose(ps[:, t, n * P:(n + 1) * P], u0[:, t, n * P:(n + 1) * P], ident[:, :])
                ins.then_inc(c_psum, 1)
            pe.wait_ge(c_ready, TT)
            hi, lo = split(AT["uq", 0, 0])
            for t in range(TT):
                for m, (a, n) in enumerate(((0, 512), (512, 256))):
                    for c in range(2):
                        ins = product(ps[:, (4 + m) if t == 0 else m, 0:n], cT(xT_hi, t)[:, c, :], cT(xT_lo, t)[:, c, :],
                                      hi[:, c, a:a + n], lo[:, c, a:a + n], c == 0, c == 1)
            ins.then_inc(unit_used, 1)
            hi, lo = split(AT["ukv", 0, 0])
            for t in range(TT):
                for m in range(2):
                    ins = product(ps[:, (6 if t == 0 else 2) + m, :], cT(xT_hi, t)[:, 2, :], cT(xT_lo, t)[:, 2, :],
                                  hi[:, 0, m * N:(m + 1) * N], lo[:, 0, m * N:(m + 1) * N], True, True)
            ins.then_inc(unit_used, 1)
            pe.wait_ge(qk_normed, 1)
            for t in range(TT):
                for half in range(2):
                    for m, src in enumerate((qa, ka)):
                        turn_heads(4 * t + 2 * half + m,
                                   lambda n: src[:, t, (4 * half + n) * A_QK:(4 * half + n + 1) * A_QK], A_QK)
            for t in range(TT):
                for m, first in enumerate((O_BQ, O_BK)):
                    turn_heads(8 + 2 * t + m, lambda n: u0[:, t, first + n * P:first + (n + 1) * P], P)
            pe.wait_ge(q_turned, 6)
            pe.wait_ge(k_turned, 6)
            heads = A_HEADS + B_HEADS
            for i in range(heads + 3):
                if i < A_HEADS:
                    scores(i, lambda t: qta[0:A_QK, i, t * P:(t + 1) * P], lambda n: kta[0:A_QK, i, 0:n])
                elif i < heads:
                    pair, m = divmod(i - A_HEADS, 2)
                    r = slice(m * B_DH, (m + 1) * B_DH)
                    scores(i, lambda t: qtb[r, pair, t * P:(t + 1) * P], lambda n: ktb[r, pair, 0:n])
                if 2 <= i < heads + 2:
                    turn_p(i - 2, exp_done, i - 1, s0, (i - 2) % S0)
                if i >= 3:
                    n = i - 3
                    if n < A_HEADS:
                        weigh_values(n, pt0, lambda t: kva[:, t, n * P + A_NOPE:(n + 1) * P],
                                     ps[:, 4, n * A_V:(n + 1) * A_V], ps[:, 5, n * A_V:(n + 1) * A_V])
                    else:
                        m = n - A_HEADS
                        weigh_values(n, pt0, lambda t: u0[:, t, O_BV + m * B_DH:O_BV + (m + 1) * B_DH],
                                     ps[:, 6, m * B_DH:(m + 1) * B_DH], ps[:, 7, m * B_DH:(m + 1) * B_DH])
            out_projection(0)

            norm_turn(1)
            pe.wait_ge(xT_ready, 8)
            for j in range(FCH + 1):
                for part, kind in enumerate(("gate", "up")):
                    for u in range(2):
                        if j < FCH:
                            m = cols(j, FF)[1]
                            hi, lo = split(AT[kind, j, u])
                            for t in range(TT):
                                use = 4 * j + 2 * part + t
                                if u == 0 and use >= 3:
                                    jj, was = divmod(use - 3, 4)
                                    pe.wait_ge(ff_silu if was < 2 else ff_prod, TT * jj + was % 2 + 1)
                                tok = slice(t * P, (t + 1) * P)
                                for c in range(4):
                                    k = 4 * u + c
                                    ins = product(ps[:, use % 3, 0:m], xT_hi[:, k, tok], xT_lo[:, k, tok], hi[:, c, :], lo[:, c, :],
                                                  k == 0, k == DC - 1)
                            ins.then_inc(unit_used, 1)
                        if kind == "gate" and j >= 1:
                            m, s = cols(j - 1, FF)[1], TT * (j - 1) + u
                            pe.wait_ge(ff_prod, s + 1)
                            if s >= 1:
                                pe.wait_ge(ff_hT, s)
                            for n in range(-(-m // P)):
                                k = min(P, m - n * P)
                                ins = pe.transpose(ps[0:k, 3, n * P:(n + 1) * P], prod[:, u, n * P:n * P + k], ident[:, :])
                            ins.then_inc(ff_turned, 1)
                if j >= 1:
                    pe.wait_ge(ff_hT, TT * j)
                    for k in range(4 * (j - 1), min(4 * j, FK)):
                        if k % 2 == 0:
                            hi, lo = split(AT["down", j - 1, k % 4 // 2])
                        r = min(P, FF - k * P)
                        for n in range(4):
                            t, nn = divmod(n, 2)
                            tok, col = slice(t * P, (t + 1) * P), slice(nn * N, (nn + 1) * N)
                            ins = product(ps[:, 4 + n, :], hT_hi[0:r, k % 4, tok], hT_lo[0:r, k % 4, tok],
                                          hi[0:r, k % 2, col], lo[0:r, k % 2, col], k == 0, k == FK - 1)
                        if k % 2 == 1:
                            ins.then_inc(unit_used, 1)

            norm_turn(2)
            project(1, "qkv", 3 * C_MIX, 2)
            pe.wait_ge(qk_normed, 2)
            for t in range(TT):
                for half in range(2):
                    for m in range(2):
                        turn_heads(12 + 4 * t + 2 * half + m,
                                   lambda n: u1[:, t, m * C_MIX + (4 * half + n) * P:m * C_MIX + (4 * half + n + 1) * P], P)
            pe.wait_ge(q_turned, 10)
            pe.wait_ge(k_turned, 10)
            for i in range(C_HEADS + 2):
                if i < C_HEADS:
                    for m in range(2):
                        r = slice(m * C_DH, (m + 1) * C_DH)
                        scores(16 + 2 * i + m, lambda t: qtc[r, i, t * P:(t + 1) * P], lambda n: ktc[r, i, 0:n])
                if i >= 1 and i <= C_HEADS:
                    turn_p(16 + i - 1, diff_done, i, s1, (2 * (i - 1)) % S1)
                if i >= 2:
                    n = i - 2
                    c = (n % 4) * P
                    weigh_values(16 + n, pt1, lambda t: u1[:, t, 2 * C_MIX + n * P:2 * C_MIX + (n + 1) * P],
                                 ps[:, 4 + n // 4, c:c + P], ps[:, 6 + n // 4, c:c + P])
            out_projection(1)

            norm_turn(3)
            pe.wait_ge(xT_ready, 16)
            pe.wait_ge(router_split, 2)
            for t in range(TT):
                for c in range(DC):
                    ins = product(ps[:, 4, t * E:(t + 1) * E], xT_hi[:, c, t * P:(t + 1) * P], xT_lo[:, c, t * P:(t + 1) * P],
                                  router_hi[:, c, :], router_lo[:, c, :], c == 0, c == DC - 1)
            ins.then_inc(logits_psum, 1)
            pe.wait_ge(chosen_ready, 1)
            chosen = gate_t[:, 6, :, :]
            pe.matmul(ps[:, 5, 0:E], tri[:, :], chosen[:, 0, :], start=True, stop=True)
            pe.matmul(ps[:, 5, E:2 * E], ones[:, :], chosen[:, 0, :], start=True, stop=False)
            pe.matmul(ps[:, 5, E:2 * E], tri[:, :], chosen[:, 1, :], start=False, stop=True)
            pe.matmul(ps[:, 5, 2 * E:3 * E], ones[:, :], chosen[:, 0, :], start=True, stop=False)
            pe.matmul(ps[:, 5, 2 * E:3 * E], ones[:, :], chosen[:, 1, :], start=False, stop=True).then_inc(rank_psum, 1)
            pe.wait_ge(routed, 1)

            def expert(i):
                first = i * len(EXPERT) + DENSE
                pe.wait_ge(sel_ready, i + 1)
                for t in range(TT):
                    ins = pe.transpose(ps[:, 4, t * P:(t + 1) * P], wsel[:, t, :], ident[:, :])
                ins.then_inc(wselT_psum, 1)
                for c in range(DC):
                    for t in range(TT):
                        ins = pe.matmul(ps[:, 6 + c // 4, (c % 4) * P:(c % 4 + 1) * P], xs[:, t, c * P:(c + 1) * P], sel[:, t, :],
                                        start=(t == 0), stop=(t == TT - 1))
                    if c % 4 == 3:
                        ins.then_inc(gather_psum, 1)
                pe.wait_ge(xg_ready, 2 * i + 2)
                pe.wait_ge(wselT_ready, i + 1)
                pe.wait_ge(scatter_read, 4 * i + 1)

                def turn(j):
                    pe.wait_ge(prod_done, i * ECH + j + 1)
                    if j >= 2:
                        pe.wait_ge(hT_ready, i * ECH + j - 1)
                    for n in range(4):
                        ins = pe.transpose(ps[:, 4 + j % 2, n * P:(n + 1) * P], prod[:, j % 2, n * P:(n + 1) * P], ident[:, :])
                    ins.then_inc(turn_done, 1)

                for q, (kind, j, u) in enumerate(EXPERT):
                    if kind == "down" and u == 0:
                        if j == ECH - 1:
                            turn(j)
                        pe.wait_ge(hT_ready, i * ECH + j + 1)
                    pe.wait_ge(lo_ready, first + q + 1)
                    k = (DENSE + q) % SPLIT
                    hi, lo = w_hi[:, k, :], w_lo[:, k, :]
                    if kind == "down":
                        for c in range(2):
                            for nn in range(2):
                                col = slice(c * D + nn * N, c * D + (nn + 1) * N)
                                ins = product(ps[:, 6 + nn, :], hT_hi[:, 2 * u + c, 0:P], hT_lo[:, 2 * u + c, 0:P], hi[:, col], lo[:, col],
                                              j == 0 and u == 0 and c == 0, j == ECH - 1 and u == 1 and c == 1)
                    else:
                        bank = 2 * (j % 2) + (kind == "up")
                        if j >= 2 and u == 0:
                            pe.wait_ge(prod_done if kind == "up" else silu_done, i * ECH + j - 1)
                        for c in range(4):
                            col = slice(c * N, (c + 1) * N)
                            ins = product(ps[:, bank, :], xT_hi[:, 4 * u + c, 0:P], xT_lo[:, 4 * u + c, 0:P], hi[:, col], lo[:, col],
                                          u == 0 and c == 0, u == 1 and c == 3)
                    ins.then_inc(unit_used, 1)
                    if kind == "gate" and u == 1 and j >= 1:
                        turn(j - 1)
                pe.wait_ge(y_act, i + 1)
                pe.wait_ge(y_vec, i + 1)
                for n in range(4):
                    t, nn = divmod(n, 2)
                    pe.matmul(ps[:, n, :], wselT[:, t, :], ysb[:, nn * N:(nn + 1) * N], start=True, stop=True).then_inc(scatter_psum, 1)

            with pe.Fori(0, E) as i:
                expert(i)
            n_over = pe.value_load(over_i[0:1, SPARE:SPARE + 1], min_val=0, max_val=SPARE)
            for s in range(SPARE):
                with pe.If(n_over > s):
                    expert(E + s)

        @block.gpsimd
        def _(pool):
            pool.wait_ge(rel_extended, 1)
            pool.dma_start(rel_scratch, rel[:, :]).then_inc(rel_stored, 16)
            pool.wait_ge(rel_stored, 16)
            for head in range(B_HEADS):
                shifted = bass.AP(rel_scratch.tensor, head * 384 + 1, [[1, P], [1, T]])
                pool.dma_start(bias_rev[:, head, :], shifted).then_inc(bias_landed, 16)


_INS = ['x', 'positions', 'ev_norm_mix', 'ev_w_in', 'ev_g_cq', 'ev_g_ckv', 'ev_w_uq', 'ev_w_ukv',
        'ev_a_qnorm', 'ev_a_knorm', 'ev_b_qnorm', 'ev_b_knorm', 'ev_b_rel_bias', 'ev_w_out',
        'ev_norm_ff', 'ev_ff_gate', 'ev_ff_up', 'ev_ff_down',
        'od_norm_mix', 'od_w_qkv', 'od_c_qnorm', 'od_c_knorm', 'od_lam_q1', 'od_lam_k1',
        'od_lam_q2', 'od_lam_k2', 'od_c_subnorm', 'od_w_out', 'od_norm_ff', 'od_router',
        'od_ex_gate', 'od_ex_up', 'od_ex_down']


def kernel(**inputs):
    import numpy as _np
    import concourse.bacc as _bacc
    from concourse import mybir as _mybir
    from concourse.bass_utils import run_bass_kernel_spmd as _run

    nc = _bacc.Bacc("TRN2", target_bir_lowering=False, num_devices=1)
    arrays, aps = {}, {}
    for name in _INS:
        a = _np.ascontiguousarray(inputs[name])
        arrays[f"in_{name}_dram"] = a
        aps[name] = nc.dram_tensor(f"in_{name}_dram", a.shape, _mybir.dt.from_np(a.dtype), kind="ExternalInput").ap()
    out = nc.dram_tensor("out_0_dram", (1, T, D), _mybir.dt.float32, kind="ExternalOutput").ap()
    trunk(nc, aps, out)
    r = _run(nc, [arrays], core_ids=[0])
    return r.results[0]["out_0_dram"]
```

```python
import math
from contextlib import ExitStack

import numpy as np

import concourse.bass as bass
from concourse import mybir

F32 = mybir.dt.float32
F32R = mybir.dt.float32r
I32 = mybir.dt.int32
ALU = mybir.AluOpType
ACT = mybir.ActivationFunctionType
AX = mybir.AxisListType

P = 128
D = 1024
T = 256
TT = T // P
DC = D // P
CHUNK = 64
EPS = 1e-6
NEG = -1e30

A_HEADS, A_NOPE, A_ROPE, A_V, A_QL, A_KVL = 8, 64, 32, 64, 256, 128
A_QK = A_NOPE + A_ROPE
B_HEADS, B_DH, B_CLIP = 8, 64, 128
EVEN_IN = A_QL + A_KVL + A_ROPE + 3 * B_HEADS * B_DH
O_CKV = A_QL
O_KR = O_CKV + A_KVL
O_BQ = O_KR + A_ROPE
O_BK = O_BQ + B_HEADS * B_DH
O_BV = O_BK + B_HEADS * B_DH
C_HEADS, C_DH, C_ROPE = 8, 64, 16
C_MIX = C_HEADS * 2 * C_DH
C_GROUPS = 2 * C_HEADS
FF = 2752
E = 8
FE = 3584
N = 512

RAW = 7
SPLIT = 3
UNIT = 2048
FCH = -(-FF // N)
FK = -(-FF // P)
ECH = FE // N
UP_AFTER = 2
SPARE = 3
ITEMS = E + SPARE
FAR = 1024.0

G_MIX0, G_FF0, G_MIX1, G_FF1 = 0, 8, 16, 24
G_C = 32
G_AQ, G_AK, G_BQ, G_BK, G_CQ, G_CK, G_SUB = 35, 36, 37, 38, 39, 40, 41
G_ROWS = 42

FREQ = np.concatenate([
    np.float32(1.0) / (np.float32(theta) ** (np.arange(0, dim, 2, dtype=np.float32) / np.float32(dim)))
    for dim, theta in ((A_ROPE, 10000.0), (C_ROPE, 500000.0))]).astype(np.float32)
NF_A = A_ROPE // 2
NF_C = C_ROPE // 2
NF = NF_A + NF_C
TURN_1 = 6.28125
TURN_2 = float(np.float32(round((2 * math.pi - TURN_1) * 2 ** 21) / 2 ** 21))
TURN_3 = 2 * math.pi - TURN_1 - TURN_2
ROUND = 1.5 * 2 ** 23
PI_BELOW = 3.1415925
LAM_INIT = 0.8 - 0.6 * math.exp(-0.3 * 1)


def weight_stream():
    s = [("in", j, u) for j in range(UP_AFTER) for u in range(2)]
    s += [("uq", 0, 0), ("ukv", 0, 0)]
    s += [("in", j, u) for j in range(UP_AFTER, -(-EVEN_IN // N)) for u in range(2)]
    s += [("out0", 0, u) for u in range(DC // 2)]
    for j in range(FCH + 1):
        if j < FCH:
            s += [("gate", j, 0), ("gate", j, 1), ("up", j, 0), ("up", j, 1)]
        if j >= 1:
            s += [("down", j - 1, u) for u in range(-(-min(4, FK - 4 * (j - 1)) // 2))]
    s += [("qkv", j, u) for j in range(3 * C_MIX // N) for u in range(2)]
    s += [("out1", 0, u) for u in range(DC // 2)]
    return s


def expert_stream():
    s = []
    for j in range(ECH + 1):
        if j < ECH:
            s += [("gate", j, 0), ("gate", j, 1), ("up", j, 0), ("up", j, 1)]
        if j >= 1:
            s += [("down", j - 1, 0), ("down", j - 1, 1)]
    return s


STREAM = weight_stream()
DENSE = len(STREAM)
EXPERT = expert_stream()
AT = {item: n for n, item in enumerate(STREAM)}
NARROW = 4
WIDE_FROM = AT["gate", 0, 0]
LAST_TURN = EXPERT.index(("down", ECH - 2, 0))
LAST_UP = EXPERT.index(("up", ECH - 1, 1))
assert len(EXPERT) % RAW == 0 and len(EXPERT) % SPLIT == 0


def raw_of(n):
    return n % NARROW if n < WIDE_FROM else (n - WIDE_FROM) % RAW


def before(n):
    found = [m for m in range(max(0, n - RAW - NARROW), n) if raw_of(m) == raw_of(n)]
    return found[-1] if found else None


def pieces(n):
    kind, j, u = STREAM[n]
    if kind in ("in", "gate", "up", "qkv"):
        total = {"in": EVEN_IN, "gate": FF, "up": FF, "qkv": 3 * C_MIX}[kind]
        return [(P, 0, 4 * min(N, total - j * N))]
    if kind == "uq":
        return [(P, 0, 2 * A_HEADS * A_QK)]
    if kind == "ukv":
        return [(P, 0, A_HEADS * (A_NOPE + A_V))]
    k = 4 * j + 2 * u
    if kind == "down" and (k + 2) * P > FF:
        return [(P, 0, D), (FF - (k + 1) * P, D, D)]
    return [(P, 0, 2 * D)]


def landings(n):
    return sum(len(pieces(m)) for m in range(n + 1) if raw_of(m) == raw_of(n))


DENSE_LANDINGS = [sum(len(pieces(m)) for m in range(DENSE) if raw_of(m) == r) for r in range(RAW)]


def trunk(nc, w, out):
    with ExitStack() as ctx:
        ctx.enter_context(nc.allow_non_contiguous_dma(reason="short gain, position and router loads"))

        def sb(name, shape, dt=F32):
            return ctx.enter_context(nc.sbuf_tensor(name, shape, dt))

        def sem(name):
            return ctx.enter_context(nc.semaphore(name))

        raw = sb("raw", [P, RAW, UNIT])
        w_hi = sb("w_hi", [P, SPLIT, UNIT], F32R)
        w_lo = sb("w_lo", [P, SPLIT, UNIT], F32R)
        h = sb("h", [P, TT, D])
        xT_hi = sb("xT_hi", [P, DC, T], F32R)
        xT_lo = sb("xT_lo", [P, DC, T], F32R)
        hT_hi = sb("hT_hi", [P, 4, T], F32R)
        hT_lo = sb("hT_lo", [P, 4, T], F32R)
        xs = sb("xs", [P, TT, D])
        ident = sb("ident", [P, P])
        tri = sb("tri", [P, P])
        ones = sb("ones", [P, P])
        slots_f = sb("slots_f", [P, P])
        mask = sb("mask", [P, 384])
        eps = sb("eps", [P, 1])
        unread = sb("unread", [P, 1])
        freq = sb("freq", [P, NF])
        gain_rows = sb("gain_rows", [G_ROWS, P])
        gcol = sb("gcol", [P, G_ROWS])
        ga_rot = sb("ga_rot", [P, 2, A_ROPE])
        gc_rot = sb("gc_rot", [P, 2, C_ROPE])
        lamv = sb("lamv", [P, 4, C_DH])
        lams = sb("lams", [P, 8])
        pos_i = sb("pos_i", [P, TT], I32)
        pos_f = sb("pos_f", [P, TT])
        router = sb("router", [P, DC, E])
        router_hi = sb("router_hi", [P, DC, E], F32R)
        router_lo = sb("router_lo", [P, DC, E], F32R)
        trig = sb("trig", [P, 2, TT, NF])
        turns = sb("turns", [P, 2, TT, NF])
        angle = sb("angle", [P, TT, NF])
        ssq = sb("ssq", [P, 8])
        root = sb("root", [P, 8])
        rstd = sb("rstd", [P, 8])
        ss = sb("ss", [P, 80])
        rs = sb("rs", [P, 80])
        negmax = sb("negmax", [P, 2 * C_HEADS, TT])
        psum_l = sb("psum_l", [P, 2 * C_HEADS, TT])
        rinv = sb("rinv", [P, 2 * C_HEADS, TT])
        coef = sb("coef", [P, C_HEADS, TT])
        gate_s = sb("gate_s", [P, 12, TT])
        rank = sb("rank", [P, TT, ITEMS + 1])
        comb = sb("comb", [P, TT, ITEMS + 1])
        load8 = sb("load8", [P, 9, E])
        over_s = sb("over_s", [P, 12])
        over_i = sb("over_i", [P, 4], I32)
        WORK = 13760
        work = sb("work", [P, WORK])

        def carve(base, at, *dims):
            n = math.prod(dims)
            assert at + n <= base.shape[1]
            v = base[:, at:at + n]
            names = "abc"[:len(dims)]
            if len(dims) == 1:
                return v
            return v.rearrange(f"p ({' '.join(names)}) -> p {' '.join(names)}",
                               **{k: d for k, d in zip(names[1:], dims[1:])})

        tail = raw[:, NARROW:RAW, :].rearrange("p a b -> p (a b)")
        u0 = carve(work, 0, TT, EVEN_IN)
        qa = carve(work, 3904, TT, A_HEADS * A_QK)
        kva = carve(work, 5440, TT, A_HEADS * (A_NOPE + A_V))
        ka = carve(work, 7488, TT, A_HEADS * A_QK)
        bias = carve(work, 9024, B_HEADS, T)
        S0 = 7
        s0 = carve(work, 11072, S0, 384)
        qta, kta = carve(tail, 0, A_HEADS, T), carve(tail, 2048, A_HEADS, T)
        qtb, ktb = carve(tail, 4096, B_HEADS // 2, T), carve(tail, 5120, B_HEADS // 2, T)
        pt0 = carve(work, 7488, 2, 384)
        bias_rev = carve(tail, 0, B_HEADS, T)
        rel = carve(work, 5440, 384)[0:B_HEADS, :]
        sq_c = carve(work, 11072, TT, O_BQ)
        sq_b = carve(work, 11072, TT, 2 * B_HEADS * B_DH)
        sqa = carve(work, 11072, TT * A_HEADS, A_QK)
        sqk = carve(work, 11072 + 1536, TT, A_HEADS, A_NOPE)
        xs_flat = xs[:, :, :].rearrange("p a b -> p (a b)")
        rot_a = [carve(xs_flat, 256 * n, TT, A_HEADS, NF_A) for n in range(4)]
        rot_k = [carve(xs_flat, 1024 + 64 * n, TT, NF_A) for n in range(4)]
        rot_c = [carve(xs_flat, 256 * n, TT, C_GROUPS, NF_C) for n in range(4)]
        kr = carve(xs_flat, 1280, TT, A_ROPE)
        slots_i = work[:, 11072:11072 + P].bitcast(I32)
        u1 = carve(work, 0, TT, 3 * C_MIX)
        qtc, ktc = carve(work, 6144, C_HEADS, T), carve(work, 8192, C_HEADS, T)
        sqc = carve(work, 6144, TT, 2 * C_MIX)
        S1 = 8
        s1 = carve(work, 10240, S1, 384)
        sqo = u1[:, :, 0:C_MIX]
        pt1 = carve(work, C_MIX, 2, 384)
        sil = carve(work, 8192, 2, N)
        prod = carve(work, 9216, 2, N)
        scaled = carve(work, 12288, 2, N)
        logits_T = carve(work, 0, T)[0:E, :]
        gate_t = carve(work, T, 16, TT, E)
        sel = carve(work, 1024, TT, P)
        wsel = carve(work, 1280, TT, P)
        wselT = carve(work, 1536, TT, P)
        ysb = carve(work, 2816, D)

        ps = ctx.enter_context(nc.psum_tensor("ps", [P, 8, N], F32))

        rel_scratch = nc.dram_tensor("rel_scratch", (B_HEADS, 384), F32, kind="Internal").ap()
        w_in = w["ev_w_in"][0].rearrange("(k p) n -> p k n", p=P)
        w_uq = w["ev_w_uq"][0].rearrange("(k p) h d -> p k (h d)", p=P)
        w_ukv = w["ev_w_ukv"][0].rearrange("p h d -> p (h d)")
        w_out0 = w["ev_w_out"][0].rearrange("(k p) n -> p k n", p=P)
        w_out1 = w["od_w_out"][0].rearrange("(k p) n -> p k n", p=P)
        ff_gate = w["ev_ff_gate"][0].rearrange("(k p) n -> p k n", p=P)
        ff_up = w["ev_ff_up"][0].rearrange("(k p) n -> p k n", p=P)
        ff_down = w["ev_ff_down"][0]
        w_qkv = w["od_w_qkv"][0].rearrange("(k p) n -> p k n", p=P)
        ex_gate = w["od_ex_gate"][0].rearrange("e (k p) n -> e p k n", p=P)
        ex_up = w["od_ex_up"][0].rearrange("e (k p) n -> e p k n", p=P)
        ex_down = w["od_ex_down"][0].rearrange("e (k p) n -> e p k n", p=P)

        landed = [sem(f"landed{r}") for r in range(RAW)]
        hi_ready = sem("hi_ready")
        lo_ready = sem("lo_ready")
        unit_used = sem("unit_used")
        scaled_ready = sem("scaled_ready")
        parts_hi = sem("parts_hi")
        x_landed = [sem("x_landed0"), sem("x_landed1")]
        pos_landed = sem("pos_landed")
        gains_landed = sem("gains_landed")
        rows_landed = sem("rows_landed")
        rel_landed = sem("rel_landed")
        rel_extended = sem("rel_extended")
        rel_stored = sem("rel_stored")
        bias_landed = sem("bias_landed")
        pool_chain = sem("pool_chain")
        gain_ones = sem("gain_ones")
        consts_ready = sem("consts_ready")
        gains_turned = sem("gains_turned")
        gains_ready = sem("gains_ready")
        vec_chain = sem("vec_chain")
        act_chain = sem("act_chain")
        angles_ready = sem("angles_ready")
        trig_ready = sem("trig_ready")
        root_ready = sem("root_ready")
        xs_ready = sem("xs_ready")
        xT_psum = sem("xT_psum")
        xT_ready = sem("xT_ready")
        proj_act = [sem("proj_act0"), sem("proj_act1")]
        proj_vec = [sem("proj_vec0"), sem("proj_vec1")]
        u_squared = sem("u_squared")
        u_sums = sem("u_sums")
        u_roots = sem("u_roots")
        c_normed = sem("c_normed")
        c_psum = sem("c_psum")
        c_ready = sem("c_ready")
        up_act = sem("up_act")
        up_vec = sem("up_vec")
        a_squared = sem("a_squared")
        a_sums = sem("a_sums")
        a_roots = sem("a_roots")
        qk_normed = sem("qk_normed")
        qk_psum = sem("qk_psum")
        q_turned = sem("q_turned")
        k_turned = sem("k_turned")
        scores_psum = sem("scores_psum")
        scores_read = sem("scores_read")
        max_ready = sem("max_ready")
        exp_done = sem("exp_done")
        diff_done = sem("diff_done")
        p_psum = sem("p_psum")
        p_turned = sem("p_turned")
        pv_done = sem("pv_done")
        outputs_ready = sem("outputs_ready")
        y_ready = sem("y_ready")
        yT_psum = sem("yT_psum")
        yT_hi = sem("yT_hi")
        yT_ready = sem("yT_ready")
        router_split = sem("router_split")
        h_ready = sem("h_ready")
        lam_sums = sem("lam_sums")
        lam_exps = sem("lam_exps")
        o_squared = sem("o_squared")
        o_sums = sem("o_sums")
        o_roots = sem("o_roots")
        ff_silu = sem("ff_silu")
        ff_prod = sem("ff_prod")
        ff_turned = sem("ff_turned")
        ff_hT_hi = sem("ff_hT_hi")
        ff_hT = sem("ff_hT")
        logits_psum = sem("logits_psum")
        gate_diff = sem("gate_diff")
        gate_exp = sem("gate_exp")
        chosen_ready = sem("chosen_ready")
        logits_copied = sem("logits_copied")
        rank_psum = sem("rank_psum")
        routed = sem("routed")
        sel_ready = sem("sel_ready")
        wselT_psum = sem("wselT_psum")
        wselT_ready = sem("wselT_ready")
        gather_psum = sem("gather_psum")
        xg_ready = sem("xg_ready")
        silu_done = sem("silu_done")
        prod_done = sem("prod_done")
        turn_done = sem("turn_done")
        hT_part = sem("hT_part")
        hT_ready = sem("hT_ready")
        y_act = sem("y_act")
        y_vec = sem("y_vec")
        scatter_psum = sem("scatter_psum")
        scatter_read = sem("scatter_read")
        stored = sem("stored")

        SCORE_BANKS = (0, 1, 6, 7)
        DIFF_LAG, TURN_LAG, VALUE_LAG = 2, 3, 5

        def part_groups(x, m):
            return x[:, 0:TT * 2 * C_GROUPS].rearrange("p (t g) -> p t g", t=TT)[:, :, m * C_GROUPS:(m + 1) * C_GROUPS]

        def side(j):
            return slice(j % 2 * P, (j % 2 + 1) * P)

        def half_heads(x, half):
            return x[:, 0:TT * C_HEADS].rearrange("p (t g) -> p t g", t=TT)[:, :, half * C_HEADS // 2:(half + 1) * C_HEADS // 2]

        def score_bank(unit):
            return SCORE_BANKS[unit % len(SCORE_BANKS)]

        def output_bank(layer, n):
            per, width = (2, 2 * C_DH) if layer else (4, A_V)
            return 4 + n // per % 2, [t * per * width + n % per * width for t in range(TT)]

        n_gains = 17
        n_rows = 9
        IN_J = -(-EVEN_IN // N)
        QKV_J = 3 * C_MIX // N

        def cols(j, total):
            return j * N, min(N, total - j * N)

        def blocks(bank, n=4):
            return ps[:, bank, 0:n * P].rearrange("p (a b) -> p a b", b=P)

        def gains(first, n, width):
            return gcol[:, first:first + n].unsqueeze(2).to_broadcast([P, n, width])

        def cT(x, t):
            return x[:, 0:3, t * P:(t + 1) * P]

        block = ctx.enter_context(nc.Block())

        @block.sync
        def _(sp):
            for t in range(TT):
                sp.dma_start(h[:, t, :], w["x"][0, t * P:(t + 1) * P, :]).then_inc(x_landed[t], 16)
            sp.wait_ge(gain_ones, 1)
            for first, name in ((G_MIX0, "ev_norm_mix"), (G_FF0, "ev_norm_ff"), (G_MIX1, "od_norm_mix"), (G_FF1, "od_norm_ff")):
                sp.dma_start(gain_rows[first:first + DC, :], w[name][0].rearrange("(k p) -> k p", p=P)).then_inc(gains_landed, 16)
            sp.dma_start(gain_rows[G_C:G_C + 2, :], w["ev_g_cq"][0].rearrange("(k p) -> k p", p=P)).then_inc(gains_landed, 16)
            sp.dma_start(gain_rows[G_C + 2:G_C + 3, :], w["ev_g_ckv"]).then_inc(gains_landed, 16)
            sp.dma_start(gain_rows[G_SUB:G_SUB + 1, :], w["od_c_subnorm"]).then_inc(gains_landed, 16)

            def head_gains():
                for row, name in ((G_AQ, "ev_a_qnorm"), (G_AK, "ev_a_knorm")):
                    sp.dma_start(gain_rows[row:row + 1, 0:A_NOPE], w[name][:, 0:A_NOPE]).then_inc(gains_landed, 16)
                for row, name in ((G_BQ, "ev_b_qnorm"), (G_BK, "ev_b_knorm")):
                    for m in range(2):
                        sp.dma_start(gain_rows[row:row + 1, m * B_DH:(m + 1) * B_DH], w[name]).then_inc(gains_landed, 16)
                for row, name in ((G_CQ, "od_c_qnorm"), (G_CK, "od_c_knorm")):
                    for m in range(2):
                        sp.dma_start(gain_rows[row:row + 1, m * C_DH + C_ROPE:(m + 1) * C_DH], w[name][:, C_ROPE:C_DH]).then_inc(gains_landed, 16)

            def rows(n):
                kind, j, u = STREAM[n]
                if kind in ("in", "gate", "up", "qkv"):
                    src, total = {"in": (w_in, EVEN_IN), "gate": (ff_gate, FF), "up": (ff_up, FF),
                                  "qkv": (w_qkv, 3 * C_MIX)}[kind]
                    a, m = cols(j, total)
                    return [src[:, 4 * u:4 * u + 4, a:a + m]]
                if kind == "uq":
                    return [w_uq]
                if kind == "ukv":
                    return [w_ukv.unsqueeze(1)]
                if kind in ("out0", "out1"):
                    return [(w_out0 if kind == "out0" else w_out1)[:, 2 * u:2 * u + 2, :]]
                k = 4 * j + 2 * u
                if len(pieces(n)) == 2:
                    return [ff_down[k * P:(k + 1) * P, :].unsqueeze(1), ff_down[(k + 1) * P:FF, :].unsqueeze(1)]
                return [ff_down[k * P:(k + 2) * P, :].rearrange("(k p) n -> p k n", p=P)]

            for n in range(DENSE):
                if n == 1:
                    head_gains()
                if before(n) is not None:
                    sp.wait_ge(lo_ready, before(n) + 1)
                elif raw_of(n) >= NARROW:
                    sp.wait_ge(pv_done, A_HEADS + B_HEADS)
                for (r, a, m), src in zip(pieces(n), rows(n)):
                    k = src.shape[1]
                    dst = raw[0:r, raw_of(n), a:a + m].rearrange("p (k n) -> p k n", k=k)
                    sp.dma_start(dst, src).then_inc(landed[raw_of(n)], 16)

            def load_expert(i, e):
                for q, (kind, j, u) in enumerate(EXPERT):
                    sp.wait_ge(lo_ready, i * len(EXPERT) + DENSE + q - RAW + 1)
                    one = bass.ds(e, 1)
                    if kind == "down":
                        src = ex_down[one, :, 4 * j + 2 * u:4 * j + 2 * u + 2, :]
                    else:
                        src = (ex_gate if kind == "gate" else ex_up)[one, :, 4 * u:4 * u + 4, j * N:(j + 1) * N]
                    r = raw_of(DENSE + q)
                    dst = raw[:, r, :].rearrange("p (k n) -> p k n", k=2 if kind == "down" else 4)
                    sp.dma_start(dst, src.rearrange("e p k n -> p (e k) n")).then_inc(landed[r], 16)

            load_expert(0, 0)
            with sp.Fori(1, E) as i:
                load_expert(i, i)
            sp.wait_ge(routed, 1)
            n_over = sp.value_load(over_i[0:1, SPARE:SPARE + 1], min_val=0, max_val=SPARE)
            for s in range(SPARE):
                with sp.If(n_over > s):
                    e = sp.value_load(over_i[0:1, s:s + 1], min_val=0, max_val=E - 1)
                    load_expert(E + s, e)
            for t in range(TT):
                sp.wait_ge(scatter_read, 4 * (n_over + E) - 2 * (TT - 1 - t))
                sp.dma_start(out[0, t * P:(t + 1) * P, :], h[:, t, :]).then_inc(stored, 16)
            sp.wait_ge(stored, 16 * TT)

        @block.gpsimd
        def _(pool):
            pool.memset(gain_rows[:, :], 1.0).then_inc(gain_ones, 1)
            pool.memset(eps[:, :], EPS).then_inc(consts_ready, 1)
            pool.memset(ident[:, :], 0.0).then_inc(pool_chain, 1)
            pool.memset(tri[:, :], 1.0).then_inc(pool_chain, 1)
            pool.memset(mask[:, :], 0.0).then_inc(pool_chain, 1)
            pool.wait_ge(pool_chain, 3)
            pool.affine_select(out=ident[:, :], in_=ident[:, :], compare_op=ALU.not_equal, fill=1.0,
                               base=0, pattern=[[-1, P]], channel_multiplier=1).then_inc(consts_ready, 1)
            pool.affine_select(out=tri[:, :], in_=tri[:, :], compare_op=ALU.is_gt, fill=0.0,
                               base=0, pattern=[[1, P]], channel_multiplier=-1).then_inc(consts_ready, 1)
            pool.memset(mask[0:CHUNK, CHUNK:P], NEG).then_inc(consts_ready, 1)
            pool.memset(mask[0:CHUNK, 384 - CHUNK:384], NEG).then_inc(consts_ready, 1)
            pool.memset(ones[:, :], 1.0).then_inc(consts_ready, 1)
            for f in range(NF):
                pool.memset(freq[:, f:f + 1], float(FREQ[f])).then_inc(consts_ready, 1)
            pool.iota(slots_i[:, :], pattern=[[1, P]], base=0, channel_multiplier=0).then_inc(consts_ready, 1)

        n_consts = 6 + NF + 1

        @block.scalar
        def _(act):
            chain = [0]

            def link(ins):
                chain[0] += 1
                ins.then_inc(act_chain, 1)
                act.wait_ge(act_chain, chain[0])

            act.dma_start(pos_i[:, :], w["positions"][0].rearrange("(t p) -> p t", p=P)).then_inc(pos_landed, 16)
            act.dma_start(rel[:, 0:2 * B_CLIP + 1], w["ev_b_rel_bias"][0]).then_inc(rel_landed, 16)

            def load_rows():
                for m, name in enumerate(("ev_a_qnorm", "ev_a_knorm")):
                    act.dma_start(ga_rot[:, m, :], w[name][0, A_NOPE:A_QK].partition_broadcast(P)).then_inc(rows_landed, 16)
                for m, name in enumerate(("od_c_qnorm", "od_c_knorm")):
                    act.dma_start(gc_rot[:, m, :], w[name][0, 0:C_ROPE].partition_broadcast(P)).then_inc(rows_landed, 16)
                for m, name in enumerate(("od_lam_q1", "od_lam_k1", "od_lam_q2", "od_lam_k2")):
                    act.dma_start(lamv[:, m, :], w[name][0].partition_broadcast(P)).then_inc(rows_landed, 16)
                act.dma_start(router[:, :, :], w["od_router"][0].rearrange("(k p) e -> p k e", p=P)).then_inc(rows_landed, 16)

            done = [0]

            def split_to(end):
                for n in range(done[0], min(end, DENSE)):
                    act.wait_ge(landed[raw_of(n)], 16 * landings(n))
                    if n >= SPLIT:
                        act.wait_ge(unit_used, n - SPLIT + 1)
                    for r, a, m in pieces(n):
                        ins = act.activation(w_hi[0:r, n % SPLIT, a:a + m], raw[0:r, raw_of(n), a:a + m], ACT.Copy)
                    ins.then_inc(hi_ready, 1)
                done[0] = max(done[0], end)

            def parts(c, dst, n=N):
                act.wait_ge(scaled_ready, c + 1)
                act.activation(dst, scaled[:, c % 2, 0:n].rearrange("p (a b) -> p a b", b=P), ACT.Copy).then_inc(parts_hi, 1)

            def norm_parts(k, c):
                for f in range(4):
                    t, half = divmod(f, 2)
                    parts(c + f, xT_hi[:, 4 * half:4 * half + 4, t * P:(t + 1) * P])

            def load_root_table():
                act.activation(unread[:, :], eps[:, :], ACT.Sqrt)

            def norm_roots(k):
                if k:
                    load_root_table()
                for t in range(TT):
                    if k == 0:
                        act.wait_ge(x_landed[t], 16)
                        act.wait_ge(consts_ready, 1)
                    else:
                        act.wait_ge(h_ready, 4 * (k - 1) + 2 * (t + 1))
                    if k:
                        act.wait_ge(xT_psum, 4 * k)
                    link(act.activation(xs[:, t, :], h[:, t, :], ACT.Square, accum_out=ssq[:, 2 * k + t:2 * k + t + 1]))
                    act.activation(root[:, 2 * k + t:2 * k + t + 1], ssq[:, 2 * k + t:2 * k + t + 1], ACT.Sqrt,
                                   scale=1.0 / D, bias=eps[:, 0:1]).then_inc(root_ready, 1)

            def project(kind, layer, u, total, chunks):
                for j in chunks:
                    a, m = cols(j, total)
                    n = AT[kind, j, 1]
                    split_to(n + SPLIT + 1 if kind != "in" else min(n + SPLIT + 1, AT["out0", 0, 0]))
                    act.wait_ge(unit_used, n + 1)
                    act.activation(u[:, 0, a:a + m], ps[:, 4 + 2 * (j % 2), 0:m], ACT.Copy).then_inc(proj_act[layer], 1)

            def turn_q(f, dst, rows, col):
                act.wait_ge(qk_psum, f + 1)
                act.activation(dst, blocks(f % 4)[0:rows], ACT.Copy, scale=gcol[0:rows, col:col + 1]).then_inc(q_turned, 1)

            def exponentials(u, unit, s, slot):
                act.wait_ge(max_ready, unit + 1)
                act.activation(s[:, slot, 0:P], s[:, slot, 0:P], ACT.Exp,
                               bias=negmax[:, u, 0:1], accum_out=psum_l[:, u, 0:1])
                act.activation(s[:, slot, P:384], s[:, slot, P:384], ACT.Exp,
                               bias=negmax[:, u, 1:2], accum_out=psum_l[:, u, 1:2]).then_inc(exp_done, 1)

            def turn_p(head, pt):
                act.wait_ge(p_psum, head + 1)
                if head >= 2:
                    act.wait_ge(pv_done, head - 1)
                act.activation(pt[:, head % 2, :], ps[:, 2 + head % 2, 0:384], ACT.Copy).then_inc(p_turned, 1)

            def turn_y(layer, half):
                for t in range(TT):
                    f = 2 * half + t
                    act.wait_ge(yT_psum, 4 * layer + f + 1)
                    scale = 1.0 if layer == 0 else gcol[:, G_SUB:G_SUB + 1]
                    act.activation(xT_hi[:, 4 * half:4 * half + 4, t * P:(t + 1) * P], blocks(f), ACT.Copy,
                                   scale=scale).then_inc(yT_hi, 1)

            norm_roots(0)
            split_to(1)
            norm_parts(0, 0)
            split_to(SPLIT)
            load_rows()
            act.wait_ge(rows_landed, 16 * n_rows)
            act.activation(router_hi[:, :, :], router[:, :, :], ACT.Copy).then_inc(router_split, 1)
            act.wait_ge(angles_ready, 1)
            act.activation(trig[:, :, :, :], turns[:, :, :, :], ACT.Sin).then_inc(trig_ready, 1)
            project("in", 0, u0, EVEN_IN, [0])
            act.wait_ge(proj_vec[0], 1)
            act.wait_ge(proj_act[0], 1)
            act.activation(sq_c, u0[:, :, 0:O_BQ], ACT.Square).then_inc(u_squared, 1)
            act.wait_ge(u_sums, 1)
            act.activation(rs[:, 0:2], ss[:, 0:2], ACT.Sqrt, scale=1.0 / A_QL, bias=eps[:, 0:1])
            act.activation(rs[:, 2:4], ss[:, 2:4], ACT.Sqrt, scale=1.0 / A_KVL, bias=eps[:, 0:1])
            act.activation(rs[:, 4:6], ss[:, 4:6], ACT.Sqrt, scale=1.0 / A_ROPE, bias=eps[:, 0:1]).then_inc(u_roots, 1)
            for t in range(TT):
                parts(4 + t, cT(hT_hi, t), 3 * P)
            project("in", 0, u0, EVEN_IN, range(1, UP_AFTER))
            act.wait_ge(unit_used, AT["uq", 0, 0] + 1)
            for t in range(TT):
                for m, (a, n) in enumerate(((0, 512), (512, 256))):
                    act.activation(qa[:, t, a:a + n], ps[:, 2 * t + m, 0:n], ACT.Copy).then_inc(up_act, 1)
            split_to(AT["ukv", 0, 0] + SPLIT + 1)
            act.wait_ge(up_act, 4)
            act.wait_ge(up_vec, 4)
            act.activation(sqa, qa.rearrange("p t (g d) -> p (t g) d", d=A_QK), ACT.Square)
            act.activation(sqk, kva.rearrange("p t (g d) -> p t g d", d=A_NOPE + A_V)[:, :, :, 0:A_NOPE],
                           ACT.Square).then_inc(a_squared, 1)
            split_to(AT["in", UP_AFTER, 0] + SPLIT + 1)
            act.wait_ge(a_sums, 1)
            act.activation(rs[:, 0:32], ss[:, 0:32], ACT.Sqrt, scale=1.0 / A_NOPE, bias=eps[:, 0:1])
            act.activation(rs[:, 32:48], ss[:, 32:48], ACT.Sqrt, scale=1.0 / A_ROPE, bias=eps[:, 0:1]).then_inc(a_roots, 1)
            project("in", 0, u0, EVEN_IN, [UP_AFTER])
            act.wait_ge(proj_vec[0], UP_AFTER + 1)
            act.wait_ge(proj_act[0], UP_AFTER + 1)
            act.activation(sq_b, u0[:, :, O_BQ:O_BV], ACT.Square).then_inc(u_squared, 1)
            act.wait_ge(u_sums, 2)
            act.activation(rs[:, 48:80], ss[:, 48:80], ACT.Sqrt, scale=1.0 / B_DH, bias=eps[:, 0:1]).then_inc(u_roots, 1)
            project("in", 0, u0, EVEN_IN, range(UP_AFTER + 1, IN_J))
            for t in range(TT):
                for half in range(2):
                    turn_q(4 * t + 2 * half, qta[0:A_QK, 4 * half:4 * half + 4, t * P:(t + 1) * P], A_QK, G_AQ)
            for t in range(TT):
                turn_q(8 + 2 * t, qtb[:, :, t * P:(t + 1) * P], P, G_BQ)
            act.wait_ge(lam_sums, 1)
            act.activation(lams[:, 2:4], lams[:, 0:2], ACT.Exp).then_inc(lam_exps, 1)
            out0 = AT["out0", 0, 0]
            for i in range(A_HEADS + B_HEADS + TURN_LAG):
                if i in (4, 7, 10):
                    split_to(out0 + i // 3)
                if i < A_HEADS + B_HEADS:
                    exponentials(i, i, s0, i % S0)
                if i >= TURN_LAG:
                    turn_p(i - TURN_LAG, pt0)
            turn_y(0, 0)
            turn_y(0, 1)

            split_to(WIDE_FROM + SPLIT - 1)
            norm_roots(1)
            norm_parts(1, 6)
            split_to(WIDE_FROM + SPLIT)
            for j in range(FCH + 1):
                for t in range(TT):
                    if j < FCH:
                        split_to(AT["gate", j, t] + SPLIT + 1)
                    if j >= 1:
                        m = cols(j - 1, FF)[1]
                        whole, s = m // P, TT * (j - 1) + t
                        act.wait_ge(ff_turned, s + 1)
                        if m % P:
                            act.activation(hT_hi[0:m % P, whole, t * P:(t + 1) * P], ps[0:m % P, 3, whole * P:(whole + 1) * P], ACT.Copy)
                        act.activation(hT_hi[:, 0:whole, t * P:(t + 1) * P], blocks(3, whole), ACT.Copy).then_inc(ff_hT_hi, 1)
                if j < FCH:
                    m = cols(j, FF)[1]
                    act.wait_ge(unit_used, AT["gate", j, 1] + 1)
                    for t in range(TT):
                        if j >= 1:
                            act.wait_ge(ff_prod, TT * (j - 1) + t + 1)
                        act.activation(sil[:, t, 0:m], ps[:, (4 * j + t) % 3, 0:m], ACT.Silu).then_inc(ff_silu, 1)
                    split_to(AT["up", j, 1] + SPLIT + 1)
            last_down = AT["qkv", 0, 0] - 1
            split_to(last_down + SPLIT)

            norm_roots(2)
            split_to(last_down + SPLIT + 1)
            norm_parts(2, 10)
            for m in range(2):
                project("qkv", 1, u1, 3 * C_MIX, range(2 * m, 2 * m + 2))
                act.wait_ge(proj_vec[1], 2 * m + 2)
                act.wait_ge(proj_act[1], 2 * m + 2)
                act.activation(sqc[:, :, m * C_MIX:(m + 1) * C_MIX], u1[:, :, m * C_MIX:(m + 1) * C_MIX],
                               ACT.Square).then_inc(u_squared, 1)
                act.wait_ge(u_sums, 2 + m + 1)
                act.activation(part_groups(rs, m), part_groups(ss, m), ACT.Sqrt, scale=1.0 / C_DH, bias=eps[:, 0:1]).then_inc(u_roots, 1)
            project("qkv", 1, u1, 3 * C_MIX, range(4, QKV_J))
            for t in range(TT):
                for half in range(2):
                    turn_q(12 + 4 * t + 2 * half, qtc[:, 4 * half:4 * half + 4, t * P:(t + 1) * P], P, G_CQ)
            def square_outputs(half):
                act.wait_ge(outputs_ready, 4 + 2 * half + 2)
                act.activation(sqo[:, :, half * N:(half + 1) * N], xs[:, :, half * N:(half + 1) * N], ACT.Square).then_inc(o_squared, 1)

            def output_roots(half):
                act.wait_ge(o_sums, half + 1)
                act.activation(half_heads(rs, half), half_heads(ss, half), ACT.Sqrt, scale=1.0 / (2 * C_DH), bias=eps[:, 0:1]).then_inc(o_roots, 1)

            for i in range(C_HEADS + TURN_LAG):
                if i < C_HEADS:
                    for m in range(2):
                        exponentials(2 * i + m, A_HEADS + B_HEADS + 2 * i + m, s1, (2 * i + m) % S1)
                if i == C_HEADS:
                    load_root_table()
                if i == C_HEADS + 1:
                    square_outputs(0)
                if i >= TURN_LAG:
                    turn_p(A_HEADS + B_HEADS + i - TURN_LAG, pt1)
            output_roots(0)
            turn_y(1, 0)
            square_outputs(1)
            output_roots(1)
            turn_y(1, 1)
            split_to(DENSE)

            def split_unit(i, q):
                r = raw_of(DENSE + q)
                act.wait_ge(landed[r], i * (16 * len(EXPERT) // RAW) + 16 * (DENSE_LANDINGS[r] + q // RAW + 1))
                act.wait_ge(unit_used, i * len(EXPERT) + DENSE + q - SPLIT + 1)
                act.activation(w_hi[:, (DENSE + q) % SPLIT, :], raw[:, r, :], ACT.Copy).then_inc(hi_ready, 1)

            def gathered(i):
                for half in range(2):
                    act.wait_ge(scaled_ready, 2 * i + 18 + half + 1)
                    act.activation(xT_hi[:, 4 * half:4 * half + 4, 0:P], scaled[:, half, :].rearrange("p (a b) -> p a b", b=P),
                                   ACT.Copy).then_inc(parts_hi, 1)

            def outputs(i):
                act.wait_ge(unit_used, i * len(EXPERT) + DENSE)
                act.activation(ysb[:, 0:N], ps[:, 6, :], ACT.Copy).then_inc(y_act, 1)

            def hidden_turned(i, m):
                act.wait_ge(turn_done, i * ECH + m + 1)
                act.activation(hT_hi[:, :, side(m)], blocks(4 + m % 2), ACT.Copy).then_inc(hT_part, 1)

            def expert(i, first_item=False):
                first = i * len(EXPERT) + DENSE
                if not first_item:
                    for q in range(SPLIT):
                        split_unit(i, q)
                    outputs(i)
                for q, (kind, j, u) in enumerate(EXPERT):
                    if q == LAST_TURN:
                        hidden_turned(i, ECH - 1)
                    if q + SPLIT < len(EXPERT):
                        split_unit(i, q + SPLIT)
                    if kind == "gate" and u == 1:
                        if j >= 2:
                            act.wait_ge(prod_done, i * ECH + j - 1)
                        act.wait_ge(unit_used, first + q + 1)
                        act.activation(sil[:, j % 2, :], ps[:, 2 * (j % 2), :], ACT.Silu).then_inc(silu_done, 1)
                    if q == LAST_UP:
                        act.wait_ge(wselT_psum, i + 1)
                        act.activation(wselT, blocks(4, 2), ACT.Copy).then_inc(wselT_ready, 1)
                        gathered(i + 1)
                    if kind == "gate" and u == 1 and j >= 1:
                        hidden_turned(i, j - 1)

            for q in range(SPLIT - 1):
                split_unit(0, q)
            norm_roots(3)
            split_unit(0, SPLIT - 1)
            norm_parts(3, 14)
            act.wait_ge(gate_diff, 1)
            act.activation(gate_s[:, 5, :], gate_s[:, 4, :], ACT.Exp).then_inc(gate_exp, 1)
            gathered(0)
            expert(0, True)
            with act.Fori(1, E) as i:
                expert(i)
            act.wait_ge(routed, 1)
            n_over = act.value_load(over_i[0:1, SPARE:SPARE + 1], min_val=0, max_val=SPARE)
            for s in range(SPARE):
                with act.If(n_over > s):
                    expert(E + s)
            outputs(n_over + E)

        @block.vector
        def _(dve):
            chain = [0]

            def link(ins):
                chain[0] += 1
                ins.then_inc(vec_chain, 1)
                dve.wait_ge(vec_chain, chain[0])

            done = [0]

            def split_to(end):
                for n in range(done[0], min(end, DENSE)):
                    dve.wait_ge(hi_ready, n + 1)
                    for r, a, m in pieces(n):
                        ins = dve.tensor_tensor(w_lo[0:r, n % SPLIT, a:a + m], raw[0:r, raw_of(n), a:a + m],
                                                w_hi[0:r, n % SPLIT, a:a + m].bitcast(F32), ALU.subtract)
                    ins.then_inc(lo_ready, 1)
                done[0] = max(done[0], end)

            def scale(c, bank, n, first):
                dve.tensor_tensor(scaled[:, c % 2, 0:n * P].rearrange("p (a b) -> p a b", b=P), blocks(bank, n),
                                  gains(first, n, P), ALU.mult).then_inc(scaled_ready, 1)

            def low_part(c, lo, hi, n=4):
                dve.wait_ge(scaled_ready, c + 1)
                dve.wait_ge(parts_hi, c + 1)
                return dve.tensor_tensor(lo, scaled[:, c % 2, 0:n * P].rearrange("p (a b) -> p a b", b=P),
                                         hi.bitcast(F32), ALU.subtract)

            def norm_apply(k, first, c):
                for t in range(TT):
                    col = slice(2 * k + t, 2 * k + t + 1)
                    dve.wait_ge(root_ready, 2 * k + t + 1)
                    link(dve.reciprocal(rstd[:, col], root[:, col]))
                    dve.tensor_scalar(xs[:, t, :], h[:, t, :], rstd[:, col], None, ALU.mult).then_inc(xs_ready, 1)
                if k == 0:
                    split_to(1)
                    turn_gains()
                for f in range(5):
                    if f < 4:
                        dve.wait_ge(xT_psum, 4 * k + f + 1)
                        if f >= 2:
                            dve.wait_ge(xT_ready, 4 * k + f - 1)
                        scale(c + f, f, 4, first + 4 * (f % 2))
                    if f >= 1:
                        t, half = divmod(f - 1, 2)
                        v = (slice(None), slice(4 * half, 4 * half + 4), slice(t * P, (t + 1) * P))
                        low_part(c + f - 1, xT_lo[v], xT_hi[v]).then_inc(xT_ready, 1)

            def turn_gains():
                dve.wait_ge(gains_turned, 1)
                dve.tensor_copy(gcol[:, :], ps[:, 7, 0:G_ROWS]).then_inc(gains_ready, 1)
                dve.wait_ge(gains_ready, 1)
                dve.tensor_scalar(gcol[:, G_SUB:G_SUB + 1], gcol[:, G_SUB:G_SUB + 1], 1.0 - LAM_INIT, None,
                                  ALU.mult).then_inc(gains_ready, 1)

            def project(kind, layer, u, total, chunks):
                for j in chunks:
                    n = AT[kind, j, 1]
                    split_to(n + SPLIT + 1 if kind != "in" else min(n + SPLIT + 1, AT["out0", 0, 0]))
                    copy_out(kind, layer, u, total, j)

            def copy_out(kind, layer, u, total, j):
                a, m = cols(j, total)
                dve.wait_ge(unit_used, AT[kind, j, 1] + 1)
                dve.tensor_copy(u[:, 1, a:a + m], ps[:, 5 + 2 * (j % 2), 0:m]).then_inc(proj_vec[layer], 1)

            def rotate(x1, x2, cos, sin, tmp):
                dve.tensor_tensor(tmp[0], x1, cos, ALU.mult)
                dve.tensor_tensor(tmp[1], x2, sin, ALU.mult)
                dve.tensor_tensor(tmp[2], x2, cos, ALU.mult)
                link(dve.tensor_tensor(tmp[3], x1, sin, ALU.mult))
                dve.tensor_tensor(x1, tmp[0], tmp[1], ALU.subtract)
                link(dve.tensor_tensor(x2, tmp[2], tmp[3], ALU.add))

            def turn_k(f, dst, rows, col):
                dve.wait_ge(qk_psum, f + 1)
                dve.tensor_scalar(dst, blocks(f % 4)[0:rows], gcol[0:rows, col:col + 1], None, ALU.mult).then_inc(k_turned, 1)

            def scores(u, unit, s, slot, factor, added, slot_head):
                dve.wait_ge(scores_psum, unit + 1)
                if slot_head is not None:
                    dve.wait_ge(p_psum, slot_head + 1)
                for a, n, rows in added:
                    ins = dve.scalar_tensor_tensor(out=s[:, slot, a:a + n], in0=ps[:, score_bank(unit), a:a + n], scalar=factor,
                                                   in1=rows, op0=ALU.mult, op1=ALU.add)
                ins.then_inc(scores_read, 1)
                dve.wait_ge(scores_read, unit + 1)
                dve.tensor_reduce(negmax[:, u, 0:1], s[:, slot, 0:P], AX.X, ALU.max, negate=True)
                dve.tensor_reduce(negmax[:, u, 1:2], s[:, slot, P:384], AX.X, ALU.max, negate=True).then_inc(max_ready, 1)

            def low_y(layer, half):
                for t in range(TT):
                    f = 2 * half + t
                    v = (slice(None), slice(4 * half, 4 * half + 4), slice(t * P, (t + 1) * P))
                    dve.wait_ge(yT_hi, 4 * layer + f + 1)
                    if layer == 0:
                        ins = dve.tensor_tensor(xT_lo[v], blocks(f), xT_hi[v].bitcast(F32), ALU.subtract)
                    else:
                        ins = dve.scalar_tensor_tensor(out=xT_lo[v], in0=blocks(f), scalar=gcol[:, G_SUB:G_SUB + 1],
                                                       in1=xT_hi[v].bitcast(F32), op0=ALU.mult, op1=ALU.subtract)
                    ins.then_inc(yT_ready, 1)

            def add_out(banks, last):
                dve.wait_ge(unit_used, last + 1)
                for n in range(4):
                    t, nn = divmod(n, 2)
                    dve.tensor_tensor(h[:, t, nn * N:(nn + 1) * N], h[:, t, nn * N:(nn + 1) * N],
                                      ps[:, banks[n], :], ALU.add).then_inc(h_ready, 1)

            dve.wait_ge(rel_landed, 16)
            dve.tensor_copy(rel[:, 2 * B_CLIP + 1:384],
                            rel[:, 2 * B_CLIP:2 * B_CLIP + 1].to_broadcast([B_HEADS, 383 - 2 * B_CLIP])).then_inc(rel_extended, 1)
            dve.wait_ge(pos_landed, 16)
            dve.wait_ge(consts_ready, n_consts)
            dve.tensor_copy(slots_f[:, :], slots_i[:, :])
            link(dve.tensor_copy(pos_f[:, :], pos_i[:, :]))
            for t in range(TT):
                ins = dve.tensor_scalar(angle[:, t, :], freq[:, :], pos_f[:, t:t + 1], None, ALU.mult)
            link(ins)
            dve.tensor_scalar(turns[:, 0, :, :], angle[:, :, :], 1.0 / (2 * math.pi), None, ALU.mult)
            link(dve.tensor_scalar(turns[:, 1, :, :], angle[:, :, :], 1.0 / (2 * math.pi), 0.25, ALU.mult, ALU.add))
            link(dve.tensor_scalar(turns[:, :, :, :], turns[:, :, :, :], ROUND, None, ALU.add))
            link(dve.tensor_scalar(turns[:, :, :, :], turns[:, :, :, :], ROUND, None, ALU.subtract))
            for m in range(2):
                ins = dve.scalar_tensor_tensor(out=trig[:, m, :, :], in0=turns[:, m, :, :], scalar=-TURN_1,
                                               in1=angle[:, :, :], op0=ALU.mult, op1=ALU.add)
            link(ins)
            for part in (TURN_2, TURN_3):
                link(dve.scalar_tensor_tensor(out=trig[:, :, :, :], in0=turns[:, :, :, :], scalar=-part,
                                              in1=trig[:, :, :, :], op0=ALU.mult, op1=ALU.add))
            link(dve.tensor_scalar(trig[:, 1, :, :], trig[:, 1, :, :], math.pi / 2, None, ALU.add))
            dve.tensor_scalar(turns[:, :, :, :], trig[:, :, :, :], PI_BELOW, -PI_BELOW, ALU.min, ALU.max).then_inc(angles_ready, 1)
            norm_apply(0, G_MIX0, 0)
            st = bias_rev.ap[0][0]

            def reversed_keys(head, first, n):
                last = bias_rev[:, head, T - 1 - first:T - first]
                return bass.AP(last.tensor, last.offset, [[st, P], [-1, n]])

            split_to(SPLIT)
            dve.wait_ge(rows_landed, 16 * n_rows)
            for m in range(2):
                ins = dve.tensor_tensor(lamv[:, 2 * m, :], lamv[:, 2 * m, :], lamv[:, 2 * m + 1, :], ALU.mult)
            link(ins)
            for m in range(2):
                ins = dve.tensor_reduce(lams[:, m:m + 1], lamv[:, 2 * m, :], AX.X, ALU.add)
            ins.then_inc(lam_sums, 1)
            dve.wait_ge(router_split, 1)
            dve.tensor_tensor(router_lo[:, :, :], router[:, :, :], router_hi[:, :, :].bitcast(F32), ALU.subtract).then_inc(router_split, 1)
            dve.wait_ge(bias_landed, 16 * B_HEADS)
            for head in range(B_HEADS):
                dve.tensor_tensor(bias[:, head, :], reversed_keys(head, 0, T), mask[:, P:384], ALU.add)

            project("in", 0, u0, EVEN_IN, [0])
            dve.wait_ge(u_squared, 1)
            dve.tensor_reduce(ss[:, 0:2], sq_c[:, :, 0:O_CKV], AX.X, ALU.add)
            dve.tensor_reduce(ss[:, 2:4], sq_c[:, :, O_CKV:O_KR], AX.X, ALU.add)
            dve.tensor_reduce(ss[:, 4:6], sq_c[:, :, O_KR:O_BQ], AX.X, ALU.add).then_inc(u_sums, 1)
            dve.wait_ge(u_roots, 1)
            link(dve.reciprocal(rs[:, 0:6], rs[:, 0:6]))
            for t in range(TT):
                dve.tensor_scalar(u0[:, t, 0:O_CKV], u0[:, t, 0:O_CKV], rs[:, t:t + 1], None, ALU.mult)
                dve.tensor_scalar(u0[:, t, O_CKV:O_KR], u0[:, t, O_CKV:O_KR], rs[:, 2 + t:3 + t], None, ALU.mult).then_inc(c_normed, 1)
            for t in range(TT):
                dve.scalar_tensor_tensor(out=kr[:, t, :], in0=u0[:, t, O_KR:O_BQ], scalar=rs[:, 4 + t:5 + t],
                                         in1=ga_rot[:, 1, :], op0=ALU.mult, op1=ALU.mult)
            for t in range(TT):
                dve.wait_ge(c_psum, t + 1)
                scale(4 + t, t, 3, G_C)
            for t in range(TT):
                low_part(4 + t, cT(hT_lo, t), cT(hT_hi, t), 3).then_inc(c_ready, 1)
            project("in", 0, u0, EVEN_IN, range(1, UP_AFTER))
            dve.wait_ge(unit_used, AT["ukv", 0, 0] + 1)
            for t in range(TT):
                for m in range(2):
                    dve.tensor_copy(kva[:, t, m * N:(m + 1) * N], ps[:, 4 + 2 * t + m, :]).then_inc(up_vec, 1)
            split_to(AT["ukv", 0, 0] + SPLIT + 1)
            dve.wait_ge(a_squared, 1)
            dve.tensor_reduce(ss[:, 0:16], sqa[:, :, 0:A_NOPE], AX.X, ALU.add)
            dve.tensor_reduce(ss[:, 16:32].rearrange("p (t g) -> p t g", t=TT), sqk, AX.X, ALU.add)
            dve.tensor_reduce(ss[:, 32:48], sqa[:, :, A_NOPE:A_QK], AX.X, ALU.add).then_inc(a_sums, 1)
            split_to(AT["in", UP_AFTER, 0] + SPLIT + 1)
            dve.wait_ge(a_roots, 1)
            link(dve.reciprocal(rs[:, 0:48], rs[:, 0:48]))
            qh = qa.rearrange("p t (g d) -> p (t g) d", d=A_QK)
            kh = ka.rearrange("p t (g d) -> p t g d", d=A_QK)
            kvh = kva.rearrange("p t (g d) -> p t g d", d=A_NOPE + A_V)
            dve.tensor_tensor(qh[:, :, 0:A_NOPE], qh[:, :, 0:A_NOPE], rs[:, 0:16].unsqueeze(2).to_broadcast([P, 16, A_NOPE]), ALU.mult)
            for t in range(TT):
                dve.tensor_tensor(kh[:, t, :, 0:A_NOPE], kvh[:, t, :, 0:A_NOPE],
                                  rs[:, 16 + 8 * t:24 + 8 * t].unsqueeze(2).to_broadcast([P, 8, A_NOPE]), ALU.mult)
            link(dve.tensor_tensor(qh[:, :, A_NOPE:A_QK], qh[:, :, A_NOPE:A_QK],
                                   rs[:, 32:48].unsqueeze(2).to_broadcast([P, 16, A_ROPE]), ALU.mult))
            link(dve.tensor_tensor(qh[:, :, A_NOPE:A_QK], qh[:, :, A_NOPE:A_QK],
                                   ga_rot[:, 0:1, :].to_broadcast([P, 16, A_ROPE]), ALU.mult))
            project("in", 0, u0, EVEN_IN, [UP_AFTER])
            dve.wait_ge(trig_ready, 1)
            q4 = qa.rearrange("p t (g d) -> p t g d", d=A_QK)

            def turn_mla_keys(t):
                for half in range(2):
                    turn_k(4 * t + 2 * half + 1, kta[0:A_QK, 4 * half:4 * half + 4, t * P:(t + 1) * P], A_QK, G_AK)

            def tables(first, n, groups):
                return [trig[:, m, :, first:first + n].unsqueeze(2).to_broadcast([P, TT, groups, n]) for m in (1, 0)]

            cos, sin = tables(0, NF_A, A_HEADS)
            rotate(q4[:, :, :, A_NOPE:A_NOPE + NF_A], q4[:, :, :, A_NOPE + NF_A:A_QK], cos, sin, rot_a)
            rotate(kr[:, :, 0:NF_A], kr[:, :, NF_A:A_ROPE], trig[:, 1, :, 0:NF_A], trig[:, 0, :, 0:NF_A], rot_k)
            dve.tensor_copy(kh[:, :, :, A_NOPE:A_QK], kr.unsqueeze(2).to_broadcast([P, TT, A_HEADS, A_ROPE])).then_inc(qk_normed, 1)
            dve.wait_ge(u_squared, 2)
            dve.tensor_reduce(ss[:, 48:80].rearrange("p (t g) -> p t g", t=TT),
                              sq_b.rearrange("p t (g d) -> p t g d", d=B_DH), AX.X, ALU.add).then_inc(u_sums, 1)
            turn_mla_keys(0)
            dve.wait_ge(u_roots, 2)
            link(dve.reciprocal(rs[:, 48:80], rs[:, 48:80]))
            for t in range(TT):
                heads = u0[:, t, O_BQ:O_BV].rearrange("p (g d) -> p g d", d=B_DH)
                ins = dve.tensor_tensor(heads, heads, rs[:, 48 + 16 * t:64 + 16 * t].unsqueeze(2).to_broadcast([P, 16, B_DH]), ALU.mult)
            ins.then_inc(qk_normed, 1)
            turn_mla_keys(1)
            project("in", 0, u0, EVEN_IN, range(UP_AFTER + 1, IN_J))
            for t in range(TT):
                turn_k(8 + 2 * t + 1, ktb[:, :, t * P:(t + 1) * P], P, G_BK)

            def head_outputs(layer, g):
                per, width, step = (2, 2 * C_DH, 2) if layer else (4, A_V, 1)
                first = g * per
                dve.wait_ge(pv_done, 16 * layer + first + per)
                if not layer:
                    link(dve.reciprocal(rinv[:, first:first + per, :], psum_l[:, first:first + per, :]))
                n = per * width
                r = rinv[:, first * step:(first + per) * step, :].rearrange("p (k s) t -> p s t k", s=step)[:, 0]
                bank = output_bank(layer, first)[0]
                dve.tensor_tensor(xs[:, :, g * n:(g + 1) * n].rearrange("p t (k d) -> p t k d", d=width),
                                  ps[:, bank, 0:TT * n].rearrange("p (t k d) -> p t k d", t=TT, d=width),
                                  r.unsqueeze(3).to_broadcast([P, TT, per, width]), ALU.mult).then_inc(outputs_ready, 1)

            out0 = AT["out0", 0, 0]
            for u in range(A_HEADS + B_HEADS):
                if u in (6, 9, 12):
                    split_to(out0 + u // 3 - 1)
                if u < A_HEADS:
                    added, factor = [(0, 384, mask[:, :])], A_QK ** -0.5
                else:
                    row = bias[:, u - A_HEADS, :]
                    added, factor = [(0, P, row[:, P:T]), (P, T, row)], B_DH ** -0.5
                scores(u, u, s0, u % S0, factor, added, u - S0 if u >= S0 else None)
                if u in (10, 14):
                    head_outputs(0, (u - 10) // 4)
            for g in (2, 3):
                head_outputs(0, g)
            low_y(0, 0)
            low_y(0, 1)
            split_to(WIDE_FROM + 2)
            add_out([4, 5, 6, 7], AT["out0", 0, DC // 2 - 1])

            norm_apply(1, G_FF0, 6)
            split_to(WIDE_FROM + SPLIT)
            for j in range(FCH + 1):
                for t in range(TT):
                    if j < FCH:
                        split_to(AT["gate", j, t] + SPLIT + 1)
                    if j >= 1:
                        m = cols(j - 1, FF)[1]
                        whole, s = m // P, TT * (j - 1) + t
                        dve.wait_ge(ff_hT_hi, s + 1)
                        if m % P:
                            v = (slice(0, m % P), whole, slice(t * P, (t + 1) * P))
                            dve.tensor_tensor(hT_lo[v], ps[0:m % P, 3, whole * P:(whole + 1) * P], hT_hi[v].bitcast(F32), ALU.subtract)
                        v = (slice(None), slice(0, whole), slice(t * P, (t + 1) * P))
                        dve.tensor_tensor(hT_lo[v], blocks(3, whole), hT_hi[v].bitcast(F32), ALU.subtract).then_inc(ff_hT, 1)
                if j < FCH:
                    m = cols(j, FF)[1]
                    split_to(AT["up", j, 0] + SPLIT + 1)
                    dve.wait_ge(unit_used, AT["up", j, 1] + 1)
                    for t in range(TT):
                        dve.wait_ge(ff_silu, TT * j + t + 1)
                        dve.tensor_tensor(prod[:, t, 0:m], sil[:, t, 0:m], ps[:, (4 * j + 2 + t) % 3, 0:m], ALU.mult).then_inc(ff_prod, 1)
                    split_to(AT["up", j, 1] + SPLIT + 1)
            last_down = AT["qkv", 0, 0] - 1
            split_to(last_down + SPLIT)
            add_out([4, 5, 6, 7], last_down)

            norm_apply(2, G_MIX1, 10)
            split_to(last_down + SPLIT + 1)
            dve.wait_ge(lam_exps, 1)
            link(dve.tensor_tensor(lams[:, 4:5], lams[:, 3:4], lams[:, 2:3], ALU.subtract))
            link(dve.tensor_scalar(lams[:, 5:6], lams[:, 4:5], -LAM_INIT, None, ALU.add))
            cos, sin = tables(NF_A, NF_C, C_GROUPS)
            for m in range(2):
                project("qkv", 1, u1, 3 * C_MIX, range(2 * m + (m > 0), 2 * m + 2))
                part = u1[:, :, m * C_MIX:(m + 1) * C_MIX].rearrange("p t (g d) -> p t g d", d=C_DH)
                dve.wait_ge(u_squared, 2 + m + 1)
                dve.tensor_reduce(part_groups(ss, m), sqc[:, :, m * C_MIX:(m + 1) * C_MIX].rearrange("p t (g d) -> p t g d", d=C_DH),
                                  AX.X, ALU.add).then_inc(u_sums, 1)
                project("qkv", 1, u1, 3 * C_MIX, [2 * m + 2])
                dve.wait_ge(u_roots, 2 + m + 1)
                link(dve.reciprocal(part_groups(rs, m), part_groups(rs, m)))
                for t in range(TT):
                    r = part_groups(rs, m)[:, t, :]
                    ins = dve.tensor_tensor(part[:, t], part[:, t], r.unsqueeze(2).to_broadcast([P, C_GROUPS, C_DH]), ALU.mult)
                link(ins)
                for t in range(TT):
                    rot = part[:, t, :, 0:C_ROPE]
                    ins = dve.tensor_tensor(rot, rot, gc_rot[:, m:m + 1, :].to_broadcast([P, C_GROUPS, C_ROPE]), ALU.mult)
                link(ins)
                rotate(part[:, :, :, 0:NF_C], part[:, :, :, NF_C:C_ROPE], cos, sin, rot_c)
            dve.engine_nop().then_inc(qk_normed, 1)
            copy_out("qkv", 1, u1, 3 * C_MIX, QKV_J - 1)
            for t in range(TT):
                for half in range(2):
                    turn_k(12 + 4 * t + 2 * half + 1, ktc[:, 4 * half:4 * half + 4, t * P:(t + 1) * P], P, G_CK)

            def difference(i):
                dve.wait_ge(exp_done, 16 + 2 * i + 2)
                link(dve.reciprocal(rinv[:, 2 * i:2 * i + 2, :], psum_l[:, 2 * i:2 * i + 2, :]))
                link(dve.scalar_tensor_tensor(out=coef[:, i, :], in0=psum_l[:, 2 * i, :], scalar=lams[:, 5:6],
                                              in1=rinv[:, 2 * i + 1, :], op0=ALU.mult, op1=ALU.mult))
                a, b = (2 * i) % S1, (2 * i + 1) % S1
                for t, (c0, c1) in enumerate(((0, P), (P, 384))):
                    ins = dve.scalar_tensor_tensor(out=s1[:, a, c0:c1], in0=s1[:, b, c0:c1], scalar=coef[:, i, t:t + 1],
                                                   in1=s1[:, a, c0:c1], op0=ALU.mult, op1=ALU.add)
                ins.then_inc(diff_done, 1)

            for i in range(C_HEADS + DIFF_LAG):
                if i < C_HEADS:
                    for m in range(2):
                        scores(2 * i + m, 16 + 2 * i + m, s1, (2 * i + m) % S1, C_DH ** -0.5, [(0, 384, mask[:, :])],
                               16 + i - S1 // 2 if i >= S1 // 2 else None)
                if i >= C_HEADS - 1:
                    split_to(AT["out1", 0, 0] + i - C_HEADS + 2)
                if i >= DIFF_LAG:
                    difference(i - DIFF_LAG)
                if i in (7, 9):
                    head_outputs(1, (i - 7) // 2)

            def output_norm(half):
                heads = xs[:, :, half * N:(half + 1) * N].rearrange("p t (g d) -> p t g d", d=2 * C_DH)
                squares = sqo[:, :, half * N:(half + 1) * N].rearrange("p t (g d) -> p t g d", d=2 * C_DH)
                dve.wait_ge(o_squared, half + 1)
                dve.tensor_reduce(half_heads(ss, half), squares, AX.X, ALU.add).then_inc(o_sums, 1)
                dve.wait_ge(o_roots, half + 1)
                link(dve.reciprocal(half_heads(rs, half), half_heads(rs, half)))
                r = half_heads(rs, half)
                dve.tensor_tensor(heads, heads, r.unsqueeze(3).to_broadcast([P, TT, C_HEADS // 2, 2 * C_DH]), ALU.mult).then_inc(y_ready, 1)

            output_norm(0)
            for g in (2, 3):
                head_outputs(1, g)
            low_y(1, 0)
            output_norm(1)
            low_y(1, 1)
            split_to(DENSE)

            def split_unit(i, q):
                dve.wait_ge(hi_ready, i * len(EXPERT) + DENSE + q + 1)
                k = (DENSE + q) % SPLIT
                dve.tensor_tensor(w_lo[:, k, :], raw[:, raw_of(DENSE + q), :], w_hi[:, k, :].bitcast(F32),
                                  ALU.subtract).then_inc(lo_ready, 1)

            for q in range(SPLIT - 1):
                split_unit(0, q)
            add_out([4, 5, 6, 7], AT["out1", 0, DC // 2 - 1])
            norm_apply(3, G_FF1, 14)
            split_unit(0, SPLIT - 1)
            dve.memset(rank[:, :, ITEMS:ITEMS + 1], FAR)
            dve.memset(comb[:, :, ITEMS:ITEMS + 1], 0.0)
            g, gs = gate_t, gate_s

            def per_token(a):
                return a.unsqueeze(2).to_broadcast([P, TT, E])

            link(dve.tensor_scalar(load8[:, 8, :], slots_f[:, 0:E], -1.0, float(E), ALU.mult, ALU.add))
            keys = load8[:, 8:9, :].to_broadcast([P, TT, E])
            dve.wait_ge(logits_psum, 1)
            dve.tensor_copy(logits_T[:, :], ps[0:E, 4, 0:T]).then_inc(logits_copied, 1)
            dve.wait_ge(logits_psum, 2)
            link(dve.tensor_copy(g[:, 0, :, :], ps[:, 5, 0:TT * E].rearrange("p (t e) -> p t e", e=E)))

            def top(src, m, key, hot):
                link(dve.tensor_reduce(gs[:, m, :], g[:, src, :, :], AX.X, ALU.max))
                link(dve.tensor_tensor(g[:, key, :, :], g[:, src, :, :], per_token(gs[:, m, :]), ALU.is_equal))
                link(dve.tensor_tensor(g[:, key, :, :], g[:, key, :, :], keys, ALU.mult))
                link(dve.tensor_reduce(gs[:, m + 1, :], g[:, key, :, :], AX.X, ALU.max))
                link(dve.tensor_tensor(g[:, hot, :, :], g[:, key, :, :], per_token(gs[:, m + 1, :]), ALU.is_equal))

            top(0, 0, 1, 2)
            link(dve.scalar_tensor_tensor(out=g[:, 3, :, :], in0=g[:, 2, :, :], scalar=-3e38, in1=g[:, 0, :, :],
                                          op0=ALU.mult, op1=ALU.add))
            top(3, 2, 4, 5)
            dve.tensor_tensor(g[:, 6, :, :], g[:, 2, :, :], g[:, 5, :, :], ALU.add).then_inc(chosen_ready, 1)
            dve.tensor_tensor(gs[:, 4, :], gs[:, 2, :], gs[:, 0, :], ALU.subtract).then_inc(gate_diff, 1)
            dve.wait_ge(gate_exp, 1)
            link(dve.tensor_scalar(gs[:, 6, :], gs[:, 5, :], 1.0, None, ALU.add))
            link(dve.reciprocal(gs[:, 7, :], gs[:, 6, :]))
            link(dve.tensor_tensor(gs[:, 8, :], gs[:, 5, :], gs[:, 7, :], ALU.mult))
            dve.tensor_tensor(g[:, 7, :, :], g[:, 2, :, :], per_token(gs[:, 7, :]), ALU.mult)
            link(dve.tensor_tensor(g[:, 8, :, :], g[:, 5, :, :], per_token(gs[:, 8, :]), ALU.mult))
            dve.tensor_tensor(comb[:, :, 0:E], g[:, 7, :, :], g[:, 8, :, :], ALU.add)
            dve.wait_ge(chosen_ready, 1)
            link(dve.tensor_scalar(g[:, 9, :, :], g[:, 6, :, :], -FAR, FAR, ALU.mult, ALU.add))
            dve.wait_ge(rank_psum, 1)
            link(dve.tensor_tensor(rank[:, :, 0:E], g[:, 9, :, :], ps[:, 6, 0:TT * E].rearrange("p (t e) -> p t e", e=E), ALU.add))

            def spare_items():
                link(dve.tensor_scalar(load8[:, 0, :], ps[:, 6, TT * E:(TT + 1) * E], float(P), None, ALU.is_gt))
                link(dve.memset(load8[:, 1, :], 0.0))
                for e in range(1, E):
                    link(dve.tensor_tensor(load8[:, 1, e:e + 1], load8[:, 1, e - 1:e], load8[:, 0, e - 1:e], ALU.add))
                dve.tensor_tensor(over_s[:, SPARE:SPARE + 1], load8[:, 1, E - 1:E], load8[:, 0, E - 1:E], ALU.add)
                for s in range(SPARE):
                    ins = dve.scalar_tensor_tensor(out=load8[:, 2 + s, :], in0=load8[:, 1, :], scalar=float(s), in1=load8[:, 0, :],
                                                   op0=ALU.is_equal, op1=ALU.mult)
                link(ins)
                for s in range(SPARE):
                    pick = load8[:, 2 + s:3 + s, :].to_broadcast([P, TT, E])
                    dve.tensor_reduce(over_s[:, 4 + s:5 + s], load8[:, 2 + s, :], AX.X, ALU.add)
                    dve.tensor_tensor(load8[:, 5 + s, :], load8[:, 2 + s, :], slots_f[:, 0:E], ALU.mult)
                    dve.tensor_tensor(g[:, 10 + s, :, :], pick, rank[:, :, 0:E], ALU.mult)
                    ins = dve.tensor_tensor(g[:, 13 + s, :, :], pick, comb[:, :, 0:E], ALU.mult)
                link(ins)
                for s in range(SPARE):
                    dve.tensor_reduce(over_s[:, s:s + 1], load8[:, 5 + s, :], AX.X, ALU.add)
                    dve.tensor_scalar(over_s[:, 8 + s:9 + s], over_s[:, 4 + s:5 + s], -FAR, FAR - P, ALU.mult, ALU.add)
                    dve.tensor_reduce(gs[:, 9 + s, :], g[:, 10 + s, :, :], AX.X, ALU.add)
                    ins = dve.tensor_reduce(comb[:, :, E + s], g[:, 13 + s, :, :], AX.X, ALU.add)
                link(ins)
                for s in range(SPARE):
                    ins = dve.tensor_scalar(rank[:, :, E + s], gs[:, 9 + s, :], over_s[:, 8 + s:9 + s], None, ALU.add)
                link(ins)
                dve.tensor_copy(over_i[:, :], over_s[:, 0:4]).then_inc(routed, 1)

            def select(i, weighted):
                for t in range(TT):
                    r, c = rank[:, t, bass.ds(i, 1)], comb[:, t, bass.ds(i, 1)]
                    if weighted:
                        ins = dve.tensor_scalar(wsel[:, t, :], slots_f[:, :], r, c, ALU.is_equal, ALU.mult)
                    else:
                        ins = dve.tensor_scalar(sel[:, t, :], slots_f[:, :], r, None, ALU.is_equal)
                return ins

            def gathered(i):
                for half in range(2):
                    dve.wait_ge(gather_psum, 2 * i + half + 1)
                    dve.tensor_tensor(scaled[:, half, :].rearrange("p (a b) -> p a b", b=P), blocks(2 + half),
                                      gains(G_FF1 + 4 * half, 4, P), ALU.mult).then_inc(scaled_ready, 1)
                for half in range(2):
                    v = (slice(None), slice(4 * half, 4 * half + 4), slice(0, P))
                    dve.wait_ge(parts_hi, 2 * i + 18 + half + 1)
                    dve.tensor_tensor(xT_lo[v], scaled[:, half, :].rearrange("p (a b) -> p a b", b=P), xT_hi[v].bitcast(F32),
                                      ALU.subtract).then_inc(xg_ready, 1)

            def outputs(i):
                dve.wait_ge(unit_used, i * len(EXPERT) + DENSE)
                dve.tensor_copy(ysb[:, N:D], ps[:, 7, :]).then_inc(y_vec, 1)

            def add_scattered(i, n):
                t, nn = divmod(n, 2)
                dve.wait_ge(scatter_psum, 4 * (i - 1) + n + 1)
                dve.tensor_tensor(h[:, t, nn * N:(nn + 1) * N], h[:, t, nn * N:(nn + 1) * N], ps[:, 2 + n, :],
                                  ALU.add).then_inc(scatter_read, 1)

            def hidden_turned(i, m):
                dve.wait_ge(hT_part, i * ECH + m + 1)
                dve.tensor_tensor(hT_lo[:, :, side(m)], blocks(4 + m % 2), hT_hi[:, :, side(m)].bitcast(F32),
                                  ALU.subtract).then_inc(hT_ready, 1)

            def expert(i, first_item=False):
                first = i * len(EXPERT) + DENSE
                if not first_item:
                    for q in range(SPLIT):
                        split_unit(i, q)
                    outputs(i)
                for q, (kind, j, u) in enumerate(EXPERT):
                    if q == LAST_TURN:
                        hidden_turned(i, ECH - 1)
                    if q + SPLIT < len(EXPERT):
                        split_unit(i, q + SPLIT)
                    if not first_item:
                        if 1 <= q <= 4:
                            add_scattered(i, q - 1)
                        if q == 6:
                            dve.wait_ge(scatter_read, 4 * i)
                    if kind == "up" and u == 1 and j == ECH // 2:
                        select(i, True)
                        select(i + 1, False).then_inc(sel_ready, 1)
                    if kind == "gate" and u == 1 and j >= 1:
                        hidden_turned(i, j - 1)
                    if kind == "up" and u == 1:
                        dve.wait_ge(silu_done, i * ECH + j + 1)
                        dve.wait_ge(unit_used, first + q + 1)
                        dve.tensor_tensor(prod[:, j % 2, :], sil[:, j % 2, :], ps[:, 2 * (j % 2) + 1, :], ALU.mult).then_inc(prod_done, 1)
                    if q == LAST_UP:
                        gathered(i + 1)

            select(0, False).then_inc(sel_ready, 1)
            spare_items()
            dve.wait_ge(routed, 1)
            gathered(0)
            expert(0, True)
            with dve.Fori(1, E) as i:
                expert(i)
            n_over = dve.value_load(over_i[0:1, SPARE:SPARE + 1], min_val=0, max_val=SPARE)
            for s in range(SPARE):
                with dve.If(n_over > s):
                    expert(E + s)
            outputs(n_over + E)
            for n in range(4):
                add_scattered(n_over + E, n)

        @block.tensor
        def _(pe):
            def split(n):
                pe.wait_ge(lo_ready, n + 1)
                k = {"uq": 2, "ukv": 1, "out0": 2, "out1": 2, "down": 2}.get(STREAM[n][0], 4)
                m = pieces(n)[0][2] if len(pieces(n)) == 1 else 2 * D
                return [x[:, n % SPLIT, 0:m].rearrange("p (k n) -> p k n", k=k) for x in (w_hi, w_lo)]

            def product(out, x_hi, x_lo, hi, lo, start, stop):
                pe.matmul(out, x_hi, hi, start=start, stop=False)
                pe.matmul(out, x_hi, lo, start=False, stop=False)
                return pe.matmul(out, x_lo, hi, start=False, stop=stop)

            def norm_turn(k):
                for t in range(TT):
                    pe.wait_ge(xs_ready, 2 * k + t + 1)
                    for c in range(DC):
                        ins = pe.transpose(ps[:, 2 * t + c // 4, (c % 4) * P:(c % 4 + 1) * P], xs[:, t, c * P:(c + 1) * P], ident[:, :])
                        if c % 4 == 3:
                            ins.then_inc(xT_psum, 1)

            def project(layer, kind, total, k, chunks):
                for j in chunks:
                    m = cols(j, total)[1]
                    for u in range(2):
                        hi, lo = split(AT[kind, j, u])
                        for t in range(TT):
                            if j == 0:
                                pe.wait_ge(xT_ready, 4 * k + 2 * t + u + 1)
                            if u == 0 and layer == 0 and j >= UP_AFTER:
                                pe.wait_ge(up_vec, 2 * (j - UP_AFTER) + t + 1)
                            elif u == 0 and j >= 2:
                                pe.wait_ge((proj_act if t == 0 else proj_vec)[layer], j - 1)
                            tok = slice(t * P, (t + 1) * P)
                            for c in range(4):
                                k8 = 4 * u + c
                                ins = product(ps[:, 4 + (2 * j + t) % 4, 0:m], xT_hi[:, k8, tok], xT_lo[:, k8, tok],
                                              hi[:, c, :], lo[:, c, :], k8 == 0, k8 == DC - 1)
                        ins.then_inc(unit_used, 1)
                        if layer == 0 and (j, u) == (UP_AFTER - 1, 1):
                            turn_compressed()

            def turn_compressed():
                for t in range(TT):
                    pe.wait_ge(c_normed, t + 1)
                    for n in range(3):
                        ins = pe.transpose(ps[:, t, n * P:(n + 1) * P], u0[:, t, n * P:(n + 1) * P], ident[:, :])
                    ins.then_inc(c_psum, 1)

            def turn_heads(f, src, rows):
                if f % 12 >= 4:
                    pe.wait_ge(k_turned if f % 2 else q_turned, f // 2 - 1)
                for n in range(4):
                    ins = pe.transpose(ps[0:rows, f % 4, n * P:(n + 1) * P], src(n), ident[:, :])
                ins.then_inc(qk_psum, 1)

            def scores(unit, q, k):
                if unit % 16 >= len(SCORE_BANKS):
                    pe.wait_ge(scores_read, unit - len(SCORE_BANKS) + 1)
                b = score_bank(unit)
                pe.matmul(ps[:, b, 0:P], q(0), k(P), start=True, stop=True)
                pe.matmul(ps[:, b, P:384], q(1), k(T), start=True, stop=True).then_inc(scores_psum, 1)

            def turn_p(head, ready, count, s, slot):
                pe.wait_ge(ready, count)
                if head >= 2:
                    pe.wait_ge(p_turned, head - 1)
                for n in range(3):
                    ins = pe.transpose(ps[:, 2 + head % 2, n * P:(n + 1) * P], s[:, slot, n * P:(n + 1) * P], ident[:, :])
                ins.then_inc(p_psum, 1)

            def weigh_values(layer, n, pt, v, width):
                head = 16 * layer + n
                bank, at = output_bank(layer, n)
                per = 2 if layer else 4
                pe.wait_ge(p_turned, head + 1)
                if n % per == 0 and n >= 2 * per:
                    pe.wait_ge(outputs_ready, 4 * layer + n // per - 1)
                p = pt[:, head % 2, :]
                out0, out1 = (ps[:, bank, a:a + width] for a in at)
                pe.matmul(out0, p[:, 0:P], v(0), start=True, stop=True)
                pe.matmul(out1, p[:, P:2 * P], v(0), start=True, stop=False)
                pe.matmul(out1, p[:, 2 * P:384], v(1), start=False, stop=True).then_inc(pv_done, 1)

            def out_projection(layer):
                def turn(half):
                    if layer:
                        pe.wait_ge(y_ready, half + 1)
                    else:
                        pe.wait_ge(outputs_ready, 2 * half + 2)
                    for t in range(TT):
                        for n in range(4):
                            c = 4 * half + n
                            ins = pe.transpose(ps[:, 2 * half + t, n * P:(n + 1) * P], xs[:, t, c * P:(c + 1) * P], ident[:, :])
                        ins.then_inc(yT_psum, 1)

                turn(0)
                pe.wait_ge(outputs_ready, 4 * layer + 4)
                for u in range(DC // 2):
                    if u == 1:
                        turn(1)
                    pe.wait_ge(yT_ready, 4 * layer + 2 * (u // 2) + 2)
                    hi, lo = split(AT[f"out{layer}", 0, u])
                    for c in range(2):
                        k = 2 * u + c
                        for n in range(4):
                            t, nn = divmod(n, 2)
                            tok, col = slice(t * P, (t + 1) * P), slice(nn * N, (nn + 1) * N)
                            ins = product(ps[:, 4 + n, :], xT_hi[:, k, tok], xT_lo[:, k, tok], hi[:, c, col], lo[:, c, col],
                                          k == 0, k == DC - 1)
                    ins.then_inc(unit_used, 1)

            pe.wait_ge(consts_ready, n_consts)
            pe.wait_ge(gains_landed, 16 * n_gains)
            pe.transpose(ps[:, 7, 0:G_ROWS], gain_rows[:, :], ident[0:G_ROWS, 0:G_ROWS]).then_inc(gains_turned, 1)
            norm_turn(0)
            project(0, "in", EVEN_IN, 0, range(UP_AFTER))
            pe.wait_ge(c_ready, TT)
            hi, lo = split(AT["uq", 0, 0])
            for t in range(TT):
                for m, (a, n) in enumerate(((0, 512), (512, 256))):
                    for c in range(2):
                        ins = product(ps[:, 2 * t + m, 0:n], cT(hT_hi, t)[:, c, :], cT(hT_lo, t)[:, c, :],
                                      hi[:, c, a:a + n], lo[:, c, a:a + n], c == 0, c == 1)
            ins.then_inc(unit_used, 1)
            hi, lo = split(AT["ukv", 0, 0])
            for t in range(TT):
                pe.wait_ge(proj_act[0], t + 1)
                pe.wait_ge(proj_vec[0], t + 1)
                for m in range(2):
                    ins = product(ps[:, 4 + 2 * t + m, :], cT(hT_hi, t)[:, 2, :], cT(hT_lo, t)[:, 2, :],
                                  hi[:, 0, m * N:(m + 1) * N], lo[:, 0, m * N:(m + 1) * N], True, True)
            ins.then_inc(unit_used, 1)
            project(0, "in", EVEN_IN, 0, range(UP_AFTER, IN_J))
            pe.wait_ge(qk_normed, 1)
            for t in range(TT):
                for half in range(2):
                    for m, src in enumerate((qa, ka)):
                        turn_heads(4 * t + 2 * half + m,
                                   lambda n: src[:, t, (4 * half + n) * A_QK:(4 * half + n + 1) * A_QK], A_QK)
            pe.wait_ge(qk_normed, 2)
            for t in range(TT):
                for m, first in enumerate((O_BQ, O_BK)):
                    turn_heads(8 + 2 * t + m, lambda n: u0[:, t, first + n * P:first + (n + 1) * P], P)
            pe.wait_ge(q_turned, 6)
            pe.wait_ge(k_turned, 6)
            heads = A_HEADS + B_HEADS
            for i in range(heads + VALUE_LAG):
                if i < A_HEADS:
                    scores(i, lambda t: qta[0:A_QK, i, t * P:(t + 1) * P], lambda n: kta[0:A_QK, i, 0:n])
                elif i < heads:
                    pair, m = divmod(i - A_HEADS, 2)
                    r = slice(m * B_DH, (m + 1) * B_DH)
                    scores(i, lambda t: qtb[r, pair, t * P:(t + 1) * P], lambda n: ktb[r, pair, 0:n])
                if TURN_LAG <= i < heads + TURN_LAG:
                    n = i - TURN_LAG
                    turn_p(n, exp_done, n + 1, s0, n % S0)
                if i >= VALUE_LAG:
                    n = i - VALUE_LAG
                    if n < A_HEADS:
                        weigh_values(0, n, pt0, lambda t: kva[:, t, n * P + A_NOPE:(n + 1) * P], A_V)
                    else:
                        c = O_BV + (n - A_HEADS) * B_DH
                        weigh_values(0, n, pt0, lambda t: u0[:, t, c:c + B_DH], B_DH)
            out_projection(0)

            norm_turn(1)
            for j in range(FCH + 1):
                for part, kind in enumerate(("gate", "up")):
                    for u in range(2):
                        if j < FCH:
                            m = cols(j, FF)[1]
                            hi, lo = split(AT[kind, j, u])
                            for t in range(TT):
                                use = 4 * j + 2 * part + t
                                if u == 0 and use >= 3:
                                    jj, was = divmod(use - 3, 4)
                                    pe.wait_ge(ff_silu if was < 2 else ff_prod, TT * jj + was % 2 + 1)
                                if j == 0 and kind == "gate":
                                    pe.wait_ge(xT_ready, 4 + 2 * t + u + 1)
                                tok = slice(t * P, (t + 1) * P)
                                for c in range(4):
                                    k = 4 * u + c
                                    ins = product(ps[:, use % 3, 0:m], xT_hi[:, k, tok], xT_lo[:, k, tok], hi[:, c, :], lo[:, c, :],
                                                  k == 0, k == DC - 1)
                            ins.then_inc(unit_used, 1)
                        if kind == "gate" and j >= 1:
                            m, s = cols(j - 1, FF)[1], TT * (j - 1) + u
                            pe.wait_ge(ff_prod, s + 1)
                            if s >= 1:
                                pe.wait_ge(ff_hT, s)
                            for n in range(-(-m // P)):
                                k = min(P, m - n * P)
                                ins = pe.transpose(ps[0:k, 3, n * P:(n + 1) * P], prod[:, u, n * P:n * P + k], ident[:, :])
                            ins.then_inc(ff_turned, 1)
                if j >= 1:
                    pe.wait_ge(ff_hT, TT * j)
                    for k in range(4 * (j - 1), min(4 * j, FK)):
                        if k % 2 == 0:
                            hi, lo = split(AT["down", j - 1, k % 4 // 2])
                        r = min(P, FF - k * P)
                        for n in range(4):
                            t, nn = divmod(n, 2)
                            tok, col = slice(t * P, (t + 1) * P), slice(nn * N, (nn + 1) * N)
                            ins = product(ps[:, 4 + n, :], hT_hi[0:r, k % 4, tok], hT_lo[0:r, k % 4, tok],
                                          hi[0:r, k % 2, col], lo[0:r, k % 2, col], k == 0, k == FK - 1)
                        if k % 2 == 1:
                            ins.then_inc(unit_used, 1)

            norm_turn(2)
            project(1, "qkv", 3 * C_MIX, 2, range(QKV_J))
            pe.wait_ge(qk_normed, 3)
            for t in range(TT):
                for half in range(2):
                    for m in range(2):
                        turn_heads(12 + 4 * t + 2 * half + m,
                                   lambda n: u1[:, t, m * C_MIX + (4 * half + n) * P:m * C_MIX + (4 * half + n + 1) * P], P)
            pe.wait_ge(proj_vec[1], QKV_J)
            pe.wait_ge(q_turned, 10)
            pe.wait_ge(k_turned, 10)
            for i in range(C_HEADS + VALUE_LAG):
                if i < C_HEADS:
                    for m in range(2):
                        r = slice(m * C_DH, (m + 1) * C_DH)
                        scores(16 + 2 * i + m, lambda t: qtc[r, i, t * P:(t + 1) * P], lambda n: ktc[r, i, 0:n])
                if TURN_LAG <= i < C_HEADS + TURN_LAG:
                    n = i - TURN_LAG
                    turn_p(16 + n, diff_done, n + 1, s1, 2 * n % S1)
                if i >= VALUE_LAG:
                    n = i - VALUE_LAG
                    weigh_values(1, n, pt1, lambda t: u1[:, t, 2 * C_MIX + n * P:2 * C_MIX + (n + 1) * P], 2 * C_DH)
            out_projection(1)

            norm_turn(3)
            pe.wait_ge(router_split, 2)
            for c in range(DC):
                pe.wait_ge(xT_ready, 12 + TT + c // 4 + 1)
                ins = product(ps[0:E, 4, 0:T], router_hi[:, c, :], router_lo[:, c, :], xT_hi[:, c, :], xT_lo[:, c, :],
                              c == 0, c == DC - 1)
            ins.then_inc(logits_psum, 1)
            pe.wait_ge(logits_copied, 1)
            for t in range(TT):
                ins = pe.transpose(ps[:, 5, t * E:(t + 1) * E], logits_T[:, t * P:(t + 1) * P], ident[0:E, 0:E])
            ins.then_inc(logits_psum, 1)
            pe.wait_ge(chosen_ready, 1)
            chosen = gate_t[:, 6, :, :]
            pe.matmul(ps[:, 6, 0:E], tri[:, :], chosen[:, 0, :], start=True, stop=True)
            pe.matmul(ps[:, 6, E:2 * E], ones[:, :], chosen[:, 0, :], start=True, stop=False)
            pe.matmul(ps[:, 6, E:2 * E], tri[:, :], chosen[:, 1, :], start=False, stop=True)
            pe.matmul(ps[:, 6, 2 * E:3 * E], ones[:, :], chosen[:, 0, :], start=True, stop=False)
            pe.matmul(ps[:, 6, 2 * E:3 * E], ones[:, :], chosen[:, 1, :], start=False, stop=True).then_inc(rank_psum, 1)

            def gather(i):
                for c in range(DC):
                    for t in range(TT):
                        ins = pe.matmul(ps[:, 2 + c // 4, (c % 4) * P:(c % 4 + 1) * P], xs[:, t, c * P:(c + 1) * P], sel[:, t, :],
                                        start=(t == 0), stop=(t == TT - 1))
                    if c % 4 == 3:
                        ins.then_inc(gather_psum, 1)

            def scatter(i):
                pe.wait_ge(wselT_ready, i)
                pe.wait_ge(y_act, i)
                pe.wait_ge(y_vec, i)
                for n in range(4):
                    t, nn = divmod(n, 2)
                    pe.matmul(ps[:, 2 + n, :], wselT[:, t, :], ysb[:, nn * N:(nn + 1) * N], start=True, stop=True).then_inc(scatter_psum, 1)

            def expert(i, first_item=False):
                first = i * len(EXPERT) + DENSE

                def turn(j):
                    pe.wait_ge(prod_done, i * ECH + j + 1)
                    if j >= 2:
                        pe.wait_ge(hT_ready, i * ECH + j - 1)
                    elif not first_item:
                        pe.wait_ge(scatter_read, 4 * (i - 1) + 2 + j + 1)
                    if j == ECH - 1:
                        pe.wait_ge(wselT_ready, i + 1)
                    for n in range(4):
                        ins = pe.transpose(ps[:, 4 + j % 2, n * P:(n + 1) * P], prod[:, j % 2, n * P:(n + 1) * P], ident[:, :])
                    ins.then_inc(turn_done, 1)

                pe.wait_ge(xg_ready, 2 * i + 2)
                for q, (kind, j, u) in enumerate(EXPERT):
                    if kind == "down" and u == 0:
                        pe.wait_ge(hT_ready, i * ECH + j + 1)
                    pe.wait_ge(lo_ready, first + q + 1)
                    k = (DENSE + q) % SPLIT
                    hi, lo = w_hi[:, k, :], w_lo[:, k, :]
                    if kind == "down":
                        for c in range(2):
                            for nn in range(2):
                                col = slice(c * D + nn * N, c * D + (nn + 1) * N)
                                ins = product(ps[:, 6 + nn, :], hT_hi[:, 2 * u + c, side(j)], hT_lo[:, 2 * u + c, side(j)], hi[:, col], lo[:, col],
                                              j == 0 and u == 0 and c == 0, j == ECH - 1 and u == 1 and c == 1)
                    else:
                        bank = 2 * (j % 2) + (kind == "up")
                        if j >= 2 and u == 0:
                            pe.wait_ge(prod_done if kind == "up" else silu_done, i * ECH + j - 1)
                        if j == 1 and u == 0 and not first_item:
                            pe.wait_ge(scatter_read, 4 * (i - 1) + (kind == "up") + 1)
                        for c in range(4):
                            col = slice(c * N, (c + 1) * N)
                            ins = product(ps[:, bank, :], xT_hi[:, 4 * u + c, 0:P], xT_lo[:, 4 * u + c, 0:P], hi[:, col], lo[:, col],
                                          u == 0 and c == 0, u == 1 and c == 3)
                    ins.then_inc(unit_used, 1)
                    if q == 1 and not first_item:
                        scatter(i)
                    if kind == "gate" and u == 1 and j >= 1:
                        turn(j - 1)
                    if q == LAST_TURN:
                        turn(ECH - 1)
                    if q == LAST_UP:
                        pe.wait_ge(sel_ready, i + 2)
                        for t in range(TT):
                            ins = pe.transpose(ps[:, 4, t * P:(t + 1) * P], wsel[:, t, :], ident[:, :])
                        ins.then_inc(wselT_psum, 1)
                        gather(i + 1)

            pe.wait_ge(sel_ready, 1)
            gather(0)
            expert(0, True)
            with pe.Fori(1, E) as i:
                expert(i)
            pe.wait_ge(routed, 1)
            n_over = pe.value_load(over_i[0:1, SPARE:SPARE + 1], min_val=0, max_val=SPARE)
            for s in range(SPARE):
                with pe.If(n_over > s):
                    expert(E + s)
            scatter(n_over + E)

        @block.gpsimd
        def _(pool):
            pool.wait_ge(rel_extended, 1)
            pool.dma_start(rel_scratch, rel[:, :]).then_inc(rel_stored, 16)
            pool.wait_ge(rel_stored, 16)
            for head in range(B_HEADS):
                shifted = bass.AP(rel_scratch.tensor, head * 384 + 1, [[1, P], [1, T]])
                pool.dma_start(bias_rev[:, head, :], shifted).then_inc(bias_landed, 16)


_INS = ['x', 'positions', 'ev_norm_mix', 'ev_w_in', 'ev_g_cq', 'ev_g_ckv', 'ev_w_uq', 'ev_w_ukv',
        'ev_a_qnorm', 'ev_a_knorm', 'ev_b_qnorm', 'ev_b_knorm', 'ev_b_rel_bias', 'ev_w_out',
        'ev_norm_ff', 'ev_ff_gate', 'ev_ff_up', 'ev_ff_down',
        'od_norm_mix', 'od_w_qkv', 'od_c_qnorm', 'od_c_knorm', 'od_lam_q1', 'od_lam_k1',
        'od_lam_q2', 'od_lam_k2', 'od_c_subnorm', 'od_w_out', 'od_norm_ff', 'od_router',
        'od_ex_gate', 'od_ex_up', 'od_ex_down']


def kernel(**inputs):
    import numpy as _np
    import concourse.bacc as _bacc
    from concourse import mybir as _mybir
    from concourse.bass_utils import run_bass_kernel_spmd as _run

    nc = _bacc.Bacc("TRN2", target_bir_lowering=False, num_devices=1)
    arrays, aps = {}, {}
    for name in _INS:
        a = _np.ascontiguousarray(inputs[name])
        arrays[f"in_{name}_dram"] = a
        aps[name] = nc.dram_tensor(f"in_{name}_dram", a.shape, _mybir.dt.from_np(a.dtype), kind="ExternalInput").ap()
    out = nc.dram_tensor("out_0_dram", (1, T, D), _mybir.dt.float32, kind="ExternalOutput").ap()
    trunk(nc, aps, out)
    r = _run(nc, [arrays], core_ids=[0])
    return r.results[0]["out_0_dram"]
```
